# Optimizing a Trainium2 kernel written in Bass

```python
import math
import jax, jax.numpy as jnp
from jax import lax
import numpy as np

D_MODEL = 2048
BATCH = 1
SEQ = 256
DEPTH = 1
DEC_BATCH = 8
DEC_SEQ = 1
PAST_LEN = 2048
PAGE_SIZE = 128

GLA_HEADS = 4
GLA_DK = (D_MODEL // 2) // GLA_HEADS
GLA_DV = D_MODEL // GLA_HEADS
GLA_RANK = 16
GLA_TAU = 16
GLA_CHUNK = 64
CONV_DIM = D_MODEL
CONV_WIDTH = 3
PEER_HEADS = 8
N_KEYS = 128
N_EXPERTS = N_KEYS * N_KEYS
PEER_TOPK = 16
DQ_HALF = 128
PEER_BLOCK = 128
EPS = 1e-6

W_IN_WIDTHS = (GLA_HEADS * GLA_DK, GLA_HEADS * GLA_DK, GLA_HEADS * GLA_DV, GLA_HEADS * GLA_DV,
               GLA_RANK, CONV_DIM, CONV_DIM, CONV_DIM, D_MODEL, D_MODEL)
D_IN = sum(W_IN_WIDTHS)

kernel_name = "gla_shortconv_peer_hybrid_step"

def rmsnorm(x, g):
    xf = x.astype(jnp.float32)
    xf = xf * lax.rsqrt(jnp.mean(xf * xf, axis=-1, keepdims=True) + EPS)
    return (xf * g.astype(jnp.float32)).astype(x.dtype)

def gla_chunked(q, k, v, loga, s0):
    B, L, H, DK = q.shape
    DV = v.shape[-1]
    C = math.gcd(L, GLA_CHUNK)
    n = L // C

    def to_chunks(t):
        return t.astype(jnp.float32).reshape(B, n, C, H, t.shape[-1]).transpose(1, 0, 3, 2, 4)

    qs, ks, vs, gs = to_chunks(q), to_chunks(k), to_chunks(v), to_chunks(loga)
    causal = jnp.tril(jnp.ones((C, C), dtype=bool))

    def step(S, inp):
        qc, kc, vc, gc = inp
        b = jnp.cumsum(gc, axis=2)
        diff = b[:, :, :, None, :] - b[:, :, None, :, :]
        decay = jnp.exp(jnp.where(causal[None, None, :, :, None], diff, -jnp.inf))
        attn = jnp.einsum('bhid,bhjd,bhijd->bhij', qc, kc, decay)
        o = (jnp.einsum('bhij,bhjv->bhiv', attn, vc)
             + jnp.einsum('bhid,bhdv->bhiv', qc * jnp.exp(b), S))
        bl = b[:, :, -1:, :]
        S_new = (jnp.exp(bl[:, :, 0, :])[..., None] * S
                 + jnp.einsum('bhjd,bhjv->bhdv', kc * jnp.exp(bl - b), vc))
        return S_new, o

    S_fin, o = lax.scan(step, s0.astype(jnp.float32), (qs, ks, vs, gs))
    o = o.transpose(1, 0, 3, 2, 4).reshape(B, L, H, DV)
    return o.astype(q.dtype), S_fin.astype(s0.dtype)

def peer(h, w_query, sub_keys, expert_u, expert_v):
    B, L, D = h.shape
    T = B * L
    ht = h.reshape(T, D)
    q = (ht @ w_query).reshape(T, PEER_HEADS, 2, DQ_HALF)
    s1 = jnp.einsum('thd,nd->thn', q[:, :, 0], sub_keys[0]).astype(jnp.float32)
    s2 = jnp.einsum('thd,nd->thn', q[:, :, 1], sub_keys[1]).astype(jnp.float32)
    v1, i1 = lax.top_k(s1, PEER_TOPK)
    v2, i2 = lax.top_k(s2, PEER_TOPK)
    cand = (v1[..., :, None] + v2[..., None, :]).reshape(T, PEER_HEADS, PEER_TOPK * PEER_TOPK)
    cidx = (i1[..., :, None] * N_KEYS + i2[..., None, :]).reshape(T, PEER_HEADS, PEER_TOPK * PEER_TOPK)
    top, pos = lax.top_k(cand, PEER_TOPK)
    idx = jnp.take_along_axis(cidx, pos, axis=-1)
    g = jax.nn.softmax(top, axis=-1).astype(h.dtype)

    blk = math.gcd(T, PEER_BLOCK)
    nb = T // blk

    def one_block(args):
        xb, ib, gb = args
        u = jnp.take(expert_u, ib, axis=0)
        a = jnp.einsum('thkd,td->thk', u, xb)
        w = gb * jax.nn.gelu(a, approximate=False)
        vg = jnp.take(expert_v, ib, axis=0)
        return jnp.einsum('thk,thkd->td', w, vg)

    out = lax.map(one_block, (ht.reshape(nb, blk, D),
                              idx.reshape(nb, blk, PEER_HEADS, PEER_TOPK),
                              g.reshape(nb, blk, PEER_HEADS, PEER_TOPK)))
    return out.reshape(B, L, D)

def layer(x, s_gla, s_conv, norm1_g, w_in, w_alpha_up, b_alpha, gla_norm_g, conv_w, conv_b,
          w_out, norm2_g, w_query, sub_keys, expert_u, expert_v):
    B, L, _ = x.shape
    h = rmsnorm(x, norm1_g)
    p = h @ w_in
    points = []
    acc = 0
    for w in W_IN_WIDTHS[:-1]:
        acc += w
        points.append(acc)
    q, k, v, r, alr, cb, cc, cx, ga, gb = jnp.split(p, points, axis=-1)

    loga = jax.nn.log_sigmoid((alr @ w_alpha_up + b_alpha).astype(jnp.float32)) / GLA_TAU
    q = q.reshape(B, L, GLA_HEADS, GLA_DK) * (GLA_DK ** -0.5)
    k = k.reshape(B, L, GLA_HEADS, GLA_DK)
    v = v.reshape(B, L, GLA_HEADS, GLA_DV)
    loga = loga.reshape(B, L, GLA_HEADS, GLA_DK)
    o, s_gla_new = gla_chunked(q, k, v, loga, s_gla)
    o = rmsnorm(o, gla_norm_g.reshape(GLA_HEADS, GLA_DV))
    y_a = jax.nn.silu(r) * o.reshape(B, L, GLA_HEADS * GLA_DV)

    u = cc * cx
    buf = jnp.concatenate([s_conv.astype(u.dtype), u], axis=1)
    z = conv_b
    for j in range(CONV_WIDTH):
        z = z + buf[:, j:j + L] * conv_w[j]
    y_b = cb * z
    s_conv_new = buf[:, L:]

    m = jax.nn.sigmoid(ga) * y_a + jax.nn.sigmoid(gb) * y_b
    x = x + m @ w_out

    x = x + peer(rmsnorm(x, norm2_g), w_query, sub_keys, expert_u, expert_v)
    return x, s_gla_new, s_conv_new.astype(s_conv.dtype)

def setup_inputs(seed: int = 0) -> dict:
    key = jax.random.key(seed)
    ks = jax.random.split(key, 20)
    nrm = jax.random.normal
    f32 = jnp.float32
    return {
        "x_prompt": nrm(ks[0], (BATCH, SEQ, D_MODEL), f32),
        "x_sample": nrm(ks[1], (DEC_BATCH, DEC_SEQ, D_MODEL), f32),
        "state_gla": 0.5 * nrm(ks[2], (DEPTH, DEC_BATCH, GLA_HEADS, GLA_DK, GLA_DV), f32),
        "state_conv": nrm(ks[3], (DEPTH, DEC_BATCH, CONV_WIDTH - 1, CONV_DIM), f32),
        "norm1_g": 1.0 + 0.02 * nrm(ks[4], (DEPTH, D_MODEL), f32),
        "w_in": nrm(ks[5], (DEPTH, D_MODEL, D_IN), f32) * D_MODEL ** -0.5,
        "w_alpha_up": nrm(ks[6], (DEPTH, GLA_RANK, GLA_HEADS * GLA_DK), f32) * GLA_RANK ** -0.5,
        "b_alpha": 1.0 + 0.1 * nrm(ks[7], (DEPTH, GLA_HEADS * GLA_DK), f32),
        "gla_norm_g": 1.0 + 0.02 * nrm(ks[8], (DEPTH, GLA_HEADS * GLA_DV), f32),
        "conv_w": nrm(ks[9], (DEPTH, CONV_WIDTH, CONV_DIM), f32) * CONV_WIDTH ** -0.5,
        "conv_b": 0.02 * nrm(ks[10], (DEPTH, CONV_DIM), f32),
        "w_out": nrm(ks[11], (DEPTH, D_MODEL, D_MODEL), f32) * D_MODEL ** -0.5,
        "norm2_g": 1.0 + 0.02 * nrm(ks[12], (DEPTH, D_MODEL), f32),
        "w_query": nrm(ks[13], (DEPTH, D_MODEL, PEER_HEADS * 2 * DQ_HALF), f32) * D_MODEL ** -0.5,
        "sub_keys": nrm(ks[14], (DEPTH, 2, N_KEYS, DQ_HALF), f32) * DQ_HALF ** -0.5,
        "expert_u": nrm(ks[15], (DEPTH, N_EXPERTS, D_MODEL), f32) * D_MODEL ** -0.5,
        "expert_v": 0.1 * nrm(ks[16], (DEPTH, N_EXPERTS, D_MODEL), f32),
        "norm_f_g": 1.0 + 0.02 * nrm(ks[17], (D_MODEL,), f32),
    }

def reference(x_prompt, x_sample, state_gla, state_conv, norm1_g, w_in, w_alpha_up, b_alpha,
              gla_norm_g, conv_w, conv_b, w_out, norm2_g, w_query, sub_keys, expert_u, expert_v,
              norm_f_g):
    xp, xs = x_prompt, x_sample
    zero_gla = jnp.zeros((BATCH, GLA_HEADS, GLA_DK, GLA_DV), state_gla.dtype)
    zero_conv = jnp.zeros((BATCH, CONV_WIDTH - 1, CONV_DIM), state_conv.dtype)
    gla_p, conv_p, gla_s, conv_s = [], [], [], []
    for l in range(DEPTH):
        wts = (norm1_g[l], w_in[l], w_alpha_up[l], b_alpha[l], gla_norm_g[l], conv_w[l], conv_b[l],
               w_out[l], norm2_g[l], w_query[l], sub_keys[l], expert_u[l], expert_v[l])
        xp, sg, sc = layer(xp, zero_gla, zero_conv, *wts)
        gla_p.append(sg)
        conv_p.append(sc)
        xs, sg, sc = layer(xs, state_gla[l], state_conv[l], *wts)
        gla_s.append(sg)
        conv_s.append(sc)
    y_prompt = rmsnorm(xp, norm_f_g)
    y_sample = rmsnorm(xs, norm_f_g)
    return (y_prompt, y_sample, jnp.stack(gla_p), jnp.stack(conv_p), jnp.stack(gla_s), jnp.stack(conv_s))


_drawn_inputs = setup_inputs


def setup_inputs(seed=0):
    import zlib

    import numpy as np

    out = dict(_drawn_inputs(seed))
    spreads = {}
    factors = {'gla_norm_g': 8.0, 'conv_b': 5.646, 'norm2_g': 8.0, 'norm_f_g': 2.823}
    for name, (base, spread) in spreads.items():
        noise = np.random.default_rng([zlib.crc32(name.encode()), seed]).standard_normal(out[name].shape)
        drawn = base * np.exp(spread * noise) if base else spread * noise
        out[name] = __import__('jax').numpy.asarray(drawn.astype(out[name].dtype))
    for name, factor in factors.items():
        out[name] = (out[name] * factor).astype(out[name].dtype)
    return out
```

```python
from contextlib import ExitStack

import concourse.bass as bass
from concourse import mybir

F32 = mybir.dt.float32
F32R = mybir.dt.float32r
U32 = mybir.dt.uint32
ALU = mybir.AluOpType
ACT = mybir.ActivationFunctionType
AX_X = mybir.AxisListType.X

P = 128
EPS = 1e-6
CHUNK = 128
TAU = 16.0
ONE = 1
NEG_BIG = -3.0e38


def hybrid_step(nc, x_prompt, x_sample, state_gla, state_conv, norm1_g, w_in, w_alpha_up, b_alpha,
                gla_norm_g, conv_w, conv_b, w_out, norm2_g, w_query, sub_keys, expert_u, expert_v,
                norm_f_g, y_prompt, y_sample, gla_prompt, conv_prompt, gla_sample, conv_sample):
    D = x_prompt.shape[2]
    TP, TS = x_prompt.shape[1], x_sample.shape[0]
    T = TP + TS
    KT = D // P
    H, DK, DV = state_gla.shape[2:]
    KD = DK // P
    HV = DV // P
    RANK = w_alpha_up.shape[1]
    NKEY = sub_keys.shape[2]
    PH, TOPK = 8, 16
    assert T == 2 * P + TS and KD == 2 and HV == 4 and TS * TOPK == P and NKEY == P

    COL_K = H * DK
    COL_V = 2 * H * DK
    COL_R = COL_V + H * DV
    COL_ALR = COL_R + H * DV
    COL_CB = COL_ALR + RANK
    COL_CC, COL_CX, COL_GA, COL_GB = (COL_CB + D * j for j in (1, 2, 3, 4))
    SIX = (COL_R, COL_GA, COL_CB, COL_CC, COL_CX, COL_GB)

    B_Q, B_K, B_V, B_SIX = 1, 1 + H * KD, 1 + 2 * H * KD, 1 + 2 * H * KD + KT
    SIX_PER_HEAD = 2 * 6 * 2
    B_OUT = B_SIX + H * SIX_PER_HEAD
    B_QRY = B_OUT + KT
    B_END = B_QRY + 2 * PH
    N_PAR = 5 * H + 3
    N_CONSTS = 22
    N_LINKS = 17
    POSTS = 2 * 4 * 2

    def posts(n0):
        n = min(max(n0 + 1 - B_V, 0), KT)
        for b in range(min(max(n0 + 1 - B_SIX, 0), H * SIX_PER_HEAD)):
            n += (b // 2) % 6 not in (2, 3)
        return n + max(n0 + 1 - B_OUT, 0)
    GW = 2 * P

    x_p = x_prompt.rearrange("b (t p) d -> p (b t) d", p=P)
    x_s = x_sample.rearrange("b s d -> (b s) d")
    win = w_in.rearrange("o (k p) n -> p (o k) n", p=P)
    wout = w_out.rearrange("o (k p) n -> p (o k) n", p=P)
    wqry = w_query.rearrange("o (k p) n -> p (o k) n", p=P)
    eu = expert_u.rearrange("o e d -> (o e) d")
    ev = expert_v.rearrange("o e d -> (o e) d")
    st_in = state_gla.rearrange("o j h (k p) v -> p (o h) k j v", p=P)
    st_out = gla_sample.rearrange("o j h (k p) v -> p (o h) k j v", p=P)
    stp_out = gla_prompt.rearrange("o b h (k p) v -> p (o b h) k v", p=P)

    with ExitStack() as ctx:
        top = (nc.sbuf_base + 63) // 64 * 64
        where = [top]

        def sb_at(name, shape, dt, at):
            return nc.alloc_sbuf_tensor_at(name, shape, dt, offset=at)

        def room(nbytes):
            at = where[0]
            where[0] += (nbytes + 31) // 32 * 32
            assert where[0] <= nc.sbuf_usable_end, (where[0], nc.sbuf_usable_end)
            return at

        def size(shape):
            n = 4
            for s in shape[1:]:
                n *= s
            return n

        def sb(name, shape, dt=F32):
            return sb_at(name, shape, dt, room(size(shape)))

        def sem(name):
            return ctx.enter_context(nc.semaphore(name))

        ident = sb("ident", [P, P])
        causal = sb("causal", [P, P])
        eye8 = sb("eye8", [P, TS, TS])
        spread = sb("spread", [P, P])
        gather8 = sb("gather8", [P, TS])
        own16 = sb("own16", [P, TOPK])
        iota16 = sb("iota16", [P, TOPK])
        pcol = sb("pcol", [P, 120])
        keysT = sb("keysT", [P, 2, NKEY])
        ssq = sb("ssq", [P, 3])
        mean_sq = sb("mean_sq", [P, 3])
        root = sb("root", [P, 3])
        rstd = sb("rstd", [P, 3])
        keep = where[0]

        act_hi = sb("act_hi", [P, KT, T], F32R)
        act_lo = sb("act_lo", [P, KT, T], F32R)
        raw = [sb(f"raw{s}", [P, KT, GW]) for s in range(2)]
        w_hi = [sb(f"w_hi{s}", [P, KT, P], F32R) for s in range(2)]
        w_lo = [sb(f"w_lo{s}", [P, KT, P], F32R) for s in range(2)]
        at_qk = room(4 * KT * T)
        qk = sb_at("qk", [P, KT, T], F32, at_qk)
        mT = sb_at("mT", [P, KT, T], F32, at_qk)
        at_la = room(4 * H * KD * T)
        la = sb_at("la", [P, H * KD, T], F32, at_la)
        at_tok = room(4 * 3 * D)
        x_tok = sb_at("x_tok", [P, 3, D], F32, at_tok)
        v_tok = sb_at("v_tok", [P, 3, D], F32, at_tok)
        x2_tok = sb_at("x2_tok", [P, 3, D], F32, at_tok)
        at_head = where[0]
        v_h = sb("v_h", [P, 3, DV])
        q_h = sb("q_h", [P, KD, T])
        k_h = sb("k_h", [P, KD, T])
        la_h = sb("la_h", [P, KD, T])
        la_tmp = sb_at("la_tmp", [P, H * KD, T], F32, at_head)
        cols = sb("cols", [P, H * KD, 8])
        cols_h = sb("cols_h", [P, KD, 8])
        decS = sb("decS", [P, H * KD, TS])
        decS_h = sb("decS_h", [P, KD, TS])
        pcol_h = sb("pcol_h", [P, 20])
        convT = sb("convT", [P, KT, 2 * TS])
        convT_h = sb("convT_h", [P, HV, 2 * TS])
        dq = sb("dq", [P, KD, P])
        dk = sb("dk", [P, KD, P])
        dq0 = sb("dq0", [P, KD, P])
        dk1 = sb("dk1", [P, KD, P])
        k_tok = sb("k_tok", [P, KD, P])
        attn = sb("attn", [P, P])
        S = sb("S", [P, KD, DV])
        o_sb = sb("o_sb", [P, DV])
        oT = sb("oT", [P, HV, T])
        gss = sb("gss", [P, 8])
        at_ring = room(4 * 4 * DV)
        s_ring = [sb_at(f"s_ring{s}", [P, DV], F32, at_ring + 4 * s * DV) for s in range(4)]
        sq_junk = sb_at("sq_junk", [P, D], F32, at_ring)
        q_sel = sb("q_sel", [P, KD, TS, TS])
        ks_tok = sb("ks_tok", [P, DK])
        ks_sel = [sb(f"ks_sel{s}", [P, P]) for s in range(2)]
        tA = [sb(f"tA{s}", [P, T]) for s in range(2)]
        tR = [sb(f"tR{s}", [P, T]) for s in range(2)]
        u_pad = [sb(f"u_pad{s}", [P, 2 + T]) for s in range(2)]
        at_gate = where[0]
        gate = sb("gate", [P, HV, T])
        yb = sb("yb", [P, HV, T])
        u_rows = sb("u_rows", [P, HV * P])
        wau = sb_at("wau", [P, H * DK], F32, at_gate)
        prow = sb_at("prow", [P, P], F32, at_head)
        krow = sb_at("krow", [P, 2, P], F32, at_head + 512)
        crow = sb_at("crow", [P, D], F32, at_head + 2048)
        alr = sb_at("alr", [P, T], F32, at_gate + size([P, HV, T]))
        stage = [sb_at(f"stage{s}", [P, T], F32, at_head + 1056 * s) for s in range(2)]

        bank = [ctx.enter_context(nc.psum_tensor(f"bank{b}", [P, 512], F32)) for b in range(8)]
        ACC, MISC, OB, KV0, KV1, OS, OUTER = 0, 2, 3, 4, 5, 6, 7

        xn_tok = sb_at("xn_tok", [P, 3, D], F32, at_qk)
        assert at_qk + size([P, 3, D]) <= at_tok
        end_a, where[0] = where[0], at_head + 2112
        sc = sb("sc", [P, 2, 3, NKEY])
        cand = sb("cand", [P, 3, TOPK * TOPK])
        hot = [sb(f"hot{s}", [P, 3, TOPK, TOPK]) for s in range(2)]
        val = sb("val", [P, 2, 3, TOPK])
        key_u = sb("key_u", [P, 2, 3, TOPK], U32)
        key_f = sb("key_f", [P, 2, 3, TOPK])
        best = sb("best", [P, 3, TOPK])
        pos = sb("pos", [P, 3, TOPK], U32)
        pos_u = sb("pos_u", [P, 2, 3, TOPK], U32)
        pos_f = sb("pos_f", [P, 2, 3, TOPK])
        key_sel = sb("key_sel", [P, 2, 3, TOPK])
        soft = sb("soft", [P, 3, TOPK])
        soft_s = sb("soft_s", [P, 3])
        soft_r = sb("soft_r", [P, 3])
        picks = sb("picks", [P, 2, 3, TOPK])
        own = sb("own", [P, 2, TOPK])
        own_s = sb("own_s", [P, 2])
        idx_all = sb("idx_all", [P, PH * 2 * TOPK], U32)
        g_all = sb("g_all", [P, PH * 2 * TOPK])
        w_all = sb("w_all", [P, PH * 2 * TOPK])
        idx_s = sb("idx_s", [P, PH], U32)
        g_s = sb("g_s", [P, PH])
        w_s = sb("w_s", [P, PH])
        dots = sb("dots", [P, 2 * TOPK])
        dots_s = sb("dots_s", [P, PH])
        gelu = sb("gelu", [P, 2 * TOPK])
        idx_st = sb("idx_st", [P, 8], U32)
        w_st = sb("w_st", [P, TOPK])
        g_row = sb("g_row", [P, D])
        end_b, where[0] = where[0], keep
        RING = 8
        ring = [sb(f"ring{s}", [P, D]) for s in range(RING)]
        xs_rep = sb("xs_rep", [P, D])
        y_sq = sb("y_sq", [P, D])
        diag = [sb(f"diag{s}", [P, P]) for s in range(4)]
        diag_s = [sb(f"diag_s{s}", [P, TS]) for s in range(4)]
        zeros = sb("zeros", [P, 512])
        assert where[0] <= at_qk

        consts = sem("consts")
        x_in = sem("x_in")
        par_in = sem("par_in")
        conv_in = sem("conv_in")
        keys_in = sem("keys_in")
        wau_in = sem("wau_in")
        par_T = sem("par_T")
        par_ready = sem("par_ready")
        raw_in = [sem(f"raw_in{s}") for s in range(2)]
        hi_done = sem("hi_done")
        lo_done = sem("lo_done")
        mm_done = sem("mm_done")
        acc_read = sem("acc_read")
        post_done = sem("post_done")
        ss_done = sem("ss_done")
        ms_done = sem("ms_done")
        rt_done = sem("rt_done")
        rs_done = sem("rs_done")
        xn_done = sem("xn_done")
        tr_done = sem("tr_done")
        ah_done = sem("ah_done")
        al_done = sem("al_done")
        la_mm = sem("la_mm")
        la_ev = sem("la_ev")
        la_step = sem("la_step")
        la_ready = sem("la_ready")
        v_tr = sem("v_tr")
        staged = sem("staged")
        head_done = sem("head_done")
        exps = sem("exps")
        decayed = sem("decayed")
        attn_mm = sem("attn_mm")
        k_read = sem("k_read")
        attn_ready = sem("attn_ready")
        o_mm = sem("o_mm")
        o_sum = sem("o_sum")
        o_mean = sem("o_mean")
        o_root = sem("o_root")
        o_rstd = sem("o_rstd")
        o_ready = sem("o_ready")
        o_tr = sem("o_tr")
        oT_ready = sem("oT_ready")
        S_ready = sem("S_ready")
        S_out = sem("S_out")
        ks_mm = sem("ks_mm")
        ks_ready = sem("ks_ready")
        q_sel_ready = sem("q_sel_ready")
        ks_sel_ready = sem("ks_sel_ready")
        s_in = [sem(f"s_in{s}") for s in range(4)]
        s_out = [sem(f"s_out{s}") for s in range(4)]
        outer_mm = sem("outer_mm")
        s_new = sem("s_new")
        os_mm = sem("os_mm")
        u_ready = sem("u_ready")
        u_tr = sem("u_tr")
        u_read = sem("u_read")
        u_out = sem("u_out")
        chain = sem("chain")
        m_ready = sem("m_ready")
        granted = sem("granted")
        conv_copy = sem("conv_copy")
        x2_in = sem("x2_in")

        cleared = sem("cleared")
        soft_in = sem("soft_in")
        soft_e = sem("soft_e")
        picked = sem("picked")
        spread_mm = sem("spread_mm")
        retrieved = sem("retrieved")
        row_in = sem("row_in")
        h2_ready = sem("h2_ready")
        rep_mm = sem("rep_mm")
        rep_ready = sem("rep_ready")
        idx_staged = sem("idx_staged")
        ring_in = [sem(f"ring_in{s}") for s in range(RING)]
        u_used = sem("u_used")
        v_used = sem("v_used")
        gelu_done = sem("gelu_done")
        w_ready = sem("w_ready")
        w_staged = sem("w_staged")
        diag_ready = sem("diag_ready")
        sum_ready = sem("sum_ready")
        y_sum = sem("y_sum")
        y_ss = sem("y_ss")
        y_mean = sem("y_mean")
        y_root = sem("y_root")
        y_rstd = sem("y_rstd")
        y_ready = sem("y_ready")
        y_out = sem("y_out")

        from_one = (head_done, post_done, decayed, o_mm, o_tr, u_out, w_ready, diag_ready, os_mm, attn_mm, outer_mm, S_out, o_ready, gelu_done, acc_read, k_read, attn_ready, s_new, oT_ready, u_read)

        block = ctx.enter_context(nc.Block())

        def m_at(k):
            return k // 4 * 2 + k % 4 // 2 * (KT // 2) + k % 2

        def at_slot(n0):
            g = (n0 + 1) // 2
            return g % 2, g // 2, (n0 - 1) % 2 if n0 else 0

        @block.sync
        def _(sp):
            for counter in from_one:
                sp.sem_inc(counter, ONE)
            sp.dma_start(x_tok[:, 0:2, :], x_p).then_inc(x_in, 16)
            sp.dma_start(x_tok[0:TS, 2, :], x_s).then_inc(x_in, 16)
            n_par = 0
            for h in range(H):
                r = 20 * h
                span = slice(h * DV, (h + 1) * DV)
                for src in (gla_norm_g[:, span], conv_w[0, 0:1, span], conv_w[0, 1:2, span],
                            conv_w[0, 2:3, span], conv_b[:, span]):
                    sp.dma_start(prow[r:r + HV, :], src.rearrange("o (r c) -> (o r) c", c=P)).then_inc(par_in, 16)
                    r += HV
                    n_par += 1
            for r, src in ((80, norm1_g), (80 + KT, norm2_g), (80 + 2 * KT, b_alpha)):
                rows = src.shape[1] // P
                sp.dma_start(prow[r:r + rows, :], src.rearrange("o (r c) -> (o r) c", c=P)).then_inc(par_in, 16)
                n_par += 1
            assert n_par == N_PAR
            sp.dma_start(crow[0:2 * TS, :], state_conv.rearrange("o j s d -> (o j s) d")).then_inc(conv_in, 16)
            sp.dma_start(krow[:], sub_keys.rearrange("o s n d -> n (o s) d")).then_inc(keys_in, 16)
            sp.dma_start(wau[0:RANK, :], w_alpha_up.rearrange("o r n -> (o r) n")).then_inc(wau_in, 16)
            sp.dma_start(conv_sample.rearrange("o j s d -> (o j) s d")[:, 0, :],
                         state_conv.rearrange("o j s d -> (o j) s d")[:, 1, :]).then_inc(conv_copy, 16)

            def group(g0, src, free_at):
                if free_at is not None:
                    sp.wait_ge(lo_done, free_at)
                sp.dma_start(raw[g0 % 2][:, :, 0:src.shape[2]], src).then_inc(raw_in[g0 % 2], 16)

            def free(g0):
                return 2 * g0 - 3 if g0 >= 2 else None

            group(0, win[:, :, COL_ALR:COL_ALR + P], None)
            for g in (1, 2):
                group(g, win[:, :, (g - 1) * GW:g * GW], free(g))
            with sp.Fori(0, 7) as i:
                for j in (0, 1):
                    group(3 + j, win[:, :, bass.ds((2 + j) * GW + i * (2 * GW), GW)], free(3 + j) + i * 4)
            g_six = (B_SIX + 1) // 2
            with sp.Fori(0, H) as i:
                for cg in (0, 1):
                    for t, col in enumerate(SIX):
                        g = g_six + 6 * cg + t
                        group(g, win[:, :, bass.ds(col + cg * GW + i * (2 * GW), GW)], free(g) + i * 24)
            for b0, w in ((B_OUT, wout), (B_QRY, wqry)):
                g0 = (b0 + 1) // 2
                with sp.Fori(0, 4) as i:
                    for j in (0, 1):
                        group(g0 + j, w[:, :, bass.ds(j * GW + i * (2 * GW), GW)], free(g0 + j) + i * 4)
            sp.wait_ge(cleared, 1)
            sp.dma_start(g_row[:], norm2_g.partition_broadcast(P).rearrange("p o d -> p (o d)")).then_inc(row_in, 16)
            sp.wait_ge(h2_ready, 3)
            sp.dma_start(g_row[:], norm_f_g.partition_broadcast(P)).then_inc(row_in, 16)
            for t in range(3):
                sp.wait_ge(y_ready, t + 1)
                out, src = ((y_prompt.rearrange("b (t p) d -> p (b t) d", p=P)[:, t, :], x2_tok[:, t, :]) if t < 2
                            else (y_sample.rearrange("b s d -> (b s) d"), x2_tok[0:TS, 2, :]))
                sp.dma_start(out, src).then_inc(y_out, 16)
            sp.wait_ge(conv_copy, 16)
            sp.wait_ge(y_out, 48)

        @block.gpsimd
        def _(pool):
            g = nc.gpsimd
            n = 0

            def made(ins):
                nonlocal n
                n += 1
                ins.then_inc(consts, 1)

            def ones_where(out, pattern, base, mult, first=None):
                made(g.memset(out, 0.0))
                pool.wait_ge(consts, n)
                made(g.affine_select(out=out, in_=out, compare_op=ALU.not_equal, fill=1.0, base=base,
                                     pattern=pattern, channel_multiplier=mult))

            ones_where(ident[:], [[-1, P]], 0, 1)
            ones_where(eye8[:], [[1, TS], [-1, TS]], 0, 0)
            made(g.memset(causal[:], 1.0))
            pool.wait_ge(consts, n)
            made(g.affine_select(out=causal[:], in_=causal[:], compare_op=ALU.is_ge, fill=0.0, base=0,
                                 pattern=[[1, P]], channel_multiplier=-1))
            for m, pat, mult, width in ((spread, 1, -TOPK, P), (gather8, -TOPK, 1, TS)):
                made(g.memset(m[:], 1.0))
                pool.wait_ge(consts, n)
                made(g.affine_select(out=m[:], in_=m[:], compare_op=ALU.is_ge, fill=0.0, base=0,
                                     pattern=[[pat, width]], channel_multiplier=mult))
                pool.wait_ge(consts, n)
                made(g.affine_select(out=m[:], in_=m[:], compare_op=ALU.is_ge, fill=0.0, base=TOPK - 1,
                                     pattern=[[-pat, width]], channel_multiplier=-mult))
            made(g.memset(own16[:], 0.0))
            for j in range(TS):
                pool.wait_ge(consts, n)
                made(g.affine_select(out=own16[:], in_=own16[:], compare_op=ALU.not_equal, fill=1.0,
                                     base=-TOPK * j, pattern=[[-1, TOPK]], channel_multiplier=1))
            made(g.iota(iota16[:], pattern=[[1, TOPK]], base=0, channel_multiplier=0,
                        allow_small_or_imprecise_dtypes=True))
            assert n == N_CONSTS, n

            pool.wait_ge(la_ready, 3)
            pool.wait_ge(par_ready, 3)
            pool.wait_ge(post_done, ONE + KT)
            with pool.Fori(0, H) as i:
                pool.wait_ge(head_done, ONE + i)
                pool.sem_inc(granted, 1)
                g.tensor_copy(v_h[:, 0:2, :], v_tok[:, 0:2, bass.ds(i * DV, DV)]).then_inc(staged, 1)
                g.tensor_copy(v_h[0:TS, 2, :], v_tok[0:TS, 2, bass.ds(i * DV, DV)]).then_inc(staged, 1)
                g.tensor_copy(q_h[:], qk[:, bass.ds(i * KD, KD), :]).then_inc(staged, 1)
                g.tensor_copy(k_h[:], qk[:, bass.ds(i * KD + H * KD, KD), :]).then_inc(staged, 1)
                g.tensor_copy(la_h[:], la[:, bass.ds(i * KD, KD), :]).then_inc(staged, 1)
                g.tensor_copy(cols_h[:], cols[:, bass.ds(i * KD, KD), :]).then_inc(staged, 1)
                g.tensor_copy(decS_h[:], decS[:, bass.ds(i * KD, KD), :]).then_inc(staged, 1)
                g.tensor_copy(pcol_h[:], pcol[:, bass.ds(i * 20, 20)]).then_inc(staged, 1)
                g.tensor_copy(convT_h[:], convT[:, bass.ds(i * HV, HV), :]).then_inc(staged, 1)

                def load(m):
                    g.dma_start(s_ring[m % 4][:], st_in[:, bass.ds(i, 1), m % KD, m // KD, :]
                                .rearrange("p o v -> p (o v)")).then_inc(s_in[m % 4], 16)

                M = KD * TS
                for m in range(4):
                    load(m)
                for m in range(M):
                    pool.wait_ge(s_new, ONE + i * M + m + 1)
                    pool.sem_inc(granted, 1)
                    g.dma_start(st_out[:, bass.ds(i, 1), m % KD, m // KD, :]
                                .rearrange("p o v -> p (o v)"), s_ring[m % 4][:]).then_inc(s_out[m % 4], 16)
                    if m + 4 < M:
                        pool.wait_ge(s_out[m % 4], i * (4 * 16) + 16 * (m // 4) + 16)
                        pool.sem_inc(granted, 1)
                        pool.wait_ge(os_mm, ONE + i * M + m + 1)
                        pool.sem_inc(granted, 1)
                        load(m + 4)
                for s in range(4):
                    pool.wait_ge(s_out[s], i * (4 * 16) + 64)
                    pool.sem_inc(granted, 1)
            for s in range(4):
                pool.wait_ge(s_out[s], H * 64)
            pool.wait_ge(head_done, ONE + H)
            g.dma_start(x2_tok[:, 0:2, :], x_p).then_inc(x2_in, 16)
            g.dma_start(x2_tok[0:TS, 2, :], x_s).then_inc(x2_in, 16)

            def fetch(table, free_sem, free_at, src, k, n_staged):
                pool.wait_ge(free_sem, free_at)
                pool.sem_inc(granted, 1)
                g.tensor_copy(idx_st[:, k:k + 1], src).then_inc(idx_staged, 1)
                pool.wait_ge(idx_staged, n_staged)
                pool.sem_inc(granted, 1)
                g.indirect_dma_start(ring[k][:], None, table,
                                     bass.IndirectOffsetOnAxis(ap=idx_st[:, k:k + 1], axis=0)).then_inc(ring_in[k], 16)

            W = 2 * TOPK
            pool.wait_ge(retrieved, PH)
            pool.wait_ge(mm_done, B_END)
            with pool.Fori(0, PH) as i:
                for s in range(W):
                    fetch(eu, u_used, i * W + s + 1, idx_all[:, bass.ds(i * W + s, 1)], s % RING, i * W + s + 1)
            for s in range(PH):
                fetch(eu, u_used, PH * W + s + 1, idx_s[:, s:s + 1], s, PH * W + s + 1)
            U = PH * W + PH
            for t in range(2):
                with pool.Fori(0, PH) as i:
                    for s in range(TOPK):
                        q = t * PH * TOPK + s
                        fetch(ev, v_used, i * TOPK + q + 1, idx_all[:, bass.ds(i * W + t * TOPK + s, 1)],
                              s % RING, i * TOPK + U + q + 1)
            for s in range(PH):
                q = 2 * PH * TOPK + s
                fetch(ev, v_used, q + 1, idx_s[:, s:s + 1], s, U + q + 1)

        @block.scalar
        def _(act):
            a = nc.scalar

            def hi(n0, i=0, L=0):
                s, use, half = at_slot(n0)
                act.wait_ge(raw_in[s], 16 * (use + 1) + i * (16 * L // 4))
                a.activation(w_hi[n0 % 2][:], raw[s][:, :, half * P:(half + 1) * P], ACT.Copy).then_inc(hi_done, 1)

            def evac_wait(n0, i, L):
                act.wait_ge(post_done, ONE + posts(n0 - 4) + i * (POSTS if L == 24 else L if n0 >= B_V else 0))

            def norm(p, src):
                for t in range(3):
                    q = P if t < 2 else TS
                    if t:
                        act.wait_ge(ss_done, 3 * p + t)
                    a.activation(sq_junk[0:q, :], src[0:q, t, :], ACT.Square,
                                 accum_out=ssq[0:q, t:t + 1]).then_inc(ss_done, 1)
                act.wait_ge(ms_done, p + 1)
                a.activation(root[:], mean_sq[:], ACT.Sqrt).then_inc(rt_done, 1)

            def act_parts(p, gcol):
                for k in range(KT):
                    act.wait_ge(tr_done, KT * p + k + 1)
                    a.activation(act_hi[:, k, :], bank[2 + k % 6][:, 0:T], ACT.Copy,
                                 scale=pcol[:, gcol + k:gcol + k + 1]).then_inc(ah_done, 1)

            act.wait_ge(chain, 1)
            act.wait_ge(x_in, 32)
            norm(0, x_tok)
            hi(0)
            hi(1)
            act.wait_ge(par_T, 1)
            a.activation(pcol[:], bank[2][:, 0:120], ACT.Copy).then_inc(par_ready, 1)
            act.wait_ge(par_T, 2)
            a.activation(keysT[:], bank[3][:, 0:2 * NKEY].rearrange("p (s n) -> p s n", s=2), ACT.Copy).then_inc(par_ready, 1)
            act.wait_ge(par_T, 3)
            a.activation(convT[:], bank[4][:, 0:KT * 2 * TS].rearrange("p (k r) -> p k r", k=KT), ACT.Copy).then_inc(par_ready, 1)
            act.wait_ge(par_ready, 1)
            act_parts(0, 80)

            act.wait_ge(mm_done, 1)
            hi(2)
            a.activation(alr[0:RANK, :], bank[ACC][0:RANK, 0:T], ACT.Copy).then_inc(acc_read, 1)
            act.wait_ge(la_ev, H * KD)
            a.activation(la_tmp[:], la[:], ACT.Abs).then_inc(la_step, 1)
            act.wait_ge(la_step, 1)
            a.activation(la_tmp[:], la_tmp[:], ACT.Exp, scale=-1.0).then_inc(la_step, 1)
            act.wait_ge(la_step, 2)
            a.activation(la_tmp[:], la_tmp[:], ACT.Ln, bias=1.0).then_inc(la_step, 1)

            def qkv_block(n0, i, L, out):
                act.wait_ge(mm_done, n0 + 1 + i * L)
                hi(n0 + 2, i, L)
                evac_wait(n0, i, L)
                a.activation(out, bank[ACC + n0 % 2][:, 0:T], ACT.Copy).then_inc(acc_read, 1)

            with act.Fori(0, 4) as i:
                for b in range(4):
                    qkv_block(B_Q + b, i, 4, qk[:, bass.ds(i * 4 + b, 1), :].rearrange("p o t -> p (o t)"))
            with act.Fori(0, 4) as i:
                for b in range(4):
                    qkv_block(B_V + b, i, 4, stage[(B_V + b) % 2][:])

            act.wait_ge(la_ready, 1)
            act.wait_ge(la_step, 5)
            a.activation(cols[:, :, 6:8], cols[:, :, 4:6], ACT.Exp).then_inc(la_ready, 1)
            a.activation(decS[:], la[:, :, TP:T], ACT.Exp, scale=1.0 / TAU).then_inc(la_ready, 1)

            def chunk_exps(i, c):
                act.wait_ge(decayed, ONE + i * 2 + c)
                if c == 0:
                    act.wait_ge(staged, i * 9 + 9)
                act.wait_ge(o_mm, ONE + i * 2 + c)
                bt = la_h[:, :, c * P:(c + 1) * P]
                for k in range(KD):
                    for out, sc, col in ((dq, 1, 0), (dk, -1, 2), (dk1, -1, 4)):
                        a.activation(out[:, k, :], bt[:, k, :], ACT.Exp, scale=sc / TAU,
                                     bias=cols_h[:, k, col + c:col + c + 1]).then_inc(exps, 1)
                a.activation(dq0[:], bt, ACT.Exp, scale=1.0 / TAU).then_inc(exps, 1)

            def out_norm(i, c):
                q, src = (P, bank[OB]) if c < 2 else (TS, bank[OS])
                junk = o_sb[0:q, :]
                if c < 2:
                    act.wait_ge(o_mm, ONE + i * 2 + c + 1)
                else:
                    act.wait_ge(os_mm, ONE + i * (KD * TS) + KD * TS)
                act.wait_ge(o_tr, ONE + i * 3 + c)
                a.activation(junk, src[0:q, :], ACT.Square, accum_out=gss[0:q, c:c + 1]).then_inc(o_sum, 1)

            def out_scale(i, c):
                q, src = (P, bank[OB]) if c < 2 else (TS, bank[OS])
                act.wait_ge(o_mean, i * 3 + c + 1)
                a.activation(gss[0:q, 3:4], gss[0:q, 3:4], ACT.Sqrt).then_inc(o_root, 1)
                act.wait_ge(o_rstd, i * 3 + c + 1)
                a.activation(o_sb[0:q, :], src[0:q, :], ACT.Copy,
                             scale=gss[0:q, 4:5]).then_inc(o_ready, 1)

            def out_turned(i, c):
                act.wait_ge(o_tr, ONE + i * 3 + c + 1)
                if c == 0:
                    act.wait_ge(head_done, ONE + i)
                w = P if c < 2 else TS
                a.activation(oT[:, :, c * P:c * P + w],
                             bank[KV1][:, 0:HV * w].rearrange("p (b t) -> p b t", b=HV), ACT.Copy).then_inc(oT_ready, 1)

            with act.Fori(0, H) as i:
                for b in range(SIX_PER_HEAD):
                    n0 = B_SIX + b
                    cg, t, half = b // 12, (b // 2) % 6, b % 2
                    src = bank[ACC + n0 % 2][:, 0:T]
                    act.wait_ge(mm_done, n0 + 1 + i * 24)
                    hi(n0 + 2, i, 24)
                    evac_wait(n0, i, 24)
                    q = cg * 2 + half
                    if cg == 0 and t in (1, 2):
                        act.wait_ge(head_done, ONE + i)
                    if t == 0:
                        act.wait_ge(post_done, ONE + posts(n0 - 2) + i * POSTS)
                        a.activation(tR[half][:], src, ACT.Copy)
                        a.activation(tA[half][:], src, ACT.Sigmoid).then_inc(acc_read, 1)
                    elif t == 1:
                        a.activation(gate[:, q, :], src, ACT.Sigmoid).then_inc(acc_read, 1)
                    elif t in (2, 3, 4):
                        out = {2: yb[:, q, :], 3: tA[half][:], 4: tR[half][:]}[t]
                        a.activation(out, src, ACT.Copy).then_inc(acc_read, 1)
                    else:
                        act.wait_ge(post_done, ONE + posts(n0 - 2) + i * POSTS)
                        a.activation(tR[half][:], src, ACT.Sigmoid).then_inc(acc_read, 1)
                    if b == 1:
                        chunk_exps(i, 0)
                    if b == 9:
                        chunk_exps(i, 1)
                    for c in (0, 1):
                        if b == 8 * c + 4:
                            act.wait_ge(attn_mm, ONE + i * 2 + c + 1)
                            a.activation(k_tok[:], bank[MISC][:, P:3 * P].rearrange("p (k d) -> p k d", k=KD),
                                         ACT.Copy).then_inc(k_read, 1)
                    if b == 2:
                        act.wait_ge(ks_mm, i + 1)
                        a.activation(ks_tok[0:TS, :], bank[OB][0:TS, 0:DK], ACT.Copy).then_inc(ks_ready, 1)
                    for c, at in ((0, 6), (1, 14), (2, 20)):
                        if b == at:
                            out_norm(i, c)
                        if b == at + 1:
                            out_scale(i, c)
                        if b == at + 2:
                            out_turned(i, c)
                    if t == 5:
                        act.wait_ge(u_tr, i * 4 + q + 1)
                        if q == 0:
                            act.wait_ge(u_out, ONE + i * 32)
                        a.activation(u_rows[0:2 + TS, q * P:(q + 1) * P], bank[KV1][0:2 + TS, 0:P],
                                     ACT.Copy).then_inc(u_read, 1)
                act.wait_ge(u_read, ONE + i * 4 + 4)
                ch = bass.ds(i * DV, DV)
                act.dma_start(conv_prompt.rearrange("o b s d -> (o b s) d")[:, ch], u_rows[0:2, :]).then_inc(u_out, 16)
                act.dma_start(conv_sample.rearrange("o j s d -> (o j) s d")[:, 1, ch], u_rows[2:2 + TS, :]).then_inc(u_out, 16)
                act.wait_ge(S_ready, i * 2 + 2)
                act.dma_start(stp_out[:, bass.ds(i, 1), :, :].rearrange("p o k v -> p (o k) v"), S[:]).then_inc(S_out, 16)

            act.wait_ge(m_ready, 2 * H)
            act.wait_ge(mm_done, B_OUT)
            for k in range(0, KT, 2):
                a.activation(act_hi[:, k:k + 2, :], mT[:, m_at(k):m_at(k) + 2, :], ACT.Copy).then_inc(ah_done, 2)
            with act.Fori(0, 4) as i:
                for b in range(4):
                    qkv_block(B_OUT + b, i, 4, stage[(B_OUT + b) % 2][:])
            act.wait_ge(post_done, ONE + posts(B_QRY - 1))
            norm(1, x2_tok)
            act_parts(1, 80 + KT)

            def query_block(n0, i, L, more):
                act.wait_ge(mm_done, n0 + 1 + i * L)
                if more:
                    hi(n0 + 2, i, L)
                evac_wait(n0, i, L)
                a.activation(stage[n0 % 2][:], bank[ACC + n0 % 2][:, 0:T], ACT.Copy).then_inc(acc_read, 1)

            def soft_exp(h0, i):
                act.wait_ge(soft_in, i * 2 + h0 + 1)
                a.activation(soft[:], soft[:], ACT.Exp).then_inc(soft_e, 1)

            with act.Fori(0, PH // 2 - 1) as i:
                for h in range(2):
                    for half in range(2):
                        query_block(B_QRY + 2 * h + half, i, 4, True)
                    soft_exp(h, i)
            for h in range(PH - 2, PH):
                for half in range(2):
                    query_block(B_QRY + 2 * h + half, 0, 0, h < PH - 1)
                soft_exp(h, 0)

            act.wait_ge(rep_mm, 1)
            for j in range(4):
                a.activation(xs_rep[:, j * 512:(j + 1) * 512], bank[4 + j][:], ACT.Copy).then_inc(rep_ready, 1)
            W = 2 * TOPK
            with act.Fori(0, PH) as i:
                act.wait_ge(u_used, i * W + W + RING)
                act.wait_ge(w_ready, ONE + i)
                a.activation(gelu[:], dots[:], ACT.Gelu).then_inc(gelu_done, 1)
            act.wait_ge(v_used, RING)
            act.wait_ge(w_ready, ONE + PH)
            a.activation(gelu[:, 0:PH], dots_s[:], ACT.Gelu).then_inc(gelu_done, 1)

            def y_norm(t):
                q = P if t < 2 else TS
                act.wait_ge(y_sum, 4 * t + 4)
                if t:
                    act.wait_ge(y_ss, t)
                a.activation(y_sq[0:q, :], x2_tok[0:q, t, :], ACT.Square,
                             accum_out=ssq[0:q, t:t + 1]).then_inc(y_ss, 1)
                act.wait_ge(y_mean, t + 1)
                a.activation(root[0:q, t:t + 1], mean_sq[0:q, t:t + 1], ACT.Sqrt).then_inc(y_root, 1)

            for t in range(2):
                with act.Fori(0, PH) as i:
                    act.wait_ge(w_ready, ONE + PH + 1)
                    act.wait_ge(diag_ready, ONE + i * TOPK + t * PH * TOPK)
                    a.activation(w_st[:], w_all[:, bass.ds(i * W + t * TOPK, TOPK)], ACT.Copy).then_inc(w_staged, 1)
                    act.wait_ge(w_staged, i + t * PH + 1)
                    for s in range(TOPK):
                        q = t * PH * TOPK + s
                        act.wait_ge(v_used, i * TOPK + q + RING - 3)
                        a.activation(diag[s % 4][:], ident[:], ACT.Copy, scale=w_st[:, s:s + 1]).then_inc(diag_ready, 1)
                if t:
                    y_norm(0)
            for s in range(PH):
                q = 2 * PH * TOPK + s
                act.wait_ge(v_used, q + RING - 3)
                a.activation(diag_s[s % 4][:], gather8[:], ACT.Copy, scale=w_s[:, s:s + 1]).then_inc(diag_ready, 1)
            y_norm(1)
            y_norm(2)
            act.wait_ge(u_out, ONE + 32 * H)
            act.wait_ge(S_out, ONE + 16 * H)

        @block.vector
        def _(dve):
            v = nc.vector
            count = [0]

            def lo(n0, i=0, L=0):
                s, _, half = at_slot(n0)
                dve.wait_ge(hi_done, n0 + 1 + i * L)
                v.tensor_tensor(w_lo[n0 % 2][:], raw[s][:, :, half * P:(half + 1) * P],
                                w_hi[n0 % 2][:].bitcast(F32), ALU.subtract).then_inc(lo_done, 1)

            def norm(p, src, out):
                dve.wait_ge(ss_done, 3 * p + 3)
                v.tensor_scalar(mean_sq[:], ssq[:], 1.0 / D, EPS, ALU.mult, ALU.add).then_inc(ms_done, 1)
                dve.wait_ge(rt_done, p + 1)
                v.reciprocal(rstd[:], root[:]).then_inc(rs_done, 1)
                dve.wait_ge(rs_done, p + 1)
                for t in range(3):
                    q = P if t < 2 else TS
                    v.tensor_scalar(out[0:q, t, :], src[0:q, t, :], rstd[0:q, t:t + 1], None,
                                    ALU.mult).then_inc(xn_done, 1)

            def act_parts(p, gcol):
                for k in range(KT):
                    dve.wait_ge(ah_done, (2 * p) * KT + k + 1)
                    v.scalar_tensor_tensor(out=act_lo[:, k, :], in0=bank[2 + k % 6][:, 0:T],
                                           scalar=pcol[:, gcol + k:gcol + k + 1],
                                           in1=act_hi[:, k, :].bitcast(F32),
                                           op0=ALU.mult, op1=ALU.subtract).then_inc(al_done, 1)

            v.memset(ssq[:], 1.0).then_inc(chain, 1)
            for s in range(2):
                v.memset(u_pad[s][:], 0.0).then_inc(chain, 1)
            v.memset(gss[:], 1.0).then_inc(chain, 1)
            N0 = 4
            norm(0, x_tok, x_tok)
            lo(0)
            lo(1)
            act_parts(0, 80)
            lo(2)
            for m in range(H * KD):
                dve.wait_ge(la_mm, m + 1)
                v.tensor_scalar(la[:, m, :], bank[2 + m % 6][:, 0:T],
                                pcol[:, 80 + 2 * KT + m:81 + 2 * KT + m], None, ALU.add).then_inc(la_ev, 1)

            dve.wait_ge(la_step, 3)
            v.scalar_tensor_tensor(out=la[:], in0=la[:], scalar=0.0, in1=la_tmp[:], op0=ALU.min,
                                   op1=ALU.subtract).then_inc(la_step, 1)
            dve.wait_ge(la_step, 4)
            v.memset(attn[:], 1.0).then_inc(chain, 1)
            dve.wait_ge(chain, N0 + 1)
            for m in range(H * KD):
                for c in range(2):
                    run = la[:, m, c * P:(c + 1) * P]
                    v.tensor_tensor_scan(run, attn[:], run, 0.0, ALU.mult, ALU.add).then_inc(chain, 1)
            dve.wait_ge(chain, N0 + 1 + 2 * H * KD)
            mid = la[:, :, P // 2 - 1:P // 2 + P:P]
            last = la[:, :, P - 1:2 * P:P]
            v.tensor_scalar(cols[:, :, 0:2], mid, -1.0 / TAU, None, ALU.mult)
            v.tensor_scalar(cols[:, :, 2:4], mid, 1.0 / TAU, None, ALU.mult)
            v.tensor_scalar(cols[:, :, 4:6], last, 1.0 / TAU, None, ALU.mult).then_inc(la_step, 1)
            dve.wait_ge(la_step, 5)
            dve.sem_inc(la_ready, 1)

            with dve.Fori(0, 4) as i:
                for b in range(4):
                    lo(B_Q + b + 2, i, 4)

            def v_copy(n0, i, L):
                dve.wait_ge(v_tr, n0 - B_V + 1 + i * L)
                col = bass.ds((n0 - B_V) * P + i * (L * P), P) if L else slice((n0 - B_V) * P, (n0 - B_V + 1) * P)
                src = bank[MISC + n0 % 2]
                v.tensor_copy(v_tok[:, 0:2, col], src[:, 0:2 * P].rearrange("p (t c) -> p t c", t=2))
                v.tensor_copy(v_tok[0:TS, 2, col], src[0:TS, 2 * P:3 * P]).then_inc(post_done, 1)

            with dve.Fori(0, 4) as i:
                for b in range(4):
                    lo(B_V + b + 2, i, 4)
                    v_copy(B_V + b, i, 4)

            
            def head_step(i, b, link):
                n0 = B_SIX + b
                cg, t, half = b // 12, (b // 2) % 6, b % 2
                q = cg * 2 + half
                lo(n0 + 2, i, 24)
                if b == 1:
                    dve.wait_ge(staged, i * 9 + 9)
                dve.wait_ge(acc_read, ONE + n0 + 1 + i * 24)
                dve.wait_ge(post_done, ONE + posts(n0 - 1) + i * POSTS)
                up = u_pad[half]
                if t == 0:
                    v.tensor_tensor(tR[half][:], tR[half][:], tA[half][:], ALU.mult).then_inc(post_done, 1)
                elif t == 1:
                    v.scalar_tensor_tensor(out=gate[:, q, :], in0=gate[:, q, :], scalar=pcol_h[:, q:q + 1],
                                           in1=tR[half][:], op0=ALU.mult, op1=ALU.mult).then_inc(post_done, 1)
                elif t == 4:
                    wcol = lambda j: pcol_h[:, 4 + 4 * j + q:5 + 4 * j + q]
                    bcol = pcol_h[:, 16 + q:17 + q]
                    z, zs = tA[half], tA[half][:, TP:T]
                    link(v.tensor_tensor(up[:, 2:2 + T], tR[half][:], tA[half][:], ALU.mult))
                    dve.sem_inc(u_ready, 1)
                    link(v.tensor_scalar(z[:], up[:, 2:2 + T], wcol(2), bcol, ALU.mult, ALU.add))
                    for j in (1, 0):
                        v.scalar_tensor_tensor(out=z[:, 0:TP], in0=up[:, j:j + TP], scalar=wcol(j),
                                               in1=z[:, 0:TP], op0=ALU.mult, op1=ALU.add)
                        link(v.scalar_tensor_tensor(out=zs, in0=convT_h[:, q, j:2 * TS:2], scalar=wcol(j),
                                                    in1=zs, op0=ALU.mult, op1=ALU.add))
                    v.tensor_tensor(yb[:, q, :], yb[:, q, :], z[:], ALU.mult).then_inc(post_done, 1)
                elif t == 5:
                    v.tensor_tensor(yb[:, q, :], yb[:, q, :], tR[half][:], ALU.mult).then_inc(post_done, 1)

                for c in (0, 1):
                    if b == 8 * c + 2:
                        dve.wait_ge(exps, (i * 2 + c + 1) * (3 * KD + 1))
                        dve.wait_ge(attn_mm, ONE + i * 2 + c)
                        span = slice(c * P, (c + 1) * P)
                        for out, src, sc in ((dq, q_h, DK ** -0.5), (dk, k_h, 1.0), (dq0, q_h, DK ** -0.5),
                                             (dk1, k_h, 1.0)):
                            ins = v.scalar_tensor_tensor(out=out[:], in0=src[:, :, span], scalar=sc, in1=out[:],
                                                         op0=ALU.mult, op1=ALU.mult)
                        ins.then_inc(decayed, 1)
                    if b == 8 * c + 4:
                        dve.wait_ge(k_read, ONE + i * 2 + c + 1)
                        v.tensor_tensor(attn[:], bank[MISC][:, 0:P], causal[:], ALU.mult).then_inc(attn_ready, 1)
                    if b == 8 * c + 6:
                        dve.wait_ge(o_mm, ONE + i * 2 + c + 1)
                        if c == 0:
                            dve.wait_ge(S_out, ONE + i * 16)
                            for k in range(KD):
                                ins = v.tensor_copy(S[:, k, :], bank[KV0 + k][:])
                        else:
                            for k in range(KD):
                                ins = v.scalar_tensor_tensor(out=S[:, k, :], in0=S[:, k, :],
                                                             scalar=cols_h[:, k, 6 + c:7 + c],
                                                             in1=bank[KV0 + k][:], op0=ALU.mult, op1=ALU.add)
                        ins.then_inc(S_ready, 1)
                for c, at in ((0, 6), (1, 14), (2, 20)):
                    if b == at:
                        q_ = P if c < 2 else TS
                        dve.wait_ge(o_sum, i * 3 + c + 1)
                        dve.wait_ge(o_ready, ONE + i * 3 + c)
                        v.tensor_scalar(gss[0:q_, 3:4], gss[0:q_, c:c + 1], 1.0 / DV, EPS, ALU.mult,
                                        ALU.add).then_inc(o_mean, 1)
                    if b == at + 1:
                        q_ = P if c < 2 else TS
                        dve.wait_ge(o_root, i * 3 + c + 1)
                        v.reciprocal(gss[0:q_, 4:5], gss[0:q_, 3:4]).then_inc(o_rstd, 1)
                if b == 1:
                    dve.wait_ge(os_mm, ONE + i * (KD * TS))
                    for k in range(KD):
                        ins = v.scalar_tensor_tensor(
                            out=q_sel[:, k, :, :], in0=q_h[:, k, TP:T].unsqueeze(2).broadcast_to([P, TS, TS]),
                            scalar=DK ** -0.5, in1=eye8[:], op0=ALU.mult, op1=ALU.mult)
                    ins.then_inc(q_sel_ready, 1)
                M = KD * TS
                m = b - 2
                if 0 <= m < M:
                    if m == 0:
                        dve.wait_ge(ks_ready, i + 1)
                    dve.wait_ge(outer_mm, ONE + i * M + m)
                    v.tensor_scalar(ks_sel[m % 2][0:TS, :], ks_tok[0:TS, (m % KD) * P:(m % KD + 1) * P],
                                    ident[0:TS, m // KD:m // KD + 1], None, ALU.mult).then_inc(ks_sel_ready, 1)
                m = b - 3
                if 0 <= m < M:
                    dve.wait_ge(outer_mm, ONE + i * M + m + 1)
                    dve.wait_ge(s_in[m % 4], i * 64 + 16 * (m // 4) + 16)
                    v.scalar_tensor_tensor(out=s_ring[m % 4][:], in0=s_ring[m % 4][:],
                                           scalar=decS_h[:, m % KD, m // KD:m // KD + 1], in1=bank[OUTER][:],
                                           op0=ALU.mult, op1=ALU.add).then_inc(s_new, 1)

            with dve.Fori(0, H) as i:
                links = [0]
                base = N0 + 1 + 2 * H * KD

                def link(ins):
                    links[0] += 1
                    ins.then_inc(chain, 1)
                    dve.wait_ge(chain, i * N_LINKS + base + links[0])

                for b in range(SIX_PER_HEAD):
                    head_step(i, b, link)
                dve.wait_ge(oT_ready, ONE + i * 3 + 3)
                dve.wait_ge(post_done, ONE + posts(B_SIX + 23) + i * POSTS)
                link(v.tensor_tensor(gate[:], gate[:], oT[:], ALU.mult))
                for half in (0, 1):
                    v.tensor_tensor(mT[:, bass.ds(i * 2 + half * (KT // 2), 2), :], yb[:, 2 * half:2 * half + 2, :],
                                    gate[:, 2 * half:2 * half + 2, :], ALU.add).then_inc(m_ready, 1)
                assert links[0] == N_LINKS, links[0]
                dve.wait_ge(os_mm, ONE + i * (KD * TS) + KD * TS)
                dve.wait_ge(m_ready, i * 2 + 2)
                dve.sem_inc(head_done, 1)

            for k in range(0, KT, 2):
                dve.wait_ge(ah_done, KT + k + 2)
                v.tensor_tensor(act_lo[:, k:k + 2, :], mT[:, m_at(k):m_at(k) + 2, :],
                                act_hi[:, k:k + 2, :].bitcast(F32), ALU.subtract).then_inc(al_done, 2)

            def x_add(n0, i, L):
                if n0 == B_OUT:
                    dve.wait_ge(x2_in, 32)
                dve.wait_ge(v_tr, KT + n0 - B_OUT + 1 + i * L)
                col = bass.ds((n0 - B_OUT) * P + i * (L * P), P)
                src = bank[MISC + n0 % 2]
                v.tensor_tensor(x2_tok[:, 0:2, col], src[:, 0:2 * P].rearrange("p (t c) -> p t c", t=2),
                                x2_tok[:, 0:2, col], ALU.add)
                v.tensor_tensor(x2_tok[0:TS, 2, col], src[0:TS, 2 * P:3 * P], x2_tok[0:TS, 2, col],
                                ALU.add).then_inc(post_done, 1)

            with dve.Fori(0, 4) as i:
                for b in range(4):
                    lo(B_OUT + b + 2, i, 4)
                    x_add(B_OUT + b, i, 4)
            norm(1, x2_tok, xn_tok)
            act_parts(1, 80 + KT)
            dve.wait_ge(S_out, ONE + 16 * H)
            dve.wait_ge(u_out, ONE + 32 * H)
            for x in (sc, cand, val, best):
                ins = v.memset(x[:], 0.0)
            ins.then_inc(chain, 1)
            for x in (key_u, pos):
                ins = v.memset(x[:], 0)
            ins.then_inc(chain, 1)
            base = N0 + 1 + 2 * H * KD + H * N_LINKS + 2
            dve.wait_ge(chain, base)
            dve.sem_inc(cleared, 1)
            N_TOP = 22

            def retrieve(h0, i):
                steps = [0]

                def link(ins):
                    steps[0] += 1
                    ins.then_inc(chain, 1)
                    dve.wait_ge(chain, i * (2 * N_TOP) + base + h0 * N_TOP + steps[0])
                    dve.sem_inc(granted, 1)

                def top16(tiles):
                    for r in range(2):
                        eight = slice(8 * r, 8 * r + 8)
                        for src, vals, at in tiles:
                            ins = v.max(vals[:, eight], src)
                        link(ins)
                        for src, vals, at in tiles:
                            ins = v.max_index(at[:, eight], vals[:, eight], src)
                        link(ins)
                        if r == 0:
                            for src, vals, at in tiles:
                                ins = v.match_replace(src, vals[:, eight], src, NEG_BIG)
                            link(ins)

                rows = (P, P, TS)
                top16([(sc[0:rows[t], s, t, :], val[0:rows[t], s, t, :], key_u[0:rows[t], s, t, :])
                       for s in range(2) for t in range(3)])
                for t in range(3):
                    q = rows[t]
                    ins = v.tensor_tensor(cand[0:q, t, :].rearrange("p (a b) -> p a b", a=TOPK),
                                          val[0:q, 0, t, :].unsqueeze(2).broadcast_to([q, TOPK, TOPK]),
                                          val[0:q, 1, t, :].unsqueeze(1).broadcast_to([q, TOPK, TOPK]), ALU.add)
                link(ins)
                top16([(cand[0:rows[t], t, :], best[0:rows[t], t, :], pos[0:rows[t], t, :]) for t in range(3)])
                link(v.tensor_tensor(soft[:], best[:], best[:, :, 0:1].broadcast_to([P, 3, TOPK]), ALU.subtract))
                dve.sem_inc(soft_in, 1)
                v.tensor_copy(key_f[:], key_u[:])
                v.tensor_scalar(pos_u[:, 0], pos[:], 4, None, ALU.logical_shift_right)
                link(v.tensor_scalar(pos_u[:, 1], pos[:], 15, None, ALU.bitwise_and))
                link(v.tensor_copy(pos_f[:], pos_u[:]))
                for s in range(2):
                    ins = v.tensor_tensor(hot[s][:], pos_f[:, s].unsqueeze(3).broadcast_to([P, 3, TOPK, TOPK]),
                                          iota16[:].unsqueeze(1).unsqueeze(1).broadcast_to([P, 3, TOPK, TOPK]),
                                          ALU.is_equal)
                link(ins)
                for s in range(2):
                    ins = v.tensor_tensor(hot[s][:], hot[s][:],
                                          key_f[:, s].unsqueeze(2).broadcast_to([P, 3, TOPK, TOPK]), ALU.mult)
                link(ins)
                for s in range(2):
                    ins = v.tensor_reduce(key_sel[:, s], hot[s][:], AX_X, ALU.add)
                link(ins)
                dve.wait_ge(soft_e, i * 2 + h0 + 1)
                v.scalar_tensor_tensor(out=picks[:, 0], in0=key_sel[:, 0], scalar=float(NKEY), in1=key_sel[:, 1],
                                       op0=ALU.mult, op1=ALU.add)
                link(v.tensor_reduce(soft_s[:], soft[:], AX_X, ALU.add))
                link(v.reciprocal(soft_r[:], soft_s[:]))
                link(v.tensor_tensor(picks[:, 1], soft[:], soft_r[:].unsqueeze(2).broadcast_to([P, 3, TOPK]), ALU.mult))
                dve.sem_inc(picked, 1)
                W = 2 * TOPK
                to = bass.ds(i * (2 * W) + h0 * W, W)
                v.tensor_copy(idx_all[:, to], picks[:, 0, 0:2, :].rearrange("p t k -> p (t k)"))
                v.tensor_copy(g_all[:, to], picks[:, 1, 0:2, :].rearrange("p t k -> p (t k)"))
                dve.wait_ge(spread_mm, i * 2 + h0 + 1)
                link(v.tensor_tensor(own[:], bank[4][:, 0:2 * TOPK].rearrange("p (s k) -> p s k", s=2),
                                     own16[:].unsqueeze(1).broadcast_to([P, 2, TOPK]), ALU.mult))
                link(v.tensor_reduce(own_s[:], own[:], AX_X, ALU.add))
                one = bass.ds(i * 2 + h0, 1)
                v.tensor_copy(idx_s[:, one], own_s[:, 0:1])
                v.tensor_copy(g_s[:, one], own_s[:, 1:2]).then_inc(retrieved, 1)
                dve.wait_ge(retrieved, i * 2 + h0 + 1)
                dve.sem_inc(granted, 1)
                assert steps[0] == N_TOP, steps[0]

            def scores(n0, i, L, more):
                if more:
                    lo(n0 + 2, i, L)
                dve.wait_ge(v_tr, 2 * KT + n0 - B_QRY + 1 + i * L)
                s = (n0 - B_QRY) % 2
                src = bank[MISC + n0 % 2]
                v.tensor_copy(sc[:, s, 0:2, :], src[:, 0:2 * P].rearrange("p (t c) -> p t c", t=2))
                v.tensor_copy(sc[0:TS, s, 2, :], src[0:TS, 2 * P:3 * P]).then_inc(post_done, 1)

            def query_head(h0, i, L, more):
                for half in range(2):
                    scores(B_QRY + 2 * h0 + half, i, L, more)
                dve.wait_ge(post_done, ONE + posts(B_QRY + 2 * h0 + 1) + i * L)
                dve.sem_inc(granted, 1)
                retrieve(h0, i)

            with dve.Fori(0, PH // 2 - 1) as i:
                for h in range(2):
                    query_head(h, i, 4, True)
            for h in range(PH - 2, PH):
                query_head(h, 0, 0, h < PH - 1)

            dve.wait_ge(row_in, 16)
            dve.wait_ge(tr_done, 2 * KT)
            for t in (2, 0, 1):
                q = P if t < 2 else TS
                v.tensor_tensor(xn_tok[0:q, t, :], xn_tok[0:q, t, :], g_row[0:q, :], ALU.mult).then_inc(h2_ready, 1)
            dve.wait_ge(mm_done, B_END)
            v.memset(zeros[:], 0.0).then_inc(chain, 1)
            dve.wait_ge(chain, base + PH * N_TOP + 1)
            dve.sem_inc(cleared, 1)

            W = 2 * TOPK
            dve.sem_inc(u_used, RING)
            dve.wait_ge(h2_ready, 3)
            with dve.Fori(0, PH) as i:
                dve.wait_ge(gelu_done, ONE + i)
                dve.sem_inc(granted, 1)
                for s in range(W):
                    k = s % RING
                    dve.wait_ge(ring_in[k], i * (16 * W // RING) + 16 * (s // RING + 1))
                    v.tensor_tensor_reduce(ring[k][:], ring[k][:], xn_tok[:, s // TOPK, :], 1.0, 0.0, ALU.mult,
                                           ALU.add, dots[:, s:s + 1]).then_inc(u_used, 1)
                dve.wait_ge(gelu_done, ONE + i + 1)
                v.tensor_tensor(w_all[:, bass.ds(i * W, W)], gelu[:], g_all[:, bass.ds(i * W, W)],
                                ALU.mult).then_inc(w_ready, 1)
            dve.wait_ge(rep_ready, 4)
            for s in range(PH):
                dve.wait_ge(ring_in[s], 16 * (PH * W // RING + 1))
                v.tensor_tensor_reduce(ring[s][:], ring[s][:], xs_rep[:], 1.0, 0.0, ALU.mult, ALU.add,
                                       dots_s[:, s:s + 1]).then_inc(v_used, 1)
            dve.wait_ge(gelu_done, ONE + PH + 1)
            v.tensor_tensor(w_s[:], gelu[:, 0:PH], g_s[:], ALU.mult).then_inc(w_ready, 1)

            dve.wait_ge(row_in, 32)
            for t in range(3):
                q = P if t < 2 else TS
                if t < 2:
                    dve.wait_ge(sum_ready, t + 1)
                else:
                    dve.wait_ge(v_used, RING + 2 * PH * TOPK + PH)
                for j in range(4):
                    part = x2_tok[0:q, t, j * 512:(j + 1) * 512]
                    v.tensor_tensor(part, bank[4 * (t % 2) + j][0:q, :], part, ALU.add).then_inc(y_sum, 1)
                dve.wait_ge(y_ss, t + 1)
                v.tensor_scalar(mean_sq[0:q, t:t + 1], ssq[0:q, t:t + 1], 1.0 / D, EPS, ALU.mult,
                                ALU.add).then_inc(y_mean, 1)
                dve.wait_ge(y_root, t + 1)
                v.reciprocal(rstd[0:q, t:t + 1], root[0:q, t:t + 1]).then_inc(y_rstd, 1)
                dve.wait_ge(y_rstd, t + 1)
                v.scalar_tensor_tensor(out=x2_tok[0:q, t, :], in0=x2_tok[0:q, t, :], scalar=rstd[0:q, t:t + 1],
                                       in1=g_row[0:q, :], op0=ALU.mult, op1=ALU.mult).then_inc(y_ready, 1)

        @block.tensor
        def _(pe):
            mm = nc.tensor.matmul
            tr = nc.tensor.transpose

            def turn(p, src):
                for k in range(KT):
                    if k < 3 and p == 0:
                        pe.wait_ge(xn_done, 3)
                    if k == 0:
                        pe.wait_ge(xn_done, 3 * p + 3)
                    if k >= 6:
                        pe.wait_ge(al_done, 2 * p * KT + k - 5)
                    b = bank[2 + k % 6]
                    for t in range(3):
                        q = P if t < 2 else TS
                        ins = tr(b[:, t * P:t * P + q], src[0:q, t, k * P:(k + 1) * P], ident[0:q, 0:q])
                    ins.then_inc(tr_done, 1)

            def project(n0, i=0, L=0):
                pe.wait_ge(lo_done, n0 + 1 + i * L)
                if n0:
                    pe.wait_ge(acc_read, ONE + n0 - 1 + i * L)
                out = bank[ACC + n0 % 2][:, 0:T]
                for k in range(KT):
                    hi_, lo_ = w_hi[n0 % 2][:, k, :], w_lo[n0 % 2][:, k, :]
                    mm(out, hi_, act_hi[:, k, :], start=(k == 0), stop=False)
                    mm(out, hi_, act_lo[:, k, :], start=False, stop=False)
                    ins = mm(out, lo_, act_hi[:, k, :], start=False, stop=(k == KT - 1))
                ins.then_inc(mm_done, 1)

            def to_tokens(n0, i=0, L=0):
                pe.wait_ge(acc_read, ONE + n0 + 1 + i * L)
                pe.wait_ge(post_done, ONE + posts(n0 - 2) + i * L)
                b = bank[MISC + n0 % 2]
                st = stage[n0 % 2]
                for t in range(2):
                    tr(b[:, t * P:(t + 1) * P], st[:, t * P:(t + 1) * P], ident[:])
                mm(b[0:TS, 2 * P:3 * P], st[:, TP:T], ident[:], start=True, stop=True).then_inc(v_tr, 1)

            pe.wait_ge(consts, N_CONSTS)
            pe.wait_ge(par_in, 16 * N_PAR)
            tr(bank[2][:, 0:120], prow[0:120, :], ident[0:120, 0:120]).then_inc(par_T, 1)
            pe.wait_ge(keys_in, 16)
            for s in range(2):
                ins = tr(bank[3][:, s * P:(s + 1) * P], krow[:, s, :], ident[:])
            ins.then_inc(par_T, 1)
            pe.wait_ge(conv_in, 16)
            R = 2 * TS
            for k in range(KT):
                ins = tr(bank[4][:, k * R:(k + 1) * R], crow[0:R, k * P:(k + 1) * P], ident[0:R, 0:R])
            ins.then_inc(par_T, 1)
            pe.wait_ge(par_ready, 3)
            turn(0, x_tok)
            pe.wait_ge(al_done, KT)
            project(0)
            pe.wait_ge(wau_in, 16)
            pe.wait_ge(acc_read, ONE + 1)
            for m in range(H * KD):
                if m >= 6:
                    pe.wait_ge(la_ev, m - 5)
                mm(bank[2 + m % 6][:, 0:T], wau[0:RANK, m * P:(m + 1) * P], alr[0:RANK, :],
                   start=True, stop=True).then_inc(la_mm, 1)
            with pe.Fori(0, 4) as i:
                for b in range(4):
                    project(B_Q + b, i, 4)
            pe.wait_ge(la_ev, H * KD)
            project(B_V)
            with pe.Fori(0, 3) as i:
                for b in range(4):
                    project(B_V + b + 1, i, 4)
                    to_tokens(B_V + b, i, 4)
            for b in range(KT - 4, KT):
                if b + 1 < KT:
                    project(B_V + b + 1)
                to_tokens(B_V + b)

            def head_step(i, b):
                M = KD * TS
                project(B_SIX + b, i, 24)
                for c in (0, 1):
                    if b == 8 * c + 3:
                        pe.wait_ge(decayed, ONE + i * 2 + c + 1)
                        pe.wait_ge(attn_ready, ONE + i * 2 + c)
                        pe.wait_ge(k_read, ONE + i * 2 + c)
                        for k in range(KD):
                            mm(bank[MISC][:, 0:P], dk[:, k, :], dq[:, k, :], start=(k == 0), stop=(k == KD - 1))
                        for k in range(KD):
                            ins = tr(bank[MISC][:, (1 + k) * P:(2 + k) * P], dk1[:, k, :], ident[:])
                        ins.then_inc(attn_mm, 1)
                    if b == 8 * c + 5:
                        pe.wait_ge(attn_ready, ONE + i * 2 + c + 1)
                        pe.wait_ge(k_read, ONE + i * 2 + c + 1)
                        pe.wait_ge(o_ready, ONE + i * 3 + c)
                        if c == 0:
                            pe.wait_ge(ks_ready, i + 1)
                        else:
                            pe.wait_ge(S_ready, i * 2 + 1)
                        pe.wait_ge(oT_ready, ONE + i * 3 + c)
                        pe.wait_ge(u_read, ONE + i * 4 + 2 * c)
                        mm(bank[OB][:], attn[:], v_h[:, c, :], start=True, stop=(c == 0))
                        if c:
                            for k in range(KD):
                                mm(bank[OB][:], dq0[:, k, :], S[:, k, :], start=False, stop=(k == KD - 1))
                        for k in range(KD):
                            ins = mm(bank[KV0 + k][:], k_tok[:, k, :], v_h[:, c, :], start=True, stop=True)
                        ins.then_inc(o_mm, 1)
                for c, at in ((0, 7), (1, 15), (2, 21)):
                    if b == at:
                        pe.wait_ge(o_ready, ONE + i * 3 + c + 1)
                        if c < 2:
                            pe.wait_ge(S_ready, i * 2 + c + 1)
                        pe.wait_ge(oT_ready, ONE + i * 3 + c)
                        q, src = P if c < 2 else TS, o_sb
                        pe.sem_inc(granted, 1)
                        for d in range(HV):
                            ins = tr(bank[KV1][:, d * q:(d + 1) * q], src[0:q, d * P:(d + 1) * P], ident[0:q, 0:q])
                        ins.then_inc(o_tr, 1)
                if b == 1:
                    pe.wait_ge(staged, i * 9 + 9)
                    pe.wait_ge(o_ready, ONE + i * 3)
                    for k in range(KD):
                        ins = mm(bank[OB][0:TS, k * P:(k + 1) * P], k_h[:, k, TP:T], ident[:], start=True, stop=True)
                    ins.then_inc(ks_mm, 1)
                m = b - 3
                if 0 <= m < M:
                    pe.wait_ge(ks_sel_ready, i * M + m + 1)
                    pe.wait_ge(s_new, ONE + i * M + m)
                    mm(bank[OUTER][:], ks_sel[m % 2][0:TS, :], v_h[0:TS, 2, :], start=True, stop=True).then_inc(outer_mm, 1)
                m = b - 4
                if 0 <= m < M:
                    if m == 0:
                        pe.wait_ge(q_sel_ready, i + 1)
                        pe.wait_ge(o_ready, ONE + i * 3)
                    pe.wait_ge(s_new, ONE + i * M + m + 1)
                    mm(bank[OS][0:TS, :], q_sel[:, m % KD, m // KD, :], s_ring[m % 4][:], start=(m == 0),
                       stop=(m == M - 1)).then_inc(os_mm, 1)
                if (b // 2) % 6 == 5:
                    q = (b // 12) * 2 + b % 2
                    pe.wait_ge(u_ready, i * 4 + q + 1)
                    pe.wait_ge(u_read, ONE + i * 4 + q)
                    pe.wait_ge(oT_ready, ONE + i * 3 + (1 if q < 2 else 3))
                    mm(bank[KV1][0:2 + TS, 0:P], u_pad[b % 2][:, TP:2 + T], ident[:],
                       start=True, stop=True).then_inc(u_tr, 1)

            with pe.Fori(0, H) as i:
                for b in range(SIX_PER_HEAD):
                    head_step(i, b)
            pe.wait_ge(al_done, 2 * KT)
            project(B_OUT)
            with pe.Fori(0, 3) as i:
                for b in range(4):
                    project(B_OUT + b + 1, i, 4)
                    to_tokens(B_OUT + b, i, 4)
            for b in range(KT - 4, KT):
                if b + 1 < KT:
                    project(B_OUT + b + 1)
                to_tokens(B_OUT + b)
            turn(1, xn_tok)
            pe.wait_ge(al_done, 3 * KT)

            def scores(n0, i=0, L=0):
                pe.wait_ge(acc_read, ONE + n0 + 1 + i * L)
                pe.wait_ge(post_done, ONE + posts(n0 - 2) + i * L)
                b, st, s = bank[MISC + n0 % 2], stage[n0 % 2], (n0 - B_QRY) % 2
                for t in range(2):
                    mm(b[:, t * P:(t + 1) * P], st[:, t * P:(t + 1) * P], keysT[:, s, :], start=True, stop=True)
                mm(b[0:TS, 2 * P:3 * P], st[:, TP:T], keysT[:, s, :], start=True, stop=True).then_inc(v_tr, 1)

            def spread_picks(h0, i):
                pe.wait_ge(picked, i * 2 + h0 + 1)
                mm(bank[4][:, 0:2 * TOPK], spread[0:TS, :], picks[0:TS, :, 2, :], start=True,
                   stop=True).then_inc(spread_mm, 1)

            project(B_QRY)
            with pe.Fori(0, PH // 2 - 1) as i:
                for h in range(2):
                    for half in range(2):
                        n0 = B_QRY + 2 * h + half
                        project(n0 + 1, i, 4)
                        scores(n0, i, 4)
                    spread_picks(h, i)
            for h in range(PH - 2, PH):
                for half in range(2):
                    n0 = B_QRY + 2 * h + half
                    if n0 + 1 < B_END:
                        project(n0 + 1)
                    scores(n0)
                spread_picks(h, 0)

            pe.wait_ge(h2_ready, 1)
            pe.wait_ge(retrieved, PH)
            for j in range(4):
                ins = mm(bank[4 + j][:], spread[0:TS, :], xn_tok[0:TS, 2, j * 512:(j + 1) * 512], start=True, stop=True)
            ins.then_inc(rep_mm, 1)

            def open_sums(t, q):
                for j in range(4):
                    mm(bank[4 * (t % 2) + j][0:q, :], zeros[:, 0:q], zeros[:], start=True, stop=False)

            pe.wait_ge(cleared, 2)
            pe.wait_ge(rep_ready, 4)
            n_u = 2 * PH * TOPK // RING + 1
            for t in range(2):
                open_sums(t, P)
                with pe.Fori(0, PH) as i:
                    for s in range(TOPK):
                        q = t * PH * TOPK + s
                        k = s % RING
                        pe.wait_ge(diag_ready, ONE + i * TOPK + q + 1)
                        pe.wait_ge(ring_in[k], i * (16 * TOPK // RING) + 16 * (n_u + q // RING + 1))
                        for j in range(4):
                            ins = mm(bank[4 * t + j][:], diag[s % 4][:], ring[k][:, j * 512:(j + 1) * 512],
                                     start=False, stop=False, skip_group_check=True)
                        ins.then_inc(v_used, 1)
                for j in range(4):
                    ins = mm(bank[4 * t + j][:], zeros[:, 0:P], zeros[:], start=False, stop=True)
                ins.then_inc(sum_ready, 1)
            pe.wait_ge(y_sum, 4)
            open_sums(2, TS)
            for s in range(PH):
                q = 2 * PH * TOPK + s
                pe.wait_ge(diag_ready, ONE + q + 1)
                pe.wait_ge(ring_in[s], 16 * (n_u + q // RING + 1))
                for j in range(4):
                    ins = mm(bank[j][0:TS, :], diag_s[s % 4][:], ring[s][:, j * 512:(j + 1) * 512],
                             start=False, stop=(s == PH - 1))
                ins.then_inc(v_used, 1)


_INS = ["x_prompt", "x_sample", "state_gla", "state_conv", "norm1_g", "w_in", "w_alpha_up", "b_alpha",
        "gla_norm_g", "conv_w", "conv_b", "w_out", "norm2_g", "w_query", "sub_keys", "expert_u", "expert_v",
        "norm_f_g"]


def kernel(**inputs):
    import numpy as np
    import concourse.bacc as bacc
    from concourse.bass_utils import run_bass_kernel_spmd

    nc = bacc.Bacc("TRN2", target_bir_lowering=False, num_devices=1)
    arrays, args = {}, []
    for name in _INS:
        x = np.ascontiguousarray(inputs[name])
        arrays[f"in_{name}"] = x
        args.append(nc.dram_tensor(f"in_{name}", x.shape, mybir.dt.from_np(x.dtype), kind="ExternalInput").ap())
    xp, xs, sg, sc = (inputs[n].shape for n in _INS[:4])
    outs = [xp, xs, (sg[0], xp[0], *sg[2:]), (sc[0], xp[0], *sc[2:]), sg, sc]
    for n, shape in enumerate(outs):
        args.append(nc.dram_tensor(f"out_{n}", tuple(shape), F32, kind="ExternalOutput").ap())
    hybrid_step(nc, *args)
    r = run_bass_kernel_spmd(nc, [arrays], core_ids=[0])
    return tuple(r.results[0][f"out_{n}"] for n in range(len(outs)))
```

```python
from contextlib import ExitStack

import concourse.bass as bass
from concourse import mybir

F32 = mybir.dt.float32
F32R = mybir.dt.float32r
U32 = mybir.dt.uint32
ALU = mybir.AluOpType
ACT = mybir.ActivationFunctionType
AX_X = mybir.AxisListType.X

P = 128
EPS = 1e-6
CHUNK = 128
TAU = 16.0
ONE = 1
NEG_BIG = -3.0e38


def hybrid_step(nc, x_prompt, x_sample, state_gla, state_conv, norm1_g, w_in, w_alpha_up, b_alpha,
                gla_norm_g, conv_w, conv_b, w_out, norm2_g, w_query, sub_keys, expert_u, expert_v,
                norm_f_g, y_prompt, y_sample, gla_prompt, conv_prompt, gla_sample, conv_sample):
    D = x_prompt.shape[2]
    TP, TS = x_prompt.shape[1], x_sample.shape[0]
    T = TP + TS
    KT = D // P
    H, DK, DV = state_gla.shape[2:]
    KD = DK // P
    HV = DV // P
    RANK = w_alpha_up.shape[1]
    NKEY = sub_keys.shape[2]
    PH, TOPK = 8, 16
    assert T == 2 * P + TS and KD == 2 and HV == 4 and TS * TOPK == P and NKEY == P

    COL_K = H * DK
    COL_V = 2 * H * DK
    COL_R = COL_V + H * DV
    COL_ALR = COL_R + H * DV
    COL_CB = COL_ALR + RANK
    COL_CC, COL_CX, COL_GA, COL_GB = (COL_CB + D * j for j in (1, 2, 3, 4))
    SIX = (COL_R, COL_GA, COL_CB, COL_CC, COL_CX, COL_GB)

    B_Q, B_K, B_V, B_SIX = 1, 1 + H * KD, 1 + 2 * H * KD, 1 + 2 * H * KD + KT
    SIX_PER_HEAD = 2 * 6 * 2
    B_OUT = B_SIX + H * SIX_PER_HEAD
    B_QRY = B_OUT + KT
    B_END = B_QRY + 2 * PH
    N_PAR = 5 * H + 3
    N_CONSTS = 34
    N_LINKS = 17
    POSTS = 2 * 4 * 2

    def posts(n0):
        n = min(max(n0 + 1 - B_V, 0), KT)
        for b in range(min(max(n0 + 1 - B_SIX, 0), H * SIX_PER_HEAD)):
            n += (b // 2) % 6 not in (2, 3)
        return n + max(n0 + 1 - B_OUT, 0)
    B_LATE = B_QRY + 2

    x_p = x_prompt.rearrange("b (t p) d -> p (b t) d", p=P)
    x_s = x_sample.rearrange("b s d -> (b s) d")
    win = w_in.rearrange("o (k p) n -> p (o k) n", p=P)
    wout = w_out.rearrange("o (k p) n -> p (o k) n", p=P)
    wqry = w_query.rearrange("o (k p) n -> p (o k) n", p=P)
    eu = expert_u.rearrange("o e d -> (o e) d")
    ev = expert_v.rearrange("o e d -> (o e) d")
    st_in = state_gla.rearrange("o j h (k p) v -> p (o h) k j v", p=P)
    st_out = gla_sample.rearrange("o j h (k p) v -> p (o h) k j v", p=P)
    stp_out = gla_prompt.rearrange("o b h (k p) v -> p (o b h) k v", p=P)

    with ExitStack() as ctx:
        top = (nc.sbuf_base + 63) // 64 * 64
        where = [top]

        def sb_at(name, shape, dt, at):
            return nc.alloc_sbuf_tensor_at(name, shape, dt, offset=at)

        def room(nbytes):
            at = where[0]
            where[0] += (nbytes + 31) // 32 * 32
            assert where[0] <= nc.sbuf_usable_end, (where[0], nc.sbuf_usable_end)
            return at

        def size(shape):
            n = 4
            for s in shape[1:]:
                n *= s
            return n

        def sb(name, shape, dt=F32):
            return sb_at(name, shape, dt, room(size(shape)))

        def sem(name):
            return ctx.enter_context(nc.semaphore(name))

        ident = sb("ident", [P, P])
        causal = sb("causal", [P, P])
        eye8 = sb("eye8", [P, TS, TS])
        spread = sb("spread", [P, P])
        gather8 = sb("gather8", [P, TS])
        same_j = sb("same_j", [P, P])
        same_h = sb("same_h", [P, PH])
        own16 = sb("own16", [P, TOPK])
        iota16 = sb("iota16", [P, TOPK])
        pcol = sb("pcol", [P, 120])
        keysT = sb("keysT", [P, 2, NKEY])
        ssq = sb("ssq", [P, 3])
        mean_sq = sb("mean_sq", [P, 3])
        root = sb("root", [P, 3])
        rstd = sb("rstd", [P, 3])
        keep = where[0]

        at_act = where[0]
        act_hi = sb("act_hi", [P, KT, T], F32R)
        act_lo = sb("act_lo", [P, KT, T], F32R)
        at_raw = where[0]
        raw = [sb(f"raw{s}", [P, KT, P]) for s in range(4)]
        at_w = where[0]
        w_hi = [sb(f"w_hi{s}", [P, KT, P], F32R) for s in range(2)]
        w_lo = [sb(f"w_lo{s}", [P, KT, P], F32R) for s in range(2)]
        at_qk = room(4 * KT * T)
        qk = sb_at("qk", [P, KT, T], F32, at_qk)
        mT = sb_at("mT", [P, KT, T], F32, at_qk)
        at_la = room(4 * H * KD * T)
        la = sb_at("la", [P, H * KD, T], F32, at_la)
        at_tok = room(4 * 3 * D)
        x_tok = sb_at("x_tok", [P, 3, D], F32, at_tok)
        v_tok = sb_at("v_tok", [P, 3, D], F32, at_tok)
        x2_tok = sb_at("x2_tok", [P, 3, D], F32, at_tok)
        at_head = where[0]
        v_h = sb("v_h", [P, 3, DV])
        q_h = sb("q_h", [P, KD, T])
        k_h = sb("k_h", [P, KD, T])
        la_h = sb("la_h", [P, KD, T])
        la_tmp = sb_at("la_tmp", [P, H * KD, T], F32, at_head)
        cols = sb("cols", [P, H * KD, 8])
        cols_h = sb("cols_h", [P, KD, 8])
        decS = sb("decS", [P, H * KD, TS])
        decS_h = sb("decS_h", [P, KD, TS])
        pcol_h = sb("pcol_h", [P, 20])
        convT = sb("convT", [P, KT, 2 * TS])
        convT_h = sb("convT_h", [P, HV, 2 * TS])
        dq = sb("dq", [P, KD, P])
        dk = sb("dk", [P, KD, P])
        dq0 = sb("dq0", [P, KD, P])
        dk1 = sb("dk1", [P, KD, P])
        k_tok = sb("k_tok", [P, KD, P])
        attn = sb("attn", [P, P])
        S = sb("S", [P, KD, DV])
        o_sb = sb("o_sb", [P, DV])
        oT = sb("oT", [P, HV, T])
        gss = sb("gss", [P, 8])
        at_ring = room(4 * 4 * DV)
        s_ring = [sb_at(f"s_ring{s}", [P, DV], F32, at_ring + 4 * s * DV) for s in range(4)]
        sq_junk = sb_at("sq_junk", [P, D], F32, at_ring)
        q_sel = sb("q_sel", [P, KD, TS, TS])
        ks_tok = sb("ks_tok", [P, DK])
        ks_sel = [sb(f"ks_sel{s}", [P, P]) for s in range(2)]
        tA = [sb(f"tA{s}", [P, T]) for s in range(2)]
        tR = [sb(f"tR{s}", [P, T]) for s in range(2)]
        u_pad = [sb(f"u_pad{s}", [P, 2 + T]) for s in range(2)]
        at_gate = where[0]
        gate = sb("gate", [P, HV, T])
        yb = sb("yb", [P, HV, T])
        u_rows = sb("u_rows", [P, HV * P])
        wau = sb_at("wau", [P, H * DK], F32, at_gate)
        prow = sb_at("prow", [P, P], F32, at_head)
        krow = sb_at("krow", [P, 2, P], F32, at_head + 512)
        crow = sb_at("crow", [P, D], F32, at_head + 2048)
        alr = sb_at("alr", [P, T], F32, at_gate + size([P, HV, T]))
        stage = [sb_at(f"stage{s}", [P, T], F32, at_head + 1056 * s) for s in range(2)]

        bank = [ctx.enter_context(nc.psum_tensor(f"bank{b}", [P, 512], F32)) for b in range(8)]
        ACC, MISC, OB, KV0, KV1, OS, OUTER = 0, 2, 3, 4, 5, 6, 7

        xn_tok = sb_at("xn_tok", [P, 3, D], F32, at_qk)
        assert at_qk + size([P, 3, D]) <= at_tok
        where[0] = at_head + 2112
        g_row = sb("g_row", [P, D])
        q_s = sb("q_s", [P, 2, PH, TS])
        sc = sb("sc", [P, 2, 2, NKEY])
        cand = sb("cand", [P, 2, TOPK * TOPK])
        hot = [sb(f"hot{s}", [P, 2, TOPK, TOPK]) for s in range(2)]
        val = sb("val", [P, 2, 2, TOPK])
        key_u = sb("key_u", [P, 2, 2, TOPK], U32)
        key_f = sb("key_f", [P, 2, 2, TOPK])
        best = sb("best", [P, 2, TOPK])
        pos = sb("pos", [P, 2, TOPK], U32)
        pos_u = sb("pos_u", [P, 2, 2, TOPK], U32)
        pos_f = sb("pos_f", [P, 2, 2, TOPK])
        key_sel = sb("key_sel", [P, 2, 2, TOPK])
        soft = sb("soft", [P, 2, TOPK])
        soft_s = sb("soft_s", [P, 2])
        soft_r = sb("soft_r", [P, 2])
        picks = sb("picks", [P, 2, 2, TOPK])
        wide = sb("wide", [P, 2, PH, TOPK])
        own = sb("own", [P, 2, PH, TOPK])
        own_s = sb("own_s", [P, 2, PH])
        idx_all = sb("idx_all", [P, PH * 2 * TOPK], U32)
        g_all = sb("g_all", [P, PH * 2 * TOPK])
        w_all = sb("w_all", [P, PH * 2 * TOPK])
        idx_s = sb("idx_s", [P, PH], U32)
        g_s = sb("g_s", [P, PH])
        w_s = sb("w_s", [P, PH])
        dots = sb("dots", [P, 2 * TOPK])
        dots_s = sb("dots_s", [P, PH])
        idx_st = sb("idx_st", [P, 8], U32)
        RING = 8
        ring_at = [room(size([P, D])) for _ in range(3)]
        ring_at += [at_tok + t * size([P, D]) for t in range(3)] + [at_raw + s * size([P, D]) for s in (2, 3)]
        ring = [sb_at(f"ring{s}", [P, D], F32, at) for s, at in enumerate(ring_at)]
        where[0] = at_act
        xs_rep = sb("xs_rep", [P, D])
        y_tok = sb("y_tok", [P, 3, D])
        assert where[0] <= at_raw
        where[0] = at_w
        y_sq = sb("y_sq", [P, D])
        diag = [sb(f"diag{s}", [P, P]) for s in range(4)]
        diag_s = [sb(f"diag_s{s}", [P, TS]) for s in range(4)]
        zeros = sb("zeros", [P, 512])
        assert where[0] <= at_qk
        DVE_SLOTS = (3, 7)
        PE_SLOTS = tuple(k for k in range(RING) if k not in DVE_SLOTS)
        N_DVE, N_PE = len(DVE_SLOTS), len(PE_SLOTS)
        x2_dram = nc.dram_tensor("x2_spill", [P, 3, D], F32, kind="Internal").ap()

        consts = sem("consts")
        x_in = sem("x_in")
        par_in = sem("par_in")
        conv_in = sem("conv_in")
        keys_in = sem("keys_in")
        wau_in = sem("wau_in")
        par_T = sem("par_T")
        par_ready = sem("par_ready")
        raw_in = [sem(f"raw_in{s}") for s in range(4)]
        hi_done = sem("hi_done")
        lo_done = sem("lo_done")
        mm_done = sem("mm_done")
        acc_read = sem("acc_read")
        post_done = sem("post_done")
        ss_done = sem("ss_done")
        ms_done = sem("ms_done")
        rt_done = sem("rt_done")
        rs_done = sem("rs_done")
        xn_done = sem("xn_done")
        tr_done = sem("tr_done")
        ah_done = sem("ah_done")
        al_done = sem("al_done")
        la_mm = sem("la_mm")
        la_ev = sem("la_ev")
        la_step = sem("la_step")
        la_ready = sem("la_ready")
        v_tr = sem("v_tr")
        staged = sem("staged")
        head_done = sem("head_done")
        exps = sem("exps")
        decayed = sem("decayed")
        attn_mm = sem("attn_mm")
        k_read = sem("k_read")
        attn_ready = sem("attn_ready")
        o_mm = sem("o_mm")
        o_sum = sem("o_sum")
        o_mean = sem("o_mean")
        o_root = sem("o_root")
        o_rstd = sem("o_rstd")
        o_ready = sem("o_ready")
        o_tr = sem("o_tr")
        oT_ready = sem("oT_ready")
        S_ready = sem("S_ready")
        S_out = sem("S_out")
        ks_mm = sem("ks_mm")
        ks_ready = sem("ks_ready")
        q_sel_ready = sem("q_sel_ready")
        ks_sel_ready = sem("ks_sel_ready")
        s_in = [sem(f"s_in{s}") for s in range(4)]
        s_out = [sem(f"s_out{s}") for s in range(4)]
        outer_mm = sem("outer_mm")
        s_new = sem("s_new")
        os_mm = sem("os_mm")
        u_ready = sem("u_ready")
        u_tr = sem("u_tr")
        u_read = sem("u_read")
        u_out = sem("u_out")
        chain = sem("chain")
        m_ready = sem("m_ready")
        granted = sem("granted")
        conv_copy = sem("conv_copy")
        x2_in = sem("x2_in")

        cleared = sem("cleared")
        soft_in = sem("soft_in")
        soft_e = sem("soft_e")
        picked = sem("picked")
        spread_mm = sem("spread_mm")
        retrieved = sem("retrieved")
        row_in = sem("row_in")
        h2_ready = sem("h2_ready")
        rep_mm = sem("rep_mm")
        rep_ready = sem("rep_ready")
        idx_staged = sem("idx_staged")
        ring_in = [sem(f"ring_in{s}") for s in range(RING)]
        u_used = sem("u_used")
        pe_used = sem("pe_used")
        dve_used = sem("dve_used")
        x2_out = sem("x2_out")
        x2_back = sem("x2_back")
        q_s_ready = sem("q_s_ready")
        wide_ready = sem("wide_ready")
        s_scores = sem("s_scores")
        gelu_done = sem("gelu_done")
        w_ready = sem("w_ready")
        w_staged = sem("w_staged")
        diag_ready = sem("diag_ready")
        sum_ready = sem("sum_ready")
        y_sum = sem("y_sum")
        y_ss = sem("y_ss")
        y_mean = sem("y_mean")
        y_root = sem("y_root")
        y_rstd = sem("y_rstd")
        y_ready = sem("y_ready")
        y_out = sem("y_out")

        from_one = (head_done, post_done, decayed, o_mm, o_tr, u_out, w_ready, diag_ready, os_mm, attn_mm, outer_mm, S_out, o_ready, gelu_done, acc_read, k_read, attn_ready, s_new, oT_ready, u_read)

        block = ctx.enter_context(nc.Block())

        def m_at(k):
            return k // 4 * 2 + k % 4 // 2 * (KT // 2) + k % 2

        def raw_slot(n0):
            if n0 < B_LATE:
                return n0 % 4, n0 // 4 + 1
            s = n0 % 2
            return s, (B_LATE - 1 - s) // 4 + 1 + (n0 - B_LATE) // 2 + 1

        def raw_loads(n0, i, L):
            return 16 * raw_slot(n0)[1] + i * (16 * (L // 4 if n0 < B_LATE else L // 2))

        @block.sync
        def _(sp):
            for counter in from_one:
                sp.sem_inc(counter, ONE)
            sp.dma_start(x_tok[:, 0:2, :], x_p).then_inc(x_in, 16)
            sp.dma_start(x_tok[0:TS, 2, :], x_s).then_inc(x_in, 16)
            n_par = 0
            for h in range(H):
                r = 20 * h
                span = slice(h * DV, (h + 1) * DV)
                for src in (gla_norm_g[:, span], conv_w[0, 0:1, span], conv_w[0, 1:2, span],
                            conv_w[0, 2:3, span], conv_b[:, span]):
                    sp.dma_start(prow[r:r + HV, :], src.rearrange("o (r c) -> (o r) c", c=P)).then_inc(par_in, 16)
                    r += HV
                    n_par += 1
            for r, src in ((80, norm1_g), (80 + KT, norm2_g), (80 + 2 * KT, b_alpha)):
                rows = src.shape[1] // P
                sp.dma_start(prow[r:r + rows, :], src.rearrange("o (r c) -> (o r) c", c=P)).then_inc(par_in, 16)
                n_par += 1
            assert n_par == N_PAR
            sp.dma_start(crow[0:2 * TS, :], state_conv.rearrange("o j s d -> (o j s) d")).then_inc(conv_in, 16)
            sp.dma_start(krow[:], sub_keys.rearrange("o s n d -> n (o s) d")).then_inc(keys_in, 16)
            sp.dma_start(wau[0:RANK, :], w_alpha_up.rearrange("o r n -> (o r) n")).then_inc(wau_in, 16)
            sp.dma_start(conv_sample.rearrange("o j s d -> (o j) s d")[:, 0, :],
                         state_conv.rearrange("o j s d -> (o j) s d")[:, 1, :]).then_inc(conv_copy, 16)

            def load(n0, src, i=0, L=0):
                s = raw_slot(n0)[0]
                if n0 >= 4:
                    sp.wait_ge(lo_done, (n0 - 3 if n0 < B_LATE else n0 - 1) + i * L)
                sp.dma_start(raw[s][:], src).then_inc(raw_in[s], 16)

            load(0, win[:, :, COL_ALR:COL_ALR + P])
            for n in (1, 2, 3):
                load(n, win[:, :, (n - 1) * P:n * P])
            with sp.Fori(0, 7) as i:
                for j in range(4):
                    load(4 + j, win[:, :, bass.ds((3 + j) * P + i * (4 * P), P)], i, 4)
            load(B_SIX - 1, win[:, :, (B_SIX - 2) * P:(B_SIX - 1) * P])
            with sp.Fori(0, H) as i:
                for b in range(SIX_PER_HEAD):
                    cg, t, half = b // 12, (b // 2) % 6, b % 2
                    load(B_SIX + b, win[:, :, bass.ds(SIX[t] + (2 * cg + half) * P + i * DV, P)], i, 24)
            with sp.Fori(0, 4) as i:
                for j in range(4):
                    load(B_OUT + j, wout[:, :, bass.ds(j * P + i * (4 * P), P)], i, 4)
            for j in range(2):
                load(B_QRY + j, wqry[:, :, j * P:(j + 1) * P])
            sp.wait_ge(cleared, 1)
            sp.dma_start(g_row[:], norm2_g.partition_broadcast(P).rearrange("p o d -> p (o d)")).then_inc(row_in, 16)
            with sp.Fori(0, PH - 1) as i:
                for j in range(2):
                    load(B_LATE + j, wqry[:, :, bass.ds((2 + j) * P + i * (2 * P), P)], i, 2)
            sp.wait_ge(mm_done, B_END)
            sp.wait_ge(x2_out, 32)
            sp.dma_start(y_tok[:, 0:2, :], x2_dram[:, 0:2, :]).then_inc(x2_back, 16)
            sp.dma_start(y_tok[0:TS, 2, :], x2_dram[0:TS, 2, :]).then_inc(x2_back, 16)
            sp.wait_ge(h2_ready, 3)
            sp.dma_start(g_row[:], norm_f_g.partition_broadcast(P)).then_inc(row_in, 16)
            for t in range(3):
                sp.wait_ge(y_ready, t + 1)
                out, src = ((y_prompt.rearrange("b (t p) d -> p (b t) d", p=P)[:, t, :], y_tok[:, t, :]) if t < 2
                            else (y_sample.rearrange("b s d -> (b s) d"), y_tok[0:TS, 2, :]))
                sp.dma_start(out, src).then_inc(y_out, 16)
            sp.wait_ge(conv_copy, 16)
            sp.wait_ge(y_out, 48)

        @block.gpsimd
        def _(pool):
            g = nc.gpsimd
            n = 0

            def made(ins):
                nonlocal n
                n += 1
                ins.then_inc(consts, 1)

            def ones_where(out, pattern, base, mult, first=None):
                made(g.memset(out, 0.0))
                pool.wait_ge(consts, n)
                made(g.affine_select(out=out, in_=out, compare_op=ALU.not_equal, fill=1.0, base=base,
                                     pattern=pattern, channel_multiplier=mult))

            ones_where(ident[:], [[-1, P]], 0, 1)
            ones_where(eye8[:], [[1, TS], [-1, TS]], 0, 0)
            made(g.memset(causal[:], 1.0))
            pool.wait_ge(consts, n)
            made(g.affine_select(out=causal[:], in_=causal[:], compare_op=ALU.is_ge, fill=0.0, base=0,
                                 pattern=[[1, P]], channel_multiplier=-1))
            for m, pat, mult, width in ((spread, 1, -TOPK, P), (gather8, -TOPK, 1, TS)):
                made(g.memset(m[:], 1.0))
                pool.wait_ge(consts, n)
                made(g.affine_select(out=m[:], in_=m[:], compare_op=ALU.is_ge, fill=0.0, base=0,
                                     pattern=[[pat, width]], channel_multiplier=mult))
                pool.wait_ge(consts, n)
                made(g.affine_select(out=m[:], in_=m[:], compare_op=ALU.is_ge, fill=0.0, base=TOPK - 1,
                                     pattern=[[-pat, width]], channel_multiplier=-mult))
            made(g.memset(own16[:], 0.0))
            for j in range(TS):
                pool.wait_ge(consts, n)
                made(g.affine_select(out=own16[:], in_=own16[:], compare_op=ALU.not_equal, fill=1.0,
                                     base=-TOPK * j, pattern=[[-1, TOPK]], channel_multiplier=1))
            made(g.memset(same_h[:], 1.0))
            pool.wait_ge(consts, n)
            made(g.affine_select(out=same_h[:], in_=same_h[:], compare_op=ALU.is_ge, fill=0.0, base=0,
                                 pattern=[[-TS, PH]], channel_multiplier=1))
            pool.wait_ge(consts, n)
            made(g.affine_select(out=same_h[:], in_=same_h[:], compare_op=ALU.is_ge, fill=0.0, base=TS - 1,
                                 pattern=[[TS, PH]], channel_multiplier=-1))
            made(g.memset(same_j[:], 0.0))
            for h in range(PH):
                pool.wait_ge(consts, n)
                made(g.affine_select(out=same_j[:].rearrange("p (j r) -> p j r", j=TS),
                                     in_=same_j[:].rearrange("p (j r) -> p j r", j=TS),
                                     compare_op=ALU.not_equal, fill=1.0, base=-TS * h,
                                     pattern=[[-1, TS], [0, TOPK]], channel_multiplier=1))
            made(g.iota(iota16[:], pattern=[[1, TOPK]], base=0, channel_multiplier=0,
                        allow_small_or_imprecise_dtypes=True))
            assert n == N_CONSTS, n

            pool.wait_ge(la_ready, 3)
            pool.wait_ge(par_ready, 3)
            pool.wait_ge(post_done, ONE + KT)
            with pool.Fori(0, H) as i:
                pool.wait_ge(head_done, ONE + i)
                pool.sem_inc(granted, 1)
                g.tensor_copy(v_h[:, 0:2, :], v_tok[:, 0:2, bass.ds(i * DV, DV)]).then_inc(staged, 1)
                g.tensor_copy(v_h[0:TS, 2, :], v_tok[0:TS, 2, bass.ds(i * DV, DV)]).then_inc(staged, 1)
                g.tensor_copy(q_h[:], qk[:, bass.ds(i * KD, KD), :]).then_inc(staged, 1)
                g.tensor_copy(k_h[:], qk[:, bass.ds(i * KD + H * KD, KD), :]).then_inc(staged, 1)
                g.tensor_copy(la_h[:], la[:, bass.ds(i * KD, KD), :]).then_inc(staged, 1)
                g.tensor_copy(cols_h[:], cols[:, bass.ds(i * KD, KD), :]).then_inc(staged, 1)
                g.tensor_copy(decS_h[:], decS[:, bass.ds(i * KD, KD), :]).then_inc(staged, 1)
                g.tensor_copy(pcol_h[:], pcol[:, bass.ds(i * 20, 20)]).then_inc(staged, 1)
                g.tensor_copy(convT_h[:], convT[:, bass.ds(i * HV, HV), :]).then_inc(staged, 1)

                def load(m):
                    g.dma_start(s_ring[m % 4][:], st_in[:, bass.ds(i, 1), m % KD, m // KD, :]
                                .rearrange("p o v -> p (o v)")).then_inc(s_in[m % 4], 16)

                M = KD * TS
                for m in range(4):
                    load(m)
                for m in range(M):
                    pool.wait_ge(s_new, ONE + i * M + m + 1)
                    pool.sem_inc(granted, 1)
                    g.dma_start(st_out[:, bass.ds(i, 1), m % KD, m // KD, :]
                                .rearrange("p o v -> p (o v)"), s_ring[m % 4][:]).then_inc(s_out[m % 4], 16)
                    if m + 4 < M:
                        pool.wait_ge(s_out[m % 4], i * (4 * 16) + 16 * (m // 4) + 16)
                        pool.sem_inc(granted, 1)
                        pool.wait_ge(os_mm, ONE + i * M + m + 1)
                        pool.sem_inc(granted, 1)
                        load(m + 4)
                for s in range(4):
                    pool.wait_ge(s_out[s], i * (4 * 16) + 64)
                    pool.sem_inc(granted, 1)
            for s in range(4):
                pool.wait_ge(s_out[s], H * 64)
            pool.wait_ge(head_done, ONE + H)
            g.dma_start(x2_tok[:, 0:2, :], x_p).then_inc(x2_in, 16)
            g.dma_start(x2_tok[0:TS, 2, :], x_s).then_inc(x2_in, 16)

            def fetch(table, free_sem, free_at, src, k, n_staged):
                pool.wait_ge(free_sem, free_at)
                pool.sem_inc(granted, 1)
                g.tensor_copy(idx_st[:, k:k + 1], src).then_inc(idx_staged, 1)
                pool.wait_ge(idx_staged, n_staged)
                pool.sem_inc(granted, 1)
                g.indirect_dma_start(ring[k][:], None, table,
                                     bass.IndirectOffsetOnAxis(ap=idx_st[:, k:k + 1], axis=0)).then_inc(ring_in[k], 16)

            W = 2 * TOPK
            pool.wait_ge(x2_out, 32)
            with pool.Fori(0, PH) as i:
                pool.wait_ge(retrieved, i + 1)
                pool.sem_inc(granted, 1)
                for s in range(W):
                    fetch(eu, u_used, i * W + s + 1, idx_all[:, bass.ds(i * W + s, 1)], s % RING, i * W + s + 1)
            pool.wait_ge(retrieved, PH + 1)
            for s in range(PH):
                fetch(eu, u_used, PH * W + s + 1, idx_s[:, s:s + 1], s, PH * W + s + 1)
            U = PH * W + PH
            for t in range(2):
                with pool.Fori(0, PH) as i:
                    for s in range(TOPK):
                        k, turn = s % RING, t * (PH * TOPK // RING) + s // RING
                        who, n, nth = ((dve_used, N_DVE, DVE_SLOTS.index(k)) if k in DVE_SLOTS
                                       else (pe_used, N_PE, PE_SLOTS.index(k)))
                        fetch(ev, who, n * turn + nth + 1 + i * (n * TOPK // RING),
                              idx_all[:, bass.ds(i * W + t * TOPK + s, 1)], k, i * TOPK + U + t * PH * TOPK + s + 1)
            for k in range(PH):
                turn = 2 * PH * TOPK // RING
                who, n, nth = ((dve_used, N_DVE, DVE_SLOTS.index(k)) if k in DVE_SLOTS
                               else (pe_used, N_PE, PE_SLOTS.index(k)))
                fetch(ev, who, n * turn + nth + 1, idx_s[:, k:k + 1], k, U + 2 * PH * TOPK + k + 1)

        @block.scalar
        def _(act):
            a = nc.scalar

            def hi(n0, i=0, L=0):
                s = raw_slot(n0)[0]
                act.wait_ge(raw_in[s], raw_loads(n0, i, L))
                a.activation(w_hi[n0 % 2][:], raw[s][:], ACT.Copy).then_inc(hi_done, 1)

            def evac_wait(n0, i, L):
                act.wait_ge(post_done, ONE + posts(n0 - 4) + i * (POSTS if L == 24 else L if n0 >= B_V else 0))

            def norm(p, src):
                for t in range(3):
                    q = P if t < 2 else TS
                    if t:
                        act.wait_ge(ss_done, 3 * p + t)
                    a.activation(sq_junk[0:q, :], src[0:q, t, :], ACT.Square,
                                 accum_out=ssq[0:q, t:t + 1]).then_inc(ss_done, 1)
                act.wait_ge(ms_done, p + 1)
                a.activation(root[:], mean_sq[:], ACT.Sqrt).then_inc(rt_done, 1)

            def act_parts(p, gcol):
                for k in range(KT):
                    act.wait_ge(tr_done, KT * p + k + 1)
                    a.activation(act_hi[:, k, :], bank[2 + k % 6][:, 0:T], ACT.Copy,
                                 scale=pcol[:, gcol + k:gcol + k + 1]).then_inc(ah_done, 1)

            act.wait_ge(chain, 1)
            act.wait_ge(x_in, 32)
            norm(0, x_tok)
            hi(0)
            hi(1)
            act.wait_ge(par_T, 1)
            a.activation(pcol[:], bank[2][:, 0:120], ACT.Copy).then_inc(par_ready, 1)
            act.wait_ge(par_T, 2)
            a.activation(keysT[:], bank[3][:, 0:2 * NKEY].rearrange("p (s n) -> p s n", s=2), ACT.Copy).then_inc(par_ready, 1)
            act.wait_ge(par_T, 3)
            a.activation(convT[:], bank[4][:, 0:KT * 2 * TS].rearrange("p (k r) -> p k r", k=KT), ACT.Copy).then_inc(par_ready, 1)
            act.wait_ge(par_ready, 1)
            act_parts(0, 80)

            act.wait_ge(mm_done, 1)
            hi(2)
            a.activation(alr[0:RANK, :], bank[ACC][0:RANK, 0:T], ACT.Copy).then_inc(acc_read, 1)
            act.wait_ge(la_ev, H * KD)
            a.activation(la_tmp[:], la[:], ACT.Abs).then_inc(la_step, 1)
            act.wait_ge(la_step, 1)
            a.activation(la_tmp[:], la_tmp[:], ACT.Exp, scale=-1.0).then_inc(la_step, 1)
            act.wait_ge(la_step, 2)
            a.activation(la_tmp[:], la_tmp[:], ACT.Ln, bias=1.0).then_inc(la_step, 1)

            def qkv_block(n0, i, L, out):
                act.wait_ge(mm_done, n0 + 1 + i * L)
                hi(n0 + 2, i, L)
                evac_wait(n0, i, L)
                a.activation(out, bank[ACC + n0 % 2][:, 0:T], ACT.Copy).then_inc(acc_read, 1)

            with act.Fori(0, 4) as i:
                for b in range(4):
                    qkv_block(B_Q + b, i, 4, qk[:, bass.ds(i * 4 + b, 1), :].rearrange("p o t -> p (o t)"))
            with act.Fori(0, 4) as i:
                for b in range(4):
                    qkv_block(B_V + b, i, 4, stage[(B_V + b) % 2][:])

            act.wait_ge(la_ready, 1)
            act.wait_ge(la_step, 5)
            a.activation(cols[:, :, 6:8], cols[:, :, 4:6], ACT.Exp).then_inc(la_ready, 1)
            a.activation(decS[:], la[:, :, TP:T], ACT.Exp, scale=1.0 / TAU).then_inc(la_ready, 1)

            def chunk_exps(i, c):
                act.wait_ge(decayed, ONE + i * 2 + c)
                if c == 0:
                    act.wait_ge(staged, i * 9 + 9)
                act.wait_ge(o_mm, ONE + i * 2 + c)
                bt = la_h[:, :, c * P:(c + 1) * P]
                for k in range(KD):
                    for out, sc, col in ((dq, 1, 0), (dk, -1, 2), (dk1, -1, 4)):
                        a.activation(out[:, k, :], bt[:, k, :], ACT.Exp, scale=sc / TAU,
                                     bias=cols_h[:, k, col + c:col + c + 1]).then_inc(exps, 1)
                a.activation(dq0[:], bt, ACT.Exp, scale=1.0 / TAU).then_inc(exps, 1)

            def out_norm(i, c):
                q, src = (P, bank[OB]) if c < 2 else (TS, bank[OS])
                junk = o_sb[0:q, :]
                if c < 2:
                    act.wait_ge(o_mm, ONE + i * 2 + c + 1)
                else:
                    act.wait_ge(os_mm, ONE + i * (KD * TS) + KD * TS)
                act.wait_ge(o_tr, ONE + i * 3 + c)
                a.activation(junk, src[0:q, :], ACT.Square, accum_out=gss[0:q, c:c + 1]).then_inc(o_sum, 1)

            def out_scale(i, c):
                q, src = (P, bank[OB]) if c < 2 else (TS, bank[OS])
                act.wait_ge(o_mean, i * 3 + c + 1)
                a.activation(gss[0:q, 3:4], gss[0:q, 3:4], ACT.Sqrt).then_inc(o_root, 1)
                act.wait_ge(o_rstd, i * 3 + c + 1)
                a.activation(o_sb[0:q, :], src[0:q, :], ACT.Copy,
                             scale=gss[0:q, 4:5]).then_inc(o_ready, 1)

            def out_turned(i, c):
                act.wait_ge(o_tr, ONE + i * 3 + c + 1)
                if c == 0:
                    act.wait_ge(head_done, ONE + i)
                w = P if c < 2 else TS
                a.activation(oT[:, :, c * P:c * P + w],
                             bank[KV1 if c < 2 else OB][:, 0:HV * w].rearrange("p (b t) -> p b t", b=HV), ACT.Copy).then_inc(oT_ready, 1)

            with act.Fori(0, H) as i:
                for b in range(SIX_PER_HEAD):
                    n0 = B_SIX + b
                    cg, t, half = b // 12, (b // 2) % 6, b % 2
                    src = bank[ACC + n0 % 2][:, 0:T]
                    act.wait_ge(mm_done, n0 + 1 + i * 24)
                    hi(n0 + 2, i, 24)
                    evac_wait(n0, i, 24)
                    q = cg * 2 + half
                    if cg == 0 and t in (1, 2):
                        act.wait_ge(head_done, ONE + i)
                    if t == 0:
                        act.wait_ge(post_done, ONE + posts(n0 - 2) + i * POSTS)
                        a.activation(tR[half][:], src, ACT.Copy)
                        a.activation(tA[half][:], src, ACT.Sigmoid).then_inc(acc_read, 1)
                    elif t == 1:
                        a.activation(gate[:, q, :], src, ACT.Sigmoid).then_inc(acc_read, 1)
                    elif t in (2, 3, 4):
                        out = {2: yb[:, q, :], 3: tA[half][:], 4: tR[half][:]}[t]
                        a.activation(out, src, ACT.Copy).then_inc(acc_read, 1)
                    else:
                        act.wait_ge(post_done, ONE + posts(n0 - 2) + i * POSTS)
                        a.activation(tR[half][:], src, ACT.Sigmoid).then_inc(acc_read, 1)
                    if b == 1:
                        chunk_exps(i, 0)
                    if b == 9:
                        chunk_exps(i, 1)
                    for c in (0, 1):
                        if b == 8 * c + 4:
                            act.wait_ge(attn_mm, ONE + i * 2 + c + 1)
                            a.activation(k_tok[:], bank[MISC][:, P:3 * P].rearrange("p (k d) -> p k d", k=KD),
                                         ACT.Copy).then_inc(k_read, 1)
                    if b == 2:
                        act.wait_ge(ks_mm, i + 1)
                        a.activation(ks_tok[0:TS, :], bank[OB][0:TS, 0:DK], ACT.Copy).then_inc(ks_ready, 1)
                    for c, at in ((0, 6), (1, 14), (2, 20)):
                        if b == at:
                            out_norm(i, c)
                        if b == at + 1:
                            out_scale(i, c)
                        if b == at + (3 if c < 2 else 2):
                            out_turned(i, c)
                    if t == 5:
                        act.wait_ge(u_tr, i * 4 + q + 1)
                        if q == 0:
                            act.wait_ge(u_out, ONE + i * 32)
                        a.activation(u_rows[0:2 + TS, q * P:(q + 1) * P], bank[KV1][0:2 + TS, 0:P],
                                     ACT.Copy).then_inc(u_read, 1)
                act.wait_ge(u_read, ONE + i * 4 + 4)
                ch = bass.ds(i * DV, DV)
                act.dma_start(conv_prompt.rearrange("o b s d -> (o b s) d")[:, ch], u_rows[0:2, :]).then_inc(u_out, 16)
                act.dma_start(conv_sample.rearrange("o j s d -> (o j) s d")[:, 1, ch], u_rows[2:2 + TS, :]).then_inc(u_out, 16)
                act.wait_ge(S_ready, i * 2 + 2)
                act.dma_start(stp_out[:, bass.ds(i, 1), :, :].rearrange("p o k v -> p (o k) v"), S[:]).then_inc(S_out, 16)

            act.wait_ge(m_ready, 2 * H)
            act.wait_ge(mm_done, B_OUT)
            for k in range(0, KT, 2):
                a.activation(act_hi[:, k:k + 2, :], mT[:, m_at(k):m_at(k) + 2, :], ACT.Copy).then_inc(ah_done, 2)
            with act.Fori(0, 4) as i:
                for b in range(4):
                    qkv_block(B_OUT + b, i, 4, stage[(B_OUT + b) % 2][:])
            act.wait_ge(post_done, ONE + posts(B_QRY - 1))
            act.dma_start(x2_dram[:, 0:2, :], x2_tok[:, 0:2, :]).then_inc(x2_out, 16)
            act.dma_start(x2_dram[0:TS, 2, :], x2_tok[0:TS, 2, :]).then_inc(x2_out, 16)
            norm(1, x2_tok)
            act_parts(1, 80 + KT)

            def query_out(h0, i, L):
                for half in range(2):
                    n0 = B_QRY + 2 * h0 + half
                    act.wait_ge(mm_done, n0 + 1 + i * L)
                    evac_wait(n0, i, L)
                    src = bank[ACC + n0 % 2]
                    at = bass.ds(h0 + i, 1) if L else slice(h0, h0 + 1)
                    a.activation(q_s[:, half, at, :].rearrange("p o j -> p (o j)"), src[:, TP:T],
                                 ACT.Copy).then_inc(q_s_ready, 1)
                    a.activation(stage[n0 % 2][:, 0:TP], src[:, 0:TP], ACT.Copy).then_inc(acc_read, 1)

            def soft_exp(h0, i, tiles, rows):
                act.wait_ge(soft_in, i + h0 + 1)
                a.activation(soft[0:rows, 0:tiles, :], soft[0:rows, 0:tiles, :], ACT.Exp).then_inc(soft_e, 1)

            query_out(0, 0, 0)
            soft_exp(0, 0, 2, P)
            with act.Fori(0, PH - 1) as i:
                for half in range(2):
                    n0 = B_LATE + half
                    act.wait_ge(mm_done, n0 - 1 + i * 2)
                    hi(n0, i, 2)
                query_out(1, i, 2)
                soft_exp(1, i, 2, P)
            act.wait_ge(rep_mm, 1)
            for j in range(4):
                a.activation(xs_rep[:, j * 512:(j + 1) * 512], bank[4 + j][:], ACT.Copy).then_inc(rep_ready, 1)
            soft_exp(PH, 0, 1, PH * TS)
            W = 2 * TOPK
            act.wait_ge(w_ready, ONE + 1)
            a.activation(w_all[:], w_all[:], ACT.Gelu).then_inc(gelu_done, 1)
            act.wait_ge(dve_used, N_DVE)
            a.activation(w_s[:], dots_s[:], ACT.Gelu).then_inc(gelu_done, 1)

            def y_norm(t):
                q = P if t < 2 else TS
                act.wait_ge(y_sum, 4 * t + 4)
                if t:
                    act.wait_ge(y_ss, t)
                a.activation(y_sq[0:q, :], y_tok[0:q, t, :], ACT.Square,
                             accum_out=ssq[0:q, t:t + 1]).then_inc(y_ss, 1)
                act.wait_ge(y_mean, t + 1)
                a.activation(root[0:q, t:t + 1], mean_sq[0:q, t:t + 1], ACT.Sqrt).then_inc(y_root, 1)

            act.wait_ge(w_ready, ONE + 3)
            per = N_PE * TOPK // RING
            for t in range(2):
                with act.Fori(0, PH) as i:
                    for s in range(TOPK):
                        if s % RING in DVE_SLOTS:
                            continue
                        nth = s // RING * N_PE + PE_SLOTS.index(s % RING)
                        n = t * PH * per + nth
                        act.wait_ge(pe_used, i * per + n + N_PE - 3)
                        a.activation(diag[nth % 4][:], ident[:], ACT.Copy,
                                     scale=w_all[:, bass.ds(i * W + t * TOPK + s, 1)]).then_inc(diag_ready, 1)
                if t:
                    y_norm(0)
            for s in range(PH):
                act.wait_ge(pe_used, 2 * PH * per + s + N_PE - 3)
                a.activation(diag_s[s % 4][:], gather8[:], ACT.Copy, scale=w_s[:, s:s + 1]).then_inc(diag_ready, 1)
            y_norm(1)
            y_norm(2)
            act.wait_ge(u_out, ONE + 32 * H)
            act.wait_ge(S_out, ONE + 16 * H)

        @block.vector
        def _(dve):
            v = nc.vector
            count = [0]

            def lo(n0, i=0, L=0):
                s = raw_slot(n0)[0]
                dve.wait_ge(hi_done, n0 + 1 + i * L)
                v.tensor_tensor(w_lo[n0 % 2][:], raw[s][:], w_hi[n0 % 2][:].bitcast(F32),
                                ALU.subtract).then_inc(lo_done, 1)

            def norm(p, src, out):
                dve.wait_ge(ss_done, 3 * p + 3)
                v.tensor_scalar(mean_sq[:], ssq[:], 1.0 / D, EPS, ALU.mult, ALU.add).then_inc(ms_done, 1)
                dve.wait_ge(rt_done, p + 1)
                v.reciprocal(rstd[:], root[:]).then_inc(rs_done, 1)
                dve.wait_ge(rs_done, p + 1)
                for t in range(3):
                    q = P if t < 2 else TS
                    v.tensor_scalar(out[0:q, t, :], src[0:q, t, :], rstd[0:q, t:t + 1], None,
                                    ALU.mult).then_inc(xn_done, 1)

            def act_parts(p, gcol):
                for k in range(KT):
                    dve.wait_ge(ah_done, (2 * p) * KT + k + 1)
                    v.scalar_tensor_tensor(out=act_lo[:, k, :], in0=bank[2 + k % 6][:, 0:T],
                                           scalar=pcol[:, gcol + k:gcol + k + 1],
                                           in1=act_hi[:, k, :].bitcast(F32),
                                           op0=ALU.mult, op1=ALU.subtract).then_inc(al_done, 1)

            v.memset(ssq[:], 1.0).then_inc(chain, 1)
            for s in range(2):
                v.memset(u_pad[s][:], 0.0).then_inc(chain, 1)
            v.memset(gss[:], 1.0).then_inc(chain, 1)
            N0 = 4
            norm(0, x_tok, x_tok)
            lo(0)
            lo(1)
            act_parts(0, 80)
            lo(2)
            for m in range(H * KD):
                dve.wait_ge(la_mm, m + 1)
                v.tensor_scalar(la[:, m, :], bank[2 + m % 6][:, 0:T],
                                pcol[:, 80 + 2 * KT + m:81 + 2 * KT + m], None, ALU.add).then_inc(la_ev, 1)

            dve.wait_ge(la_step, 3)
            v.scalar_tensor_tensor(out=la[:], in0=la[:], scalar=0.0, in1=la_tmp[:], op0=ALU.min,
                                   op1=ALU.subtract).then_inc(la_step, 1)
            dve.wait_ge(la_step, 4)
            v.memset(attn[:], 1.0).then_inc(chain, 1)
            dve.wait_ge(chain, N0 + 1)
            for m in range(H * KD):
                for c in range(2):
                    run = la[:, m, c * P:(c + 1) * P]
                    v.tensor_tensor_scan(run, attn[:], run, 0.0, ALU.mult, ALU.add).then_inc(chain, 1)
            dve.wait_ge(chain, N0 + 1 + 2 * H * KD)
            mid = la[:, :, P // 2 - 1:P // 2 + P:P]
            last = la[:, :, P - 1:2 * P:P]
            v.tensor_scalar(cols[:, :, 0:2], mid, -1.0 / TAU, None, ALU.mult)
            v.tensor_scalar(cols[:, :, 2:4], mid, 1.0 / TAU, None, ALU.mult)
            v.tensor_scalar(cols[:, :, 4:6], last, 1.0 / TAU, None, ALU.mult).then_inc(la_step, 1)
            dve.wait_ge(la_step, 5)
            dve.sem_inc(la_ready, 1)

            with dve.Fori(0, 4) as i:
                for b in range(4):
                    lo(B_Q + b + 2, i, 4)

            def v_copy(n0, i, L):
                dve.wait_ge(v_tr, n0 - B_V + 1 + i * L)
                col = bass.ds((n0 - B_V) * P + i * (L * P), P) if L else slice((n0 - B_V) * P, (n0 - B_V + 1) * P)
                src = bank[MISC + n0 % 2]
                v.tensor_copy(v_tok[:, 0:2, col], src[:, 0:2 * P].rearrange("p (t c) -> p t c", t=2))
                v.tensor_copy(v_tok[0:TS, 2, col], src[0:TS, 2 * P:3 * P]).then_inc(post_done, 1)

            with dve.Fori(0, 4) as i:
                for b in range(4):
                    lo(B_V + b + 2, i, 4)
                    v_copy(B_V + b, i, 4)

            
            def head_step(i, b, link):
                n0 = B_SIX + b
                cg, t, half = b // 12, (b // 2) % 6, b % 2
                q = cg * 2 + half
                lo(n0 + 2, i, 24)
                if b == 1:
                    dve.wait_ge(staged, i * 9 + 9)
                dve.wait_ge(acc_read, ONE + n0 + 1 + i * 24)
                dve.wait_ge(post_done, ONE + posts(n0 - 1) + i * POSTS)
                up = u_pad[half]
                if t == 0:
                    v.tensor_tensor(tR[half][:], tR[half][:], tA[half][:], ALU.mult).then_inc(post_done, 1)
                elif t == 1:
                    v.scalar_tensor_tensor(out=gate[:, q, :], in0=gate[:, q, :], scalar=pcol_h[:, q:q + 1],
                                           in1=tR[half][:], op0=ALU.mult, op1=ALU.mult).then_inc(post_done, 1)
                elif t == 4:
                    wcol = lambda j: pcol_h[:, 4 + 4 * j + q:5 + 4 * j + q]
                    bcol = pcol_h[:, 16 + q:17 + q]
                    z, zs = tA[half], tA[half][:, TP:T]
                    link(v.tensor_tensor(up[:, 2:2 + T], tR[half][:], tA[half][:], ALU.mult))
                    dve.sem_inc(u_ready, 1)
                    link(v.tensor_scalar(z[:], up[:, 2:2 + T], wcol(2), bcol, ALU.mult, ALU.add))
                    for j in (1, 0):
                        v.scalar_tensor_tensor(out=z[:, 0:TP], in0=up[:, j:j + TP], scalar=wcol(j),
                                               in1=z[:, 0:TP], op0=ALU.mult, op1=ALU.add)
                        link(v.scalar_tensor_tensor(out=zs, in0=convT_h[:, q, j:2 * TS:2], scalar=wcol(j),
                                                    in1=zs, op0=ALU.mult, op1=ALU.add))
                    v.tensor_tensor(yb[:, q, :], yb[:, q, :], z[:], ALU.mult).then_inc(post_done, 1)
                elif t == 5:
                    v.tensor_tensor(yb[:, q, :], yb[:, q, :], tR[half][:], ALU.mult).then_inc(post_done, 1)

                for c in (0, 1):
                    if b == 8 * c + 2:
                        dve.wait_ge(exps, (i * 2 + c + 1) * (3 * KD + 1))
                        dve.wait_ge(attn_mm, ONE + i * 2 + c)
                        span = slice(c * P, (c + 1) * P)
                        for out, src, sc in ((dq, q_h, DK ** -0.5), (dk, k_h, 1.0), (dq0, q_h, DK ** -0.5),
                                             (dk1, k_h, 1.0)):
                            ins = v.scalar_tensor_tensor(out=out[:], in0=src[:, :, span], scalar=sc, in1=out[:],
                                                         op0=ALU.mult, op1=ALU.mult)
                        ins.then_inc(decayed, 1)
                    if b == 8 * c + 4:
                        dve.wait_ge(k_read, ONE + i * 2 + c + 1)
                        v.tensor_tensor(attn[:], bank[MISC][:, 0:P], causal[:], ALU.mult).then_inc(attn_ready, 1)
                    if b == 8 * c + 6:
                        dve.wait_ge(o_mm, ONE + i * 2 + c + 1)
                        if c == 0:
                            dve.wait_ge(S_out, ONE + i * 16)
                            for k in range(KD):
                                ins = v.tensor_copy(S[:, k, :], bank[KV0 + k][:])
                        else:
                            for k in range(KD):
                                ins = v.scalar_tensor_tensor(out=S[:, k, :], in0=S[:, k, :],
                                                             scalar=cols_h[:, k, 6 + c:7 + c],
                                                             in1=bank[KV0 + k][:], op0=ALU.mult, op1=ALU.add)
                        ins.then_inc(S_ready, 1)
                for c, at in ((0, 6), (1, 14), (2, 20)):
                    if b == at:
                        q_ = P if c < 2 else TS
                        dve.wait_ge(o_sum, i * 3 + c + 1)
                        dve.wait_ge(o_ready, ONE + i * 3 + c)
                        v.tensor_scalar(gss[0:q_, 3:4], gss[0:q_, c:c + 1], 1.0 / DV, EPS, ALU.mult,
                                        ALU.add).then_inc(o_mean, 1)
                    if b == at + 1:
                        q_ = P if c < 2 else TS
                        dve.wait_ge(o_root, i * 3 + c + 1)
                        v.reciprocal(gss[0:q_, 4:5], gss[0:q_, 3:4]).then_inc(o_rstd, 1)
                if b == 1:
                    dve.wait_ge(os_mm, ONE + i * (KD * TS))
                    for k in range(KD):
                        ins = v.scalar_tensor_tensor(
                            out=q_sel[:, k, :, :], in0=q_h[:, k, TP:T].unsqueeze(2).broadcast_to([P, TS, TS]),
                            scalar=DK ** -0.5, in1=eye8[:], op0=ALU.mult, op1=ALU.mult)
                    ins.then_inc(q_sel_ready, 1)
                M = KD * TS
                m = b - 2
                if 0 <= m < M:
                    if m == 0:
                        dve.wait_ge(ks_ready, i + 1)
                    dve.wait_ge(outer_mm, ONE + i * M + m)
                    v.tensor_scalar(ks_sel[m % 2][0:TS, :], ks_tok[0:TS, (m % KD) * P:(m % KD + 1) * P],
                                    ident[0:TS, m // KD:m // KD + 1], None, ALU.mult).then_inc(ks_sel_ready, 1)
                m = b - 3
                if 0 <= m < M:
                    dve.wait_ge(outer_mm, ONE + i * M + m + 1)
                    dve.wait_ge(s_in[m % 4], i * 64 + 16 * (m // 4) + 16)
                    v.scalar_tensor_tensor(out=s_ring[m % 4][:], in0=s_ring[m % 4][:],
                                           scalar=decS_h[:, m % KD, m // KD:m // KD + 1], in1=bank[OUTER][:],
                                           op0=ALU.mult, op1=ALU.add).then_inc(s_new, 1)

            with dve.Fori(0, H) as i:
                links = [0]
                base = N0 + 1 + 2 * H * KD

                def link(ins):
                    links[0] += 1
                    ins.then_inc(chain, 1)
                    dve.wait_ge(chain, i * N_LINKS + base + links[0])

                for b in range(SIX_PER_HEAD):
                    head_step(i, b, link)
                dve.wait_ge(oT_ready, ONE + i * 3 + 3)
                dve.wait_ge(post_done, ONE + posts(B_SIX + 23) + i * POSTS)
                link(v.tensor_tensor(gate[:], gate[:], oT[:], ALU.mult))
                for half in (0, 1):
                    v.tensor_tensor(mT[:, bass.ds(i * 2 + half * (KT // 2), 2), :], yb[:, 2 * half:2 * half + 2, :],
                                    gate[:, 2 * half:2 * half + 2, :], ALU.add).then_inc(m_ready, 1)
                assert links[0] == N_LINKS, links[0]
                dve.wait_ge(os_mm, ONE + i * (KD * TS) + KD * TS)
                dve.wait_ge(m_ready, i * 2 + 2)
                dve.sem_inc(head_done, 1)

            for k in range(0, KT, 2):
                dve.wait_ge(ah_done, KT + k + 2)
                v.tensor_tensor(act_lo[:, k:k + 2, :], mT[:, m_at(k):m_at(k) + 2, :],
                                act_hi[:, k:k + 2, :].bitcast(F32), ALU.subtract).then_inc(al_done, 2)

            def x_add(n0, i, L):
                if n0 == B_OUT:
                    dve.wait_ge(x2_in, 32)
                dve.wait_ge(v_tr, KT + n0 - B_OUT + 1 + i * L)
                col = bass.ds((n0 - B_OUT) * P + i * (L * P), P)
                src = bank[MISC + n0 % 2]
                v.tensor_tensor(x2_tok[:, 0:2, col], src[:, 0:2 * P].rearrange("p (t c) -> p t c", t=2),
                                x2_tok[:, 0:2, col], ALU.add)
                v.tensor_tensor(x2_tok[0:TS, 2, col], src[0:TS, 2 * P:3 * P], x2_tok[0:TS, 2, col],
                                ALU.add).then_inc(post_done, 1)

            with dve.Fori(0, 4) as i:
                for b in range(4):
                    lo(B_OUT + b + 2, i, 4)
                    x_add(B_OUT + b, i, 4)
            norm(1, x2_tok, xn_tok)
            act_parts(1, 80 + KT)
            dve.wait_ge(S_out, ONE + 16 * H)
            dve.wait_ge(u_out, ONE + 32 * H)
            dve.sem_inc(cleared, 1)
            dve.wait_ge(row_in, 16)
            dve.wait_ge(tr_done, 2 * KT)
            for t in (2, 0, 1):
                q = P if t < 2 else TS
                v.tensor_tensor(xn_tok[0:q, t, :], xn_tok[0:q, t, :], g_row[0:q, :], ALU.mult).then_inc(h2_ready, 1)
            dve.wait_ge(h2_ready, 3)

            base = N0 + 1 + 2 * H * KD + H * N_LINKS
            N_TOP = 20

            def scores(n0, i, L):
                dve.wait_ge(v_tr, 2 * KT + n0 - B_QRY + 1 + i * L)
                v.tensor_copy(sc[:, (n0 - B_QRY) % 2, :, :],
                              bank[MISC + n0 % 2][:, 0:2 * P].rearrange("p (t c) -> p t c", t=2)).then_inc(post_done, 1)

            def retrieval(h0, i, tiles, rows):
                steps = [0]
                r = slice(0, rows)
                ts = slice(0, tiles)

                def link(ins):
                    steps[0] += 1
                    ins.then_inc(chain, 1)
                    dve.wait_ge(chain, i * N_TOP + base + h0 * N_TOP + steps[0])
                    dve.sem_inc(granted, 1)

                def top16(work):
                    for turn in range(2):
                        eight = slice(8 * turn, 8 * turn + 8)
                        for src, vals, at in work:
                            ins = v.max(vals[:, eight], src)
                        link(ins)
                        for src, vals, at in work:
                            ins = v.max_index(at[:, eight], vals[:, eight], src)
                        link(ins)
                        if turn == 0:
                            for src, vals, at in work:
                                ins = v.match_replace(src, vals[:, eight], src, NEG_BIG)
                            link(ins)

                def best_keys():
                    top16([(sc[r, s, t, :], val[r, s, t, :], key_u[r, s, t, :])
                           for s in range(2) for t in range(tiles)])

                def best_pairs():
                    for t in range(tiles):
                        ins = v.tensor_tensor(cand[r, t, :].rearrange("p (a b) -> p a b", a=TOPK),
                                              val[r, 0, t, :].unsqueeze(2).broadcast_to([rows, TOPK, TOPK]),
                                              val[r, 1, t, :].unsqueeze(1).broadcast_to([rows, TOPK, TOPK]), ALU.add)
                    link(ins)
                    top16([(cand[r, t, :], best[r, t, :], pos[r, t, :]) for t in range(tiles)])
                    link(v.tensor_tensor(soft[r, ts], best[r, ts],
                                         best[r, ts, 0:1].broadcast_to([rows, tiles, TOPK]), ALU.subtract))
                    dve.sem_inc(soft_in, 1)

                def experts():
                    shape = [rows, tiles, TOPK, TOPK]
                    for s in range(2):
                        v.tensor_copy(key_f[r, s, ts], key_u[r, s, ts])
                    v.tensor_scalar(pos_u[r, 0, ts], pos[r, ts], 4, None, ALU.logical_shift_right)
                    link(v.tensor_scalar(pos_u[r, 1, ts], pos[r, ts], 15, None, ALU.bitwise_and))
                    for s in range(2):
                        ins = v.tensor_copy(pos_f[r, s, ts], pos_u[r, s, ts])
                    link(ins)
                    for s in range(2):
                        ins = v.tensor_tensor(hot[s][r, ts], pos_f[r, s, ts].unsqueeze(3).broadcast_to(shape),
                                              iota16[r].unsqueeze(1).unsqueeze(1).broadcast_to(shape), ALU.is_equal)
                    link(ins)
                    for s in range(2):
                        ins = v.tensor_tensor(hot[s][r, ts], hot[s][r, ts],
                                              key_f[r, s, ts].unsqueeze(2).broadcast_to(shape), ALU.mult)
                    link(ins)
                    for s in range(2):
                        ins = v.tensor_reduce(key_sel[r, s, ts], hot[s][r, ts], AX_X, ALU.add)
                    link(ins)
                    dve.wait_ge(soft_e, i + h0 + 1)
                    v.scalar_tensor_tensor(out=picks[r, 0, ts], in0=key_sel[r, 0, ts], scalar=float(NKEY),
                                           in1=key_sel[r, 1, ts], op0=ALU.mult, op1=ALU.add)
                    link(v.tensor_reduce(soft_s[r, ts], soft[r, ts], AX_X, ALU.add))
                    link(v.reciprocal(soft_r[r, ts], soft_s[r, ts]))
                    link(v.tensor_tensor(picks[r, 1, ts], soft[r, ts],
                                         soft_r[r, ts].unsqueeze(2).broadcast_to([rows, tiles, TOPK]), ALU.mult))
                    assert steps[0] == N_TOP, steps[0]

                return best_keys, best_pairs, experts

            W = 2 * TOPK

            def keep_picks(h0, i):
                to = bass.ds(h0 * W + i * W, W)
                v.tensor_copy(idx_all[:, to], picks[:, 0].rearrange("p t k -> p (t k)"))
                v.tensor_copy(g_all[:, to], picks[:, 1].rearrange("p t k -> p (t k)")).then_inc(retrieved, 1)
                dve.wait_ge(retrieved, i + h0 + 1)
                dve.sem_inc(granted, 1)

            def query_ready(h0, i):
                dve.wait_ge(post_done, ONE + posts(B_QRY + 2 * h0 + 1) + i * 2)
                dve.sem_inc(granted, 1)

            def dot(s, i):
                k = s % RING
                dve.wait_ge(ring_in[k], i * (16 * W // RING) + 16 * (s // RING + 1))
                v.tensor_tensor_reduce(ring[k][:], ring[k][:], xn_tok[:, s // TOPK, :], 1.0, 0.0, ALU.mult,
                                       ALU.add, dots[:, s:s + 1]).then_inc(u_used, 1)

            def keep_dots(i):
                dve.wait_ge(u_used, i * W + W + RING)
                v.tensor_copy(w_all[:, bass.ds(i * W, W)], dots[:]).then_inc(h2_ready, 1)
                dve.wait_ge(h2_ready, i + 4)
                dve.sem_inc(granted, 1)

            for half in range(2):
                scores(B_QRY + half, 0, 0)
            query_ready(0, 0)
            for piece in retrieval(0, 0, 2, P):
                piece()
            keep_picks(0, 0)
            dve.sem_inc(u_used, RING)
            with dve.Fori(0, PH - 1) as i:
                keys_, pairs_, experts_ = retrieval(1, i, 2, P)
                for s in range(W):
                    if s in (2, 6):
                        lo(B_LATE + (s == 6), i, 2)
                    if s in (10, 12):
                        scores(B_LATE + (s == 12), i, 2)
                    if s == 13:
                        query_ready(1, i)
                        keys_()
                    if s == 17:
                        pairs_()
                    if s == 21:
                        experts_()
                        keep_picks(1, i)
                    dot(s, i)
                keep_dots(i)
            R = PH * TS
            keys_, pairs_, experts_ = retrieval(PH, 0, 1, R)
            for s in range(W):
                if s == 4:
                    dve.wait_ge(s_scores, 1)
                    v.tensor_copy(sc[0:R, :, 0, :], bank[4][0:R, 0:2 * P].rearrange("p (s c) -> p s c", s=2)).then_inc(chain, 1)
                    n_chain = base + PH * N_TOP + 1
                    dve.wait_ge(chain, n_chain)
                    base += 1
                    keys_()
                if s == 8:
                    pairs_()
                if s == 12:
                    experts_()
                    for m in range(2):
                        ins = v.tensor_tensor(wide[0:R, m], picks[0:R, m, 0, :].unsqueeze(1).broadcast_to([R, PH, TOPK]),
                                              same_h[0:R, :].unsqueeze(2).broadcast_to([R, PH, TOPK]), ALU.mult)
                    ins.then_inc(wide_ready, 1)
                if s == 16:
                    dve.wait_ge(spread_mm, 1)
                    for m in range(2):
                        ins = v.tensor_tensor(own[:, m], bank[5][:, m * P:(m + 1) * P].rearrange("p (h k) -> p h k", h=PH),
                                              own16[:].unsqueeze(1).broadcast_to([P, PH, TOPK]), ALU.mult)
                    ins.then_inc(chain, 1)
                    dve.wait_ge(chain, base + (PH + 1) * N_TOP + 1)
                    v.tensor_reduce(own_s[:], own[:], AX_X, ALU.add).then_inc(chain, 1)
                    dve.wait_ge(chain, base + (PH + 1) * N_TOP + 2)
                    v.tensor_copy(idx_s[:], own_s[:, 0])
                    v.tensor_copy(g_s[:], own_s[:, 1]).then_inc(retrieved, 1)
                dot(s, PH - 1)
            keep_dots(PH - 1)
            dve.sem_inc(w_ready, 1)
            dve.wait_ge(rep_ready, 4)
            for s in range(PH):
                dve.wait_ge(ring_in[s], 16 * (PH * W // RING + 1))
                v.tensor_tensor_reduce(ring[s][:], ring[s][:], xs_rep[:], 1.0, 0.0, ALU.mult, ALU.add,
                                       dots_s[:, s:s + 1]).then_inc(dve_used if s in DVE_SLOTS else pe_used, 1)
            v.memset(zeros[:], 0.0).then_inc(cleared, 1)
            dve.wait_ge(gelu_done, ONE + 1)
            v.tensor_tensor(w_all[:], w_all[:], g_all[:], ALU.mult).then_inc(w_ready, 1)
            dve.wait_ge(gelu_done, ONE + 2)
            v.tensor_tensor(w_s[:], w_s[:], g_s[:], ALU.mult).then_inc(w_ready, 1)
            dve.wait_ge(w_ready, ONE + 3)
            dve.wait_ge(x2_back, 32)

            n_u = 2 * PH * TOPK // RING + 1
            for t in range(2):
                with dve.Fori(0, PH) as i:
                    for s in range(TOPK):
                        k = s % RING
                        if k not in DVE_SLOTS:
                            continue
                        nth = s // RING * N_DVE + DVE_SLOTS.index(k)
                        per = N_DVE * TOPK // RING
                        dve.wait_ge(ring_in[k], i * (16 * TOPK // RING)
                                    + 16 * (n_u + (t * PH * TOPK + s) // RING + 1))
                        dve.wait_ge(dve_used, i * per + t * PH * per + nth + N_DVE)
                        v.scalar_tensor_tensor(out=y_tok[:, t, :], in0=ring[k][:],
                                               scalar=w_all[:, bass.ds(i * W + t * TOPK + s, 1)],
                                               in1=y_tok[:, t, :], op0=ALU.mult, op1=ALU.add).then_inc(dve_used, 1)

            dve.wait_ge(row_in, 32)
            dve.wait_ge(dve_used, N_DVE * (2 * PH * TOPK // RING + 1))
            for t in range(3):
                q = P if t < 2 else TS
                dve.wait_ge(sum_ready, t + 1)
                for j in range(4):
                    part = y_tok[0:q, t, j * 512:(j + 1) * 512]
                    v.tensor_tensor(part, bank[4 * (t % 2) + j][0:q, :], part, ALU.add).then_inc(y_sum, 1)
                dve.wait_ge(y_ss, t + 1)
                v.tensor_scalar(mean_sq[0:q, t:t + 1], ssq[0:q, t:t + 1], 1.0 / D, EPS, ALU.mult,
                                ALU.add).then_inc(y_mean, 1)
                dve.wait_ge(y_root, t + 1)
                v.reciprocal(rstd[0:q, t:t + 1], root[0:q, t:t + 1]).then_inc(y_rstd, 1)
                dve.wait_ge(y_rstd, t + 1)
                v.scalar_tensor_tensor(out=y_tok[0:q, t, :], in0=y_tok[0:q, t, :], scalar=rstd[0:q, t:t + 1],
                                       in1=g_row[0:q, :], op0=ALU.mult, op1=ALU.mult).then_inc(y_ready, 1)

        @block.tensor
        def _(pe):
            mm = nc.tensor.matmul
            tr = nc.tensor.transpose

            def turn(p, src):
                for k in range(KT):
                    if k < 3 and p == 0:
                        pe.wait_ge(xn_done, 3)
                    if k == 0:
                        pe.wait_ge(xn_done, 3 * p + 3)
                    if k >= 6:
                        pe.wait_ge(al_done, 2 * p * KT + k - 5)
                    b = bank[2 + k % 6]
                    for t in range(3):
                        q = P if t < 2 else TS
                        ins = tr(b[:, t * P:t * P + q], src[0:q, t, k * P:(k + 1) * P], ident[0:q, 0:q])
                    ins.then_inc(tr_done, 1)

            def project(n0, i=0, L=0):
                pe.wait_ge(lo_done, n0 + 1 + i * L)
                if n0:
                    pe.wait_ge(acc_read, ONE + n0 - 1 + i * L)
                out = bank[ACC + n0 % 2][:, 0:T]
                for k in range(KT):
                    hi_, lo_ = w_hi[n0 % 2][:, k, :], w_lo[n0 % 2][:, k, :]
                    mm(out, hi_, act_hi[:, k, :], start=(k == 0), stop=False)
                    mm(out, hi_, act_lo[:, k, :], start=False, stop=False)
                    ins = mm(out, lo_, act_hi[:, k, :], start=False, stop=(k == KT - 1))
                ins.then_inc(mm_done, 1)

            def to_tokens(n0, i=0, L=0):
                pe.wait_ge(acc_read, ONE + n0 + 1 + i * L)
                pe.wait_ge(post_done, ONE + posts(n0 - 2) + i * L)
                b = bank[MISC + n0 % 2]
                st = stage[n0 % 2]
                for t in range(2):
                    tr(b[:, t * P:(t + 1) * P], st[:, t * P:(t + 1) * P], ident[:])
                mm(b[0:TS, 2 * P:3 * P], st[:, TP:T], ident[:], start=True, stop=True).then_inc(v_tr, 1)

            pe.wait_ge(consts, N_CONSTS)
            pe.wait_ge(par_in, 16 * N_PAR)
            tr(bank[2][:, 0:120], prow[0:120, :], ident[0:120, 0:120]).then_inc(par_T, 1)
            pe.wait_ge(keys_in, 16)
            for s in range(2):
                ins = tr(bank[3][:, s * P:(s + 1) * P], krow[:, s, :], ident[:])
            ins.then_inc(par_T, 1)
            pe.wait_ge(conv_in, 16)
            R = 2 * TS
            for k in range(KT):
                ins = tr(bank[4][:, k * R:(k + 1) * R], crow[0:R, k * P:(k + 1) * P], ident[0:R, 0:R])
            ins.then_inc(par_T, 1)
            pe.wait_ge(par_ready, 3)
            turn(0, x_tok)
            pe.wait_ge(al_done, KT)
            project(0)
            pe.wait_ge(wau_in, 16)
            pe.wait_ge(acc_read, ONE + 1)
            for m in range(H * KD):
                if m >= 6:
                    pe.wait_ge(la_ev, m - 5)
                mm(bank[2 + m % 6][:, 0:T], wau[0:RANK, m * P:(m + 1) * P], alr[0:RANK, :],
                   start=True, stop=True).then_inc(la_mm, 1)
            with pe.Fori(0, 4) as i:
                for b in range(4):
                    project(B_Q + b, i, 4)
            pe.wait_ge(la_ev, H * KD)
            project(B_V)
            with pe.Fori(0, 3) as i:
                for b in range(4):
                    project(B_V + b + 1, i, 4)
                    to_tokens(B_V + b, i, 4)
            for b in range(KT - 4, KT):
                if b + 1 < KT:
                    project(B_V + b + 1)
                to_tokens(B_V + b)

            def head_step(i, b):
                M = KD * TS
                project(B_SIX + b, i, 24)
                for c in (0, 1):
                    if b == 8 * c + 3:
                        pe.wait_ge(decayed, ONE + i * 2 + c + 1)
                        pe.wait_ge(attn_ready, ONE + i * 2 + c)
                        pe.wait_ge(k_read, ONE + i * 2 + c)
                        for k in range(KD):
                            mm(bank[MISC][:, 0:P], dk[:, k, :], dq[:, k, :], start=(k == 0), stop=(k == KD - 1))
                        for k in range(KD):
                            ins = tr(bank[MISC][:, (1 + k) * P:(2 + k) * P], dk1[:, k, :], ident[:])
                        ins.then_inc(attn_mm, 1)
                    if b == 8 * c + 5:
                        pe.wait_ge(attn_ready, ONE + i * 2 + c + 1)
                        pe.wait_ge(k_read, ONE + i * 2 + c + 1)
                        pe.wait_ge(o_ready, ONE + i * 3 + c)
                        if c == 0:
                            pe.wait_ge(ks_ready, i + 1)
                        else:
                            pe.wait_ge(S_ready, i * 2 + 1)
                        pe.wait_ge(oT_ready, ONE + i * 3 + c)
                        pe.wait_ge(u_read, ONE + i * 4 + 2 * c)
                        mm(bank[OB][:], attn[:], v_h[:, c, :], start=True, stop=(c == 0))
                        if c:
                            for k in range(KD):
                                mm(bank[OB][:], dq0[:, k, :], S[:, k, :], start=False, stop=(k == KD - 1))
                        for k in range(KD):
                            ins = mm(bank[KV0 + k][:], k_tok[:, k, :], v_h[:, c, :], start=True, stop=True)
                        ins.then_inc(o_mm, 1)
                for c, at in ((0, 9), (1, 17), (2, 22)):
                    if b == at:
                        pe.wait_ge(o_ready, ONE + i * 3 + c + 1)
                        if c < 2:
                            pe.wait_ge(S_ready, i * 2 + c + 1)
                        pe.wait_ge(oT_ready, ONE + i * 3 + c)
                        q, src = P if c < 2 else TS, o_sb
                        pe.sem_inc(granted, 1)
                        for d in range(HV):
                            ins = tr(bank[KV1 if c < 2 else OB][:, d * q:(d + 1) * q], src[0:q, d * P:(d + 1) * P], ident[0:q, 0:q])
                        ins.then_inc(o_tr, 1)
                if b == 1:
                    pe.wait_ge(staged, i * 9 + 9)
                    pe.wait_ge(oT_ready, ONE + i * 3)
                    for k in range(KD):
                        ins = mm(bank[OB][0:TS, k * P:(k + 1) * P], k_h[:, k, TP:T], ident[:], start=True, stop=True)
                    ins.then_inc(ks_mm, 1)
                m = b - 3
                if 0 <= m < M:
                    pe.wait_ge(ks_sel_ready, i * M + m + 1)
                    pe.wait_ge(s_new, ONE + i * M + m)
                    mm(bank[OUTER][:], ks_sel[m % 2][0:TS, :], v_h[0:TS, 2, :], start=True, stop=True).then_inc(outer_mm, 1)
                m = b - 4
                if 0 <= m < M:
                    if m == 0:
                        pe.wait_ge(q_sel_ready, i + 1)
                        pe.wait_ge(o_ready, ONE + i * 3)
                    pe.wait_ge(s_new, ONE + i * M + m + 1)
                    mm(bank[OS][0:TS, :], q_sel[:, m % KD, m // KD, :], s_ring[m % 4][:], start=(m == 0),
                       stop=(m == M - 1)).then_inc(os_mm, 1)
                if (b // 2) % 6 == 5:
                    q = (b // 12) * 2 + b % 2
                    pe.wait_ge(u_ready, i * 4 + q + 1)
                    pe.wait_ge(u_read, ONE + i * 4 + q)
                    pe.wait_ge(oT_ready, ONE + i * 3 + (1 if q < 2 else 2))
                    mm(bank[KV1][0:2 + TS, 0:P], u_pad[b % 2][:, TP:2 + T], ident[:],
                       start=True, stop=True).then_inc(u_tr, 1)

            with pe.Fori(0, H) as i:
                for b in range(SIX_PER_HEAD):
                    head_step(i, b)
            pe.wait_ge(al_done, 2 * KT)
            project(B_OUT)
            with pe.Fori(0, 3) as i:
                for b in range(4):
                    project(B_OUT + b + 1, i, 4)
                    to_tokens(B_OUT + b, i, 4)
            for b in range(KT - 4, KT):
                if b + 1 < KT:
                    project(B_OUT + b + 1)
                to_tokens(B_OUT + b)
            turn(1, xn_tok)
            pe.wait_ge(al_done, 3 * KT)

            def scores(n0, i=0, L=0):
                pe.wait_ge(acc_read, ONE + n0 + 1 + i * L)
                pe.wait_ge(post_done, ONE + posts(n0 - 2) + i * L)
                b, st, s = bank[MISC + n0 % 2], stage[n0 % 2], (n0 - B_QRY) % 2
                for t in range(2):
                    ins = mm(b[:, t * P:(t + 1) * P], st[:, t * P:(t + 1) * P], keysT[:, s, :], start=True, stop=True)
                ins.then_inc(v_tr, 1)

            for half in range(2):
                project(B_QRY + half)
            for half in range(2):
                scores(B_QRY + half)
            pe.wait_ge(h2_ready, 1)
            for j in range(4):
                ins = mm(bank[4 + j][:], spread[0:TS, :], xn_tok[0:TS, 2, j * 512:(j + 1) * 512], start=True, stop=True)
            ins.then_inc(rep_mm, 1)
            with pe.Fori(0, PH - 1) as i:
                for half in range(2):
                    project(B_LATE + half, i, 2)
                for half in range(2):
                    scores(B_LATE + half, i, 2)
            R = PH * TS
            pe.wait_ge(q_s_ready, 2 * PH)
            pe.wait_ge(rep_ready, 4)
            for s in range(2):
                ins = mm(bank[4][0:R, s * P:(s + 1) * P], q_s[:, s].rearrange("p h j -> p (h j)"), keysT[:, s, :],
                         start=True, stop=True)
            ins.then_inc(s_scores, 1)
            pe.wait_ge(wide_ready, 1)
            for m in range(2):
                ins = mm(bank[5][:, m * P:(m + 1) * P], same_j[0:R, :], wide[0:R, m].rearrange("p h k -> p (h k)"),
                         start=True, stop=True)
            ins.then_inc(spread_mm, 1)

            def open_sums(t, q):
                for j in range(4):
                    mm(bank[4 * (t % 2) + j][0:q, :], zeros[:, 0:q], zeros[:], start=True, stop=False)

            pe.wait_ge(cleared, 2)
            n_u = 2 * PH * TOPK // RING + 1
            per = N_PE * TOPK // RING
            for t in range(2):
                open_sums(t, P)
                with pe.Fori(0, PH) as i:
                    for s in range(TOPK):
                        k = s % RING
                        if k in DVE_SLOTS:
                            continue
                        nth = s // RING * N_PE + PE_SLOTS.index(k)
                        pe.wait_ge(diag_ready, ONE + i * per + t * PH * per + nth + 1)
                        pe.wait_ge(ring_in[k], i * (16 * TOPK // RING)
                                   + 16 * (n_u + (t * PH * TOPK + s) // RING + 1))
                        for j in range(4):
                            ins = mm(bank[4 * t + j][:], diag[nth % 4][:], ring[k][:, j * 512:(j + 1) * 512],
                                     start=False, stop=False, skip_group_check=True)
                        ins.then_inc(pe_used, 1)
                for j in range(4):
                    ins = mm(bank[4 * t + j][:], zeros[:, 0:P], zeros[:], start=False, stop=True)
                ins.then_inc(sum_ready, 1)
            pe.wait_ge(y_sum, 4)
            open_sums(2, TS)
            for s in range(PH):
                pe.wait_ge(diag_ready, ONE + 2 * PH * per + s + 1)
                pe.wait_ge(ring_in[s], 16 * (n_u + 2 * PH * TOPK // RING + 1))
                for j in range(4):
                    ins = mm(bank[j][0:TS, :], diag_s[s % 4][:], ring[s][:, j * 512:(j + 1) * 512],
                             start=False, stop=False, skip_group_check=True)
                ins.then_inc(pe_used, 1)
            for j in range(4):
                ins = mm(bank[j][0:TS, :], zeros[:, 0:TS], zeros[:], start=False, stop=True)
            ins.then_inc(sum_ready, 1)


_INS = ["x_prompt", "x_sample", "state_gla", "state_conv", "norm1_g", "w_in", "w_alpha_up", "b_alpha",
        "gla_norm_g", "conv_w", "conv_b", "w_out", "norm2_g", "w_query", "sub_keys", "expert_u", "expert_v",
        "norm_f_g"]


def kernel(**inputs):
    import numpy as np
    import concourse.bacc as bacc
    from concourse.bass_utils import run_bass_kernel_spmd

    nc = bacc.Bacc("TRN2", target_bir_lowering=False, num_devices=1)
    arrays, args = {}, []
    for name in _INS:
        x = np.ascontiguousarray(inputs[name])
        arrays[f"in_{name}"] = x
        args.append(nc.dram_tensor(f"in_{name}", x.shape, mybir.dt.from_np(x.dtype), kind="ExternalInput").ap())
    xp, xs, sg, sc = (inputs[n].shape for n in _INS[:4])
    outs = [xp, xs, (sg[0], xp[0], *sg[2:]), (sc[0], xp[0], *sc[2:]), sg, sc]
    for n, shape in enumerate(outs):
        args.append(nc.dram_tensor(f"out_{n}", tuple(shape), F32, kind="ExternalOutput").ap())
    hybrid_step(nc, *args)
    r = run_bass_kernel_spmd(nc, [arrays], core_ids=[0])
    return tuple(r.results[0][f"out_{n}"] for n in range(len(outs)))
```

```python
from contextlib import ExitStack

import concourse.bass as bass
from concourse import mybir

F32 = mybir.dt.float32
F32R = mybir.dt.float32r
U32 = mybir.dt.uint32
ALU = mybir.AluOpType
ACT = mybir.ActivationFunctionType
AX_X = mybir.AxisListType.X

P = 128
EPS = 1e-6
CHUNK = 128
TAU = 16.0
ONE = 1
NEG_BIG = -3.0e38


def hybrid_step(nc, x_prompt, x_sample, state_gla, state_conv, norm1_g, w_in, w_alpha_up, b_alpha,
                gla_norm_g, conv_w, conv_b, w_out, norm2_g, w_query, sub_keys, expert_u, expert_v,
                norm_f_g, y_prompt, y_sample, gla_prompt, conv_prompt, gla_sample, conv_sample):
    D = x_prompt.shape[2]
    TP, TS = x_prompt.shape[1], x_sample.shape[0]
    T = TP + TS
    KT = D // P
    H, DK, DV = state_gla.shape[2:]
    KD = DK // P
    HV = DV // P
    RANK = w_alpha_up.shape[1]
    NKEY = sub_keys.shape[2]
    PH, TOPK = 8, 16
    assert T == 2 * P + TS and KD == 2 and HV == 4 and TS * TOPK == P and NKEY == P

    COL_K = H * DK
    COL_V = 2 * H * DK
    COL_R = COL_V + H * DV
    COL_ALR = COL_R + H * DV
    COL_CB = COL_ALR + RANK
    COL_CC, COL_CX, COL_GA, COL_GB = (COL_CB + D * j for j in (1, 2, 3, 4))
    SIX = (COL_R, COL_GA, COL_CB, COL_CC, COL_CX, COL_GB)

    B_Q, B_K, B_V, B_SIX = 1, 1 + H * KD, 1 + 2 * H * KD, 1 + 2 * H * KD + KT
    SIX_PER_HEAD = 2 * 6 * 2
    B_OUT = B_SIX + H * SIX_PER_HEAD
    B_QRY = B_OUT + KT
    B_END = B_QRY + 2 * PH
    N_PAR = 5 * H + 3
    N_CONSTS, N_LATE_CONSTS = 22, 12
    N_LINKS = 17
    POSTS = 2 * 4 * 2

    def posts(n0):
        n = min(max(n0 + 1 - B_V, 0), KT)
        for b in range(min(max(n0 + 1 - B_SIX, 0), H * SIX_PER_HEAD)):
            n += (b // 2) % 6 not in (2, 3)
        return n + max(n0 + 1 - B_OUT, 0)
    B_LATE = B_QRY + 2

    x_p = x_prompt.rearrange("b (t p) d -> p (b t) d", p=P)
    x_s = x_sample.rearrange("b s d -> (b s) d")
    win = w_in.rearrange("o (k p) n -> p (o k) n", p=P)
    wout = w_out.rearrange("o (k p) n -> p (o k) n", p=P)
    wqry = w_query.rearrange("o (k p) n -> p (o k) n", p=P)
    eu = expert_u.rearrange("o e d -> (o e) d")
    ev = expert_v.rearrange("o e d -> (o e) d")
    st_in = state_gla.rearrange("o j h (k p) v -> p (o h) k j v", p=P)
    st_out = gla_sample.rearrange("o j h (k p) v -> p (o h) k j v", p=P)
    stp_out = gla_prompt.rearrange("o b h (k p) v -> p (o b h) k v", p=P)

    with ExitStack() as ctx:
        top = (nc.sbuf_base + 63) // 64 * 64
        where = [top]

        def sb_at(name, shape, dt, at):
            return nc.alloc_sbuf_tensor_at(name, shape, dt, offset=at)

        def room(nbytes):
            at = where[0]
            where[0] += (nbytes + 31) // 32 * 32
            assert where[0] <= nc.sbuf_usable_end, (where[0], nc.sbuf_usable_end)
            return at

        def size(shape):
            n = 4
            for s in shape[1:]:
                n *= s
            return n

        def sb(name, shape, dt=F32):
            return sb_at(name, shape, dt, room(size(shape)))

        def sem(name):
            return ctx.enter_context(nc.semaphore(name))

        ident = sb("ident", [P, P])
        causal = sb("causal", [P, P])
        eye8 = sb("eye8", [P, TS, TS])
        gather8 = sb("gather8", [P, TS])
        same_h = sb("same_h", [P, PH])
        own16 = sb("own16", [P, TOPK])
        iota16 = sb("iota16", [P, TOPK])
        pcol = sb("pcol", [P, 120])
        keysT = sb("keysT", [P, 2, NKEY])
        ssq = sb("ssq", [P, 3])
        mean_sq = sb("mean_sq", [P, 3])
        root = sb("root", [P, 3])
        rstd = sb("rstd", [P, 3])
        keep = where[0]

        at_act = where[0]
        act_hi = sb("act_hi", [P, KT, T], F32R)
        act_lo = sb("act_lo", [P, KT, T], F32R)
        at_raw = where[0]
        raw = [sb(f"raw{s}", [P, KT, P]) for s in range(4)]
        at_w = where[0]
        w_hi = [sb(f"w_hi{s}", [P, KT, P], F32R) for s in range(2)]
        w_lo = [sb(f"w_lo{s}", [P, KT, P], F32R) for s in range(2)]
        at_qk = room(4 * KT * T)
        qk = sb_at("qk", [P, KT, T], F32, at_qk)
        mT = sb_at("mT", [P, KT, T], F32, at_qk)
        at_la = room(4 * H * KD * T)
        la = sb_at("la", [P, H * KD, T], F32, at_la)
        at_tok = room(4 * 3 * D)
        x_tok = sb_at("x_tok", [P, 3, D], F32, at_tok)
        v_tok = sb_at("v_tok", [P, 3, D], F32, at_tok)
        x2_tok = sb_at("x2_tok", [P, 3, D], F32, at_tok)
        at_head = where[0]
        v_h = sb("v_h", [P, 2, DV])
        q_h = sb("q_h", [P, KD, T])
        k_h = sb("k_h", [P, KD, T])
        la_h = sb("la_h", [P, KD, T])
        la_tmp = sb_at("la_tmp", [P, H * KD, T], F32, at_head)
        cols = sb("cols", [P, H * KD, 8])
        cols_h = sb("cols_h", [P, KD, 8])
        decS = sb("decS", [P, H * KD, TS])
        decS_h = sb("decS_h", [P, KD, TS])
        pcol_h = sb("pcol_h", [P, 20])
        convT = sb("convT", [P, KT, 2 * TS])
        convT_h = sb("convT_h", [P, HV, 2 * TS])
        dq = sb("dq", [P, KD, P])
        dk = sb("dk", [P, KD, P])
        dq0 = sb("dq0", [P, KD, P])
        dk1 = sb("dk1", [P, KD, P])
        k_tok = sb("k_tok", [P, KD, P])
        attn = sb("attn", [P, P])
        S = sb("S", [P, KD, DV])
        o_sb = sb("o_sb", [P, DV])
        oT = sb("oT", [P, HV, T])
        gss = sb("gss", [P, 8])
        at_ring = room(4 * 4 * DV)
        s_ring = [sb_at(f"s_ring{s}", [P, DV], F32, at_ring + 4 * s * DV) for s in range(4)]
        sq_junk = sb_at("sq_junk", [P, D], F32, at_ring)
        q_sel = sb("q_sel", [P, KD, TS, TS])
        v_row = [sb(f"v_row{s}", [P, DV]) for s in range(2)]
        kv_even = sb("kv_even", [P, DV])
        tA = [sb(f"tA{s}", [P, T]) for s in range(2)]
        tR = [sb(f"tR{s}", [P, T]) for s in range(2)]
        u_pad = [sb(f"u_pad{s}", [P, 2 + T]) for s in range(2)]
        at_gate = where[0]
        gate = sb("gate", [P, HV, T])
        yb = sb("yb", [P, HV, T])
        u_rows = sb("u_rows", [P, HV * P])
        wau = sb_at("wau", [P, H * DK], F32, at_gate)
        prow = sb_at("prow", [P, P], F32, at_head)
        krow = sb_at("krow", [P, 2, P], F32, at_head + 512)
        crow = sb_at("crow", [P, D], F32, at_head + 2048)
        alr = sb_at("alr", [P, T], F32, at_gate + size([P, HV, T]))
        stage = [sb_at(f"stage{s}", [P, T], F32, at_head + 1056 * s) for s in range(2)]

        bank = [ctx.enter_context(nc.psum_tensor(f"bank{b}", [P, 512], F32)) for b in range(8)]
        ACC, MISC, OB, KV0, KV1, OS = 0, 2, 3, 4, 5, 6

        xn_tok = sb_at("xn_tok", [P, 3, D], F32, at_qk)
        assert at_qk + size([P, 3, D]) <= at_tok
        where[0] = at_head + 2112
        spread = sb("spread", [P, P])
        same_j = sb("same_j", [P, P])
        g_row = sb("g_row", [P, D])
        q_s = sb("q_s", [P, 2, PH, TS])
        sc = sb("sc", [P, 2, 2, NKEY])
        cand = sb("cand", [P, 2, TOPK * TOPK])
        hot = [sb(f"hot{s}", [P, 2, TOPK, TOPK]) for s in range(2)]
        val = sb("val", [P, 2, 2, TOPK])
        key_u = sb("key_u", [P, 2, 2, TOPK], U32)
        key_f = sb("key_f", [P, 2, 2, TOPK])
        best = sb("best", [P, 2, TOPK])
        pos = sb("pos", [P, 2, TOPK], U32)
        pos_u = sb("pos_u", [P, 2, 2, TOPK], U32)
        pos_f = sb("pos_f", [P, 2, 2, TOPK])
        key_sel = sb("key_sel", [P, 2, 2, TOPK])
        soft = sb("soft", [P, 2, TOPK])
        soft_s = sb("soft_s", [P, 2])
        soft_r = sb("soft_r", [P, 2])
        picks = sb("picks", [P, 2, 2, TOPK])
        wide = sb("wide", [P, 2, PH, TOPK])
        own = sb("own", [P, 2, PH, TOPK])
        own_s = sb("own_s", [P, 2, PH])
        idx_all = sb("idx_all", [P, PH * 2 * TOPK], U32)
        g_all = sb("g_all", [P, PH * 2 * TOPK])
        w_all = sb("w_all", [P, PH * 2 * TOPK])
        idx_s = sb("idx_s", [P, PH], U32)
        g_s = sb("g_s", [P, PH])
        w_s = sb("w_s", [P, PH])
        dots = sb("dots", [P, 2 * TOPK])
        dots_s = sb("dots_s", [P, PH])
        idx_st = sb("idx_st", [P, 8], U32)
        RING = 8
        ring_at = [room(size([P, D])) for _ in range(3)]
        ring_at += [at_tok + t * size([P, D]) for t in range(3)] + [at_raw + s * size([P, D]) for s in (2, 3)]
        ring = [sb_at(f"ring{s}", [P, D], F32, at) for s, at in enumerate(ring_at)]
        where[0] = at_act
        xs_rep = sb("xs_rep", [P, D])
        y_tok = sb("y_tok", [P, 3, D])
        assert where[0] <= at_raw
        where[0] = at_w
        y_sq = sb("y_sq", [P, D])
        diag = [sb(f"diag{s}", [P, P]) for s in range(4)]
        diag_s = [sb(f"diag_s{s}", [P, TS]) for s in range(4)]
        zeros = sb("zeros", [P, 512])
        assert where[0] <= at_qk
        DVE_SLOTS = (3, 7)
        PE_SLOTS = tuple(k for k in range(RING) if k not in DVE_SLOTS)
        N_DVE, N_PE = len(DVE_SLOTS), len(PE_SLOTS)
        TURNS = PH * TOPK // RING
        PE_TILE = N_PE * TURNS
        ORDER = (0, 2, 1)
        sample_slot = [PE_SLOTS[(s - 2) % N_PE] for s in range(PH)]

        def sum_bank(t):
            return 4 if t == 2 else 0

        def v_fills(t, k):
            return 0 if t == 0 else TURNS + sample_slot.count(k)
        v_dram = nc.dram_tensor("v_samples", [TS, D], F32, kind="Internal").ap()
        x2_dram = nc.dram_tensor("x2_spill", [P, 3, D], F32, kind="Internal").ap()

        consts = sem("consts")
        x_in = [sem(f"x_in{t}") for t in range(3)]
        par_in = sem("par_in")
        conv_in = sem("conv_in")
        keys_in = sem("keys_in")
        wau_in = sem("wau_in")
        par_T = sem("par_T")
        par_ready = sem("par_ready")
        raw_in = [sem(f"raw_in{s}") for s in range(4)]
        hi_done = sem("hi_done")
        lo_done = sem("lo_done")
        mm_done = sem("mm_done")
        acc_read = sem("acc_read")
        post_done = sem("post_done")
        ss_done = sem("ss_done")
        ms_done = sem("ms_done")
        rt_done = sem("rt_done")
        rs_done = sem("rs_done")
        xn_done = sem("xn_done")
        tr_done = sem("tr_done")
        ah_done = sem("ah_done")
        al_done = sem("al_done")
        la_mm = sem("la_mm")
        la_ev = sem("la_ev")
        la_step = sem("la_step")
        la_ready = sem("la_ready")
        v_tr = sem("v_tr")
        staged = sem("staged")
        head_done = sem("head_done")
        exps = sem("exps")
        decayed = sem("decayed")
        attn_mm = sem("attn_mm")
        k_read = sem("k_read")
        attn_ready = sem("attn_ready")
        o_mm = sem("o_mm")
        o_sum = sem("o_sum")
        o_mean = sem("o_mean")
        o_root = sem("o_root")
        o_rstd = sem("o_rstd")
        o_ready = sem("o_ready")
        o_tr = sem("o_tr")
        oT_ready = sem("oT_ready")
        S_ready = sem("S_ready")
        S_out = sem("S_out")
        q_sel_ready = sem("q_sel_ready")
        s_in = [sem(f"s_in{s}") for s in range(4)]
        s_out = [sem(f"s_out{s}") for s in range(4)]
        v_out = sem("v_out")
        v_in = [sem(f"v_in{s}") for s in range(2)]
        kv_ready = sem("kv_ready")
        s_new = sem("s_new")
        os_mm = sem("os_mm")
        u_ready = sem("u_ready")
        u_tr = sem("u_tr")
        u_read = sem("u_read")
        u_out = sem("u_out")
        chain = sem("chain")
        m_ready = sem("m_ready")
        granted = sem("granted")
        conv_copy = sem("conv_copy")
        x2_in = sem("x2_in")
        cleared = sem("cleared")
        soft_in = sem("soft_in")
        soft_e = sem("soft_e")
        spread_mm = sem("spread_mm")
        retrieved = sem("retrieved")
        row_in = sem("row_in")
        h2_ready = sem("h2_ready")
        rep_mm = sem("rep_mm")
        rep_ready = sem("rep_ready")
        idx_staged = sem("idx_staged")
        ring_in = [sem(f"ring_in{s}") for s in range(RING)]
        u_used = sem("u_used")
        pe_used = sem("pe_used")
        dve_used = sem("dve_used")
        x2_out = sem("x2_out")
        x2_back = sem("x2_back")
        q_s_ready = sem("q_s_ready")
        wide_ready = sem("wide_ready")
        s_scores = sem("s_scores")
        gelu_done = sem("gelu_done")
        w_ready = sem("w_ready")
        diag_ready = sem("diag_ready")
        sum_ready = sem("sum_ready")
        y_sum = sem("y_sum")
        y_ss = sem("y_ss")
        y_mean = sem("y_mean")
        y_root = sem("y_root")
        y_rstd = sem("y_rstd")
        y_ready = sem("y_ready")
        y_out = sem("y_out")

        from_one = (head_done, post_done, decayed, o_mm, o_tr, u_out, w_ready, diag_ready, os_mm, attn_mm,
                    kv_ready, S_out, o_ready, gelu_done, acc_read, k_read, attn_ready, s_new, oT_ready, u_read)

        block = ctx.enter_context(nc.Block())

        def m_at(k):
            return k // 4 * 2 + k % 4 // 2 * (KT // 2) + k % 2

        def kv_at(m):
            return kv_even if m % KD == 0 else v_row[m // KD % 2]

        def raw_slot(n0):
            if n0 < B_LATE:
                return n0 % 4, n0 // 4 + 1
            s = n0 % 2
            return s, (B_LATE - 1 - s) // 4 + 1 + (n0 - B_LATE) // 2 + 1

        def raw_loads(n0, i, L):
            return 16 * raw_slot(n0)[1] + i * (16 * (L // 4 if n0 < B_LATE else L // 2))

        @block.sync
        def _(sp):
            for counter in from_one:
                sp.sem_inc(counter, ONE)
            for t in range(2):
                sp.dma_start(x_tok[:, t, :], x_p[:, t, :]).then_inc(x_in[t], 16)
            sp.dma_start(x_tok[0:TS, 2, :], x_s).then_inc(x_in[2], 16)
            n_par = 0
            for h in range(H):
                r = 20 * h
                span = slice(h * DV, (h + 1) * DV)
                for src in (gla_norm_g[:, span], conv_w[0, 0:1, span], conv_w[0, 1:2, span],
                            conv_w[0, 2:3, span], conv_b[:, span]):
                    sp.dma_start(prow[r:r + HV, :], src.rearrange("o (r c) -> (o r) c", c=P)).then_inc(par_in, 16)
                    r += HV
                    n_par += 1
            for r, src in ((80, norm1_g), (80 + KT, norm2_g), (80 + 2 * KT, b_alpha)):
                rows = src.shape[1] // P
                sp.dma_start(prow[r:r + rows, :], src.rearrange("o (r c) -> (o r) c", c=P)).then_inc(par_in, 16)
                n_par += 1
            assert n_par == N_PAR
            sp.dma_start(crow[0:2 * TS, :], state_conv.rearrange("o j s d -> (o j s) d")).then_inc(conv_in, 16)
            sp.dma_start(krow[:], sub_keys.rearrange("o s n d -> n (o s) d")).then_inc(keys_in, 16)
            sp.dma_start(wau[0:RANK, :], w_alpha_up.rearrange("o r n -> (o r) n")).then_inc(wau_in, 16)
            sp.dma_start(conv_sample.rearrange("o j s d -> (o j) s d")[:, 0, :],
                         state_conv.rearrange("o j s d -> (o j) s d")[:, 1, :]).then_inc(conv_copy, 16)

            def load(n0, src, i=0, L=0):
                s = raw_slot(n0)[0]
                if n0 >= 4:
                    sp.wait_ge(lo_done, (n0 - 3 if n0 < B_LATE else n0 - 1) + i * L)
                sp.dma_start(raw[s][:], src).then_inc(raw_in[s], 16)

            load(0, win[:, :, COL_ALR:COL_ALR + P])
            for n in (1, 2, 3):
                load(n, win[:, :, (n - 1) * P:n * P])
            with sp.Fori(0, 7) as i:
                for j in range(4):
                    load(4 + j, win[:, :, bass.ds((3 + j) * P + i * (4 * P), P)], i, 4)
            load(B_SIX - 1, win[:, :, (B_SIX - 2) * P:(B_SIX - 1) * P])
            with sp.Fori(0, H) as i:
                for b in range(SIX_PER_HEAD):
                    cg, t, half = b // 12, (b // 2) % 6, b % 2
                    load(B_SIX + b, win[:, :, bass.ds(SIX[t] + (2 * cg + half) * P + i * DV, P)], i, 24)
            with sp.Fori(0, 4) as i:
                for j in range(4):
                    load(B_OUT + j, wout[:, :, bass.ds(j * P + i * (4 * P), P)], i, 4)
            for j in range(2):
                load(B_QRY + j, wqry[:, :, j * P:(j + 1) * P])
            sp.wait_ge(cleared, 1)
            sp.dma_start(g_row[:], norm2_g.partition_broadcast(P).rearrange("p o d -> p (o d)")).then_inc(row_in, 16)
            with sp.Fori(0, PH - 1) as i:
                for j in range(2):
                    load(B_LATE + j, wqry[:, :, bass.ds((2 + j) * P + i * (2 * P), P)], i, 2)
            sp.wait_ge(mm_done, B_END)
            sp.wait_ge(x2_out, 32)
            sp.dma_start(y_tok[:, 0:2, :], x2_dram[:, 0:2, :]).then_inc(x2_back, 16)
            sp.dma_start(y_tok[0:TS, 2, :], x2_dram[0:TS, 2, :]).then_inc(x2_back, 16)
            sp.wait_ge(h2_ready, 3)
            sp.dma_start(g_row[:], norm_f_g.partition_broadcast(P)).then_inc(row_in, 16)
            for nth, t in enumerate(ORDER):
                sp.wait_ge(y_ready, nth + 1)
                out, src = ((y_prompt.rearrange("b (t p) d -> p (b t) d", p=P)[:, t, :], y_tok[:, t, :]) if t < 2
                            else (y_sample.rearrange("b s d -> (b s) d"), y_tok[0:TS, 2, :]))
                sp.dma_start(out, src).then_inc(y_out, 16)
            sp.wait_ge(conv_copy, 16)
            sp.wait_ge(y_out, 48)

        @block.gpsimd
        def _(pool):
            g = nc.gpsimd
            n = 0

            def made(ins):
                nonlocal n
                n += 1
                ins.then_inc(consts, 1)

            def ones_where(out, pattern, base, mult, first=None):
                made(g.memset(out, 0.0))
                pool.wait_ge(consts, n)
                made(g.affine_select(out=out, in_=out, compare_op=ALU.not_equal, fill=1.0, base=base,
                                     pattern=pattern, channel_multiplier=mult))

            ones_where(ident[:], [[-1, P]], 0, 1)
            ones_where(eye8[:], [[1, TS], [-1, TS]], 0, 0)
            made(g.memset(causal[:], 1.0))
            pool.wait_ge(consts, n)
            made(g.affine_select(out=causal[:], in_=causal[:], compare_op=ALU.is_ge, fill=0.0, base=0,
                                 pattern=[[1, P]], channel_multiplier=-1))
            def sample_rows(m, pat, mult, width):
                made(g.memset(m[:], 1.0))
                pool.wait_ge(consts, n)
                made(g.affine_select(out=m[:], in_=m[:], compare_op=ALU.is_ge, fill=0.0, base=0,
                                     pattern=[[pat, width]], channel_multiplier=mult))
                pool.wait_ge(consts, n)
                made(g.affine_select(out=m[:], in_=m[:], compare_op=ALU.is_ge, fill=0.0, base=TOPK - 1,
                                     pattern=[[-pat, width]], channel_multiplier=-mult))

            sample_rows(gather8, -TOPK, 1, TS)
            made(g.memset(own16[:], 0.0))
            for j in range(TS):
                pool.wait_ge(consts, n)
                made(g.affine_select(out=own16[:], in_=own16[:], compare_op=ALU.not_equal, fill=1.0,
                                     base=-TOPK * j, pattern=[[-1, TOPK]], channel_multiplier=1))
            made(g.memset(same_h[:], 1.0))
            pool.wait_ge(consts, n)
            made(g.affine_select(out=same_h[:], in_=same_h[:], compare_op=ALU.is_ge, fill=0.0, base=0,
                                 pattern=[[-TS, PH]], channel_multiplier=1))
            pool.wait_ge(consts, n)
            made(g.affine_select(out=same_h[:], in_=same_h[:], compare_op=ALU.is_ge, fill=0.0, base=TS - 1,
                                 pattern=[[TS, PH]], channel_multiplier=-1))
            made(g.iota(iota16[:], pattern=[[1, TOPK]], base=0, channel_multiplier=0,
                        allow_small_or_imprecise_dtypes=True))
            assert n == N_CONSTS, n

            pool.wait_ge(la_ready, 3)
            pool.wait_ge(par_ready, 3)
            pool.wait_ge(post_done, ONE + KT)
            g.dma_start(v_dram[:], v_tok[0:TS, 2, :]).then_inc(v_out, 16)
            with pool.Fori(0, H) as i:
                pool.wait_ge(head_done, ONE + i)
                pool.sem_inc(granted, 1)
                g.tensor_copy(cols_h[:], cols[:, bass.ds(i * KD, KD), :]).then_inc(staged, 1)
                g.tensor_copy(la_h[:], la[:, bass.ds(i * KD, KD), :]).then_inc(staged, 1)
                g.tensor_copy(pcol_h[:], pcol[:, bass.ds(i * 20, 20)]).then_inc(staged, 1)
                g.tensor_copy(convT_h[:], convT[:, bass.ds(i * HV, HV), :]).then_inc(staged, 1)
                g.tensor_copy(q_h[:], qk[:, bass.ds(i * KD, KD), :]).then_inc(staged, 1)
                g.tensor_copy(k_h[:], qk[:, bass.ds(i * KD + H * KD, KD), :]).then_inc(staged, 1)
                g.tensor_copy(decS_h[:], decS[:, bass.ds(i * KD, KD), :]).then_inc(staged, 1)

                def load_v(j):
                    g.dma_start(v_row[j % 2][:], v_dram[j:j + 1, bass.ds(i * DV, DV)].partition_broadcast(P)
                                .rearrange("p o v -> p (o v)")).then_inc(v_in[j % 2], 16)

                def load(m):
                    g.dma_start(s_ring[m % 4][:], st_in[:, bass.ds(i, 1), m % KD, m // KD, :]
                                .rearrange("p o v -> p (o v)")).then_inc(s_in[m % 4], 16)

                M = KD * TS
                pool.wait_ge(v_out, 16)
                load_v(0)
                for m in range(4):
                    load(m)
                load_v(1)
                g.tensor_copy(v_h[:, 0:2, :], v_tok[:, 0:2, bass.ds(i * DV, DV)]).then_inc(staged, 1)
                for m in range(M):
                    pool.wait_ge(s_new, ONE + i * M + m + 1)
                    pool.sem_inc(granted, 1)
                    g.dma_start(st_out[:, bass.ds(i, 1), m % KD, m // KD, :]
                                .rearrange("p o v -> p (o v)"), s_ring[m % 4][:]).then_inc(s_out[m % 4], 16)
                    if m % KD == KD - 1 and m // KD + 2 < TS:
                        load_v(m // KD + 2)
                    if m + 4 < M:
                        pool.wait_ge(s_out[m % 4], i * (4 * 16) + 16 * (m // 4) + 16)
                        pool.sem_inc(granted, 1)
                        pool.wait_ge(os_mm, ONE + i * M + m + 1)
                        pool.sem_inc(granted, 1)
                        load(m + 4)
                for s in range(4):
                    pool.wait_ge(s_out[s], i * (4 * 16) + 64)
                    pool.sem_inc(granted, 1)
            for s in range(4):
                pool.wait_ge(s_out[s], H * 64)
            pool.wait_ge(head_done, ONE + H)
            g.dma_start(x2_tok[:, 0:2, :], x_p).then_inc(x2_in, 16)
            g.dma_start(x2_tok[0:TS, 2, :], x_s).then_inc(x2_in, 16)

            pool.wait_ge(cleared, 1)
            sample_rows(spread, 1, -TOPK, P)
            made(g.memset(same_j[:], 0.0))
            for h in range(PH):
                pool.wait_ge(consts, n)
                made(g.affine_select(out=same_j[:].rearrange("p (j r) -> p j r", j=TS),
                                     in_=same_j[:].rearrange("p (j r) -> p j r", j=TS),
                                     compare_op=ALU.not_equal, fill=1.0, base=-TS * h,
                                     pattern=[[-1, TS], [0, TOPK]], channel_multiplier=1))
            assert n == N_CONSTS + N_LATE_CONSTS, n

            def fetch(table, free_sem, free_at, src, k, n_staged):
                pool.wait_ge(free_sem, free_at)
                pool.sem_inc(granted, 1)
                g.tensor_copy(idx_st[:, k:k + 1], src).then_inc(idx_staged, 1)
                pool.wait_ge(idx_staged, n_staged)
                pool.sem_inc(granted, 1)
                g.indirect_dma_start(ring[k][:], None, table,
                                     bass.IndirectOffsetOnAxis(ap=idx_st[:, k:k + 1], axis=0)).then_inc(ring_in[k], 16)

            W = 2 * TOPK
            pool.wait_ge(x2_out, 32)
            with pool.Fori(0, PH) as i:
                pool.wait_ge(retrieved, i + 1)
                pool.sem_inc(granted, 1)
                for s in range(W):
                    if s == 3:
                        pool.wait_ge(h2_ready, 3)
                    fetch(eu, u_used, i * W + s + 1, idx_all[:, bass.ds(i * W + s, 1)], s % RING, i * W + s + 1)
            pool.wait_ge(retrieved, PH + 1)
            for s in range(PH):
                fetch(eu, u_used, PH * W + s + 1, idx_s[:, s:s + 1], s, PH * W + s + 1)
            U = PH * W + PH
            for t in range(2):
                with pool.Fori(0, PH) as i:
                    for s in range(TOPK):
                        k, turn = s % RING, t * TURNS + s // RING
                        if k in DVE_SLOTS:
                            who, n, at = dve_used, N_DVE, N_DVE * turn + DVE_SLOTS.index(k) + 1
                        else:
                            who, n, at = pe_used, N_PE, N_PE * turn + PE_SLOTS.index(k) + 1 + t * PH
                        fetch(ev, who, at + i * (n * TOPK // RING), idx_all[:, bass.ds(i * W + t * TOPK + s, 1)],
                              k, i * TOPK + U + t * (PH * TOPK + PH) + s + 1)
                if t == 0:
                    for s in range(PH):
                        fetch(ev, pe_used, N_PE + PE_TILE + (s - 1 if s < 2 else max(s - 5, 0)), idx_s[:, s:s + 1],
                              sample_slot[s], U + PH * TOPK + s + 1)

        @block.scalar
        def _(act):
            a = nc.scalar

            def hi(n0, i=0, L=0):
                s = raw_slot(n0)[0]
                act.wait_ge(raw_in[s], raw_loads(n0, i, L))
                a.activation(w_hi[n0 % 2][:], raw[s][:], ACT.Copy).then_inc(hi_done, 1)

            def evac_wait(n0, i, L):
                act.wait_ge(post_done, ONE + posts(n0 - 4) + i * (POSTS if L == 24 else L if n0 >= B_V else 0))

            def norm():
                for t in range(3):
                    q = P if t < 2 else TS
                    if t:
                        act.wait_ge(ss_done, t)
                    act.wait_ge(x_in[t], 16)
                    a.activation(sq_junk[0:q, :], x_tok[0:q, t, :], ACT.Square,
                                 accum_out=ssq[0:q, t:t + 1]).then_inc(ss_done, 1)
                act.wait_ge(ms_done, 1)
                a.activation(root[:], mean_sq[:], ACT.Sqrt).then_inc(rt_done, 1)

            def act_parts(p, gcol):
                for k in range(KT):
                    act.wait_ge(tr_done, KT * p + k + 1)
                    a.activation(act_hi[:, k, :], bank[2 + k % 6][:, 0:T], ACT.Copy,
                                 scale=pcol[:, gcol + k:gcol + k + 1]).then_inc(ah_done, 1)

            act.wait_ge(chain, 1)
            norm()
            act.wait_ge(par_T, 1)
            a.activation(pcol[:], bank[2][:, 0:120], ACT.Copy).then_inc(par_ready, 1)
            act.wait_ge(par_T, 2)
            a.activation(keysT[:], bank[3][:, 0:2 * NKEY].rearrange("p (s n) -> p s n", s=2), ACT.Copy).then_inc(par_ready, 1)
            act.wait_ge(par_T, 3)
            a.activation(convT[:], bank[4][:, 0:KT * 2 * TS].rearrange("p (k r) -> p k r", k=KT), ACT.Copy).then_inc(par_ready, 1)
            hi(0)
            act.wait_ge(par_ready, 1)
            act_parts(0, 80)
            hi(1)

            act.wait_ge(mm_done, 1)
            hi(2)
            a.activation(alr[0:RANK, :], bank[ACC][0:RANK, 0:T], ACT.Copy).then_inc(acc_read, 1)
            def log_decay(step):
                if step == 0:
                    act.wait_ge(la_ev, H * KD)
                    a.activation(la_tmp[:], la[:], ACT.Abs).then_inc(la_step, 1)
                if step == 1:
                    act.wait_ge(la_step, 1)
                    a.activation(la_tmp[:], la_tmp[:], ACT.Exp, scale=-1.0).then_inc(la_step, 1)
                if step == 2:
                    act.wait_ge(la_step, 2)
                    a.activation(la_tmp[:], la_tmp[:], ACT.Ln, bias=1.0).then_inc(la_step, 1)

            def qkv_block(n0, i, L, out):
                act.wait_ge(mm_done, n0 + 1 + i * L)
                hi(n0 + 2, i, L)
                evac_wait(n0, i, L)
                a.activation(out, bank[ACC + n0 % 2][:, 0:T], ACT.Copy).then_inc(acc_read, 1)

            for b in range(4):
                qkv_block(B_Q + b, 0, 0, qk[:, b, :])
                log_decay(b)
            with act.Fori(0, 3) as i:
                for b in range(4):
                    qkv_block(B_Q + 4 + b, i, 4, qk[:, bass.ds(i * 4 + 4 + b, 1), :].rearrange("p o t -> p (o t)"))
            with act.Fori(0, 4) as i:
                for b in range(4):
                    qkv_block(B_V + b, i, 4, stage[(B_V + b) % 2][:])

            act.wait_ge(la_ready, 1)
            act.wait_ge(la_step, 5)
            a.activation(cols[:, :, 6:8], cols[:, :, 4:6], ACT.Exp).then_inc(la_ready, 1)
            a.activation(decS[:], la[:, :, TP:T], ACT.Exp, scale=1.0 / TAU).then_inc(la_ready, 1)

            def chunk_exps(i, c):
                act.wait_ge(decayed, ONE + i * 2 + c)
                if c == 0:
                    act.wait_ge(staged, i * 8 + 2)
                act.wait_ge(o_mm, ONE + i * 2 + c)
                bt = la_h[:, :, c * P:(c + 1) * P]
                for k in range(KD):
                    for out, sc, col in ((dq, 1, 0), (dk, -1, 2), (dk1, -1, 4)):
                        a.activation(out[:, k, :], bt[:, k, :], ACT.Exp, scale=sc / TAU,
                                     bias=cols_h[:, k, col + c:col + c + 1]).then_inc(exps, 1)
                a.activation(dq0[:], bt, ACT.Exp, scale=1.0 / TAU).then_inc(exps, 1)

            def out_norm(i, c):
                q, src = (P, bank[OB]) if c < 2 else (TS, bank[OS])
                junk = o_sb[0:q, :]
                if c < 2:
                    act.wait_ge(o_mm, ONE + i * 2 + c + 1)
                else:
                    act.wait_ge(os_mm, ONE + i * (KD * TS) + KD * TS)
                act.wait_ge(o_tr, ONE + i * 3 + c)
                a.activation(junk, src[0:q, :], ACT.Square, accum_out=gss[0:q, c:c + 1]).then_inc(o_sum, 1)

            def out_scale(i, c):
                q, src = (P, bank[OB]) if c < 2 else (TS, bank[OS])
                act.wait_ge(o_mean, i * 3 + c + 1)
                a.activation(gss[0:q, 3:4], gss[0:q, 3:4], ACT.Sqrt).then_inc(o_root, 1)
                act.wait_ge(o_rstd, i * 3 + c + 1)
                a.activation(o_sb[0:q, :], src[0:q, :], ACT.Copy,
                             scale=gss[0:q, 4:5]).then_inc(o_ready, 1)

            def out_turned(i, c):
                act.wait_ge(o_tr, ONE + i * 3 + c + 1)
                if c == 0:
                    act.wait_ge(head_done, ONE + i)
                w = P if c < 2 else TS
                a.activation(oT[:, :, c * P:c * P + w],
                             bank[KV1 if c < 2 else OB][:, 0:HV * w].rearrange("p (b t) -> p b t", b=HV), ACT.Copy).then_inc(oT_ready, 1)

            with act.Fori(0, H) as i:
                for b in range(SIX_PER_HEAD):
                    n0 = B_SIX + b
                    cg, t, half = b // 12, (b // 2) % 6, b % 2
                    src = bank[ACC + n0 % 2][:, 0:T]
                    act.wait_ge(mm_done, n0 + 1 + i * 24)
                    hi(n0 + 2, i, 24)
                    evac_wait(n0, i, 24)
                    q = cg * 2 + half
                    if cg == 0 and t in (1, 2):
                        act.wait_ge(head_done, ONE + i)
                    if t == 0:
                        act.wait_ge(post_done, ONE + posts(n0 - 2) + i * POSTS)
                        a.activation(tR[half][:], src, ACT.Copy)
                        a.activation(tA[half][:], src, ACT.Sigmoid).then_inc(acc_read, 1)
                    elif t == 1:
                        a.activation(gate[:, q, :], src, ACT.Sigmoid).then_inc(acc_read, 1)
                    elif t in (2, 3, 4):
                        out = {2: yb[:, q, :], 3: tA[half][:], 4: tR[half][:]}[t]
                        a.activation(out, src, ACT.Copy).then_inc(acc_read, 1)
                    else:
                        act.wait_ge(post_done, ONE + posts(n0 - 2) + i * POSTS)
                        a.activation(tR[half][:], src, ACT.Sigmoid).then_inc(acc_read, 1)
                    if b == 1:
                        chunk_exps(i, 0)
                    if b == 9:
                        chunk_exps(i, 1)
                    for c in (0, 1):
                        if b == 8 * c + 4:
                            act.wait_ge(attn_mm, ONE + i * 2 + c + 1)
                            a.activation(k_tok[:], bank[MISC][:, P:3 * P].rearrange("p (k d) -> p k d", k=KD),
                                         ACT.Copy).then_inc(k_read, 1)
                    m = b - 3
                    if 0 <= m < KD * TS:
                        j = m // KD
                        if m == 0:
                            act.wait_ge(staged, i * 8 + 6)
                        act.wait_ge(v_in[j % 2], i * (16 * TS // 2) + 16 * (j // 2 + 1))
                        if m % KD == 0 and m:
                            act.wait_ge(s_new, ONE + i * (KD * TS) + m - 1)
                        a.activation(kv_at(m)[:], v_row[j % 2][:], ACT.Copy,
                                     scale=k_h[:, m % KD, TP + j:TP + j + 1]).then_inc(kv_ready, 1)
                    for c, at in ((0, 6), (1, 14), (2, 20)):
                        if b == at:
                            out_norm(i, c)
                        if b == at + 1:
                            out_scale(i, c)
                        if b == at + 3:
                            out_turned(i, c)
                    if t == 5:
                        act.wait_ge(u_tr, i * 4 + q + 1)
                        if q == 0:
                            act.wait_ge(u_out, ONE + i * 32)
                        a.activation(u_rows[0:2 + TS, q * P:(q + 1) * P], bank[KV1][0:2 + TS, 0:P],
                                     ACT.Copy).then_inc(u_read, 1)
                act.wait_ge(u_read, ONE + i * 4 + 4)
                ch = bass.ds(i * DV, DV)
                act.dma_start(conv_prompt.rearrange("o b s d -> (o b s) d")[:, ch], u_rows[0:2, :]).then_inc(u_out, 16)
                act.dma_start(conv_sample.rearrange("o j s d -> (o j) s d")[:, 1, ch], u_rows[2:2 + TS, :]).then_inc(u_out, 16)
                act.wait_ge(S_ready, i * 2 + 2)
                act.dma_start(stp_out[:, bass.ds(i, 1), :, :].rearrange("p o k v -> p (o k) v"), S[:]).then_inc(S_out, 16)

            act.wait_ge(mm_done, B_OUT)
            for k in range(0, KT, 2):
                act.wait_ge(m_ready, 2 * (k // (KT // H) + 1))
                a.activation(act_hi[:, k:k + 2, :], mT[:, m_at(k):m_at(k) + 2, :], ACT.Copy).then_inc(ah_done, 2)
            with act.Fori(0, 4) as i:
                for b in range(4):
                    qkv_block(B_OUT + b, i, 4, stage[(B_OUT + b) % 2][:])
            act.wait_ge(post_done, ONE + posts(B_QRY - 1))
            act.dma_start(x2_dram[:, 0:2, :], x2_tok[:, 0:2, :]).then_inc(x2_out, 16)
            act.dma_start(x2_dram[0:TS, 2, :], x2_tok[0:TS, 2, :]).then_inc(x2_out, 16)
            def squares(nth, t):
                act.wait_ge(ss_done, nth)
                q = P if t < 2 else TS
                a.activation(sq_junk[0:q, :], x2_tok[0:q, t, :], ACT.Square,
                             accum_out=ssq[0:q, t:t + 1]).then_inc(ss_done, 1)

            squares(3, 2)
            act.wait_ge(ms_done, 2)
            a.activation(root[:, 2:3], mean_sq[:, 2:3], ACT.Sqrt).then_inc(rt_done, 1)
            act_parts(1, 80 + KT)
            squares(4, 0)
            squares(5, 1)
            act.wait_ge(ms_done, 3)
            a.activation(root[:, 0:2], mean_sq[:, 0:2], ACT.Sqrt).then_inc(rt_done, 1)

            def query_out(h0, i, L):
                for half in range(2):
                    n0 = B_QRY + 2 * h0 + half
                    act.wait_ge(mm_done, n0 + 1 + i * L)
                    evac_wait(n0, i, L)
                    src = bank[ACC + n0 % 2]
                    at = bass.ds(h0 + i, 1) if L else slice(h0, h0 + 1)
                    a.activation(q_s[:, half, at, :].rearrange("p o j -> p (o j)"), src[:, TP:T],
                                 ACT.Copy).then_inc(q_s_ready, 1)
                    a.activation(stage[n0 % 2][:, 0:TP], src[:, 0:TP], ACT.Copy).then_inc(acc_read, 1)

            def soft_exp(h0, i, tiles, rows):
                act.wait_ge(soft_in, i + h0 + 1)
                a.activation(soft[0:rows, 0:tiles, :], soft[0:rows, 0:tiles, :], ACT.Exp).then_inc(soft_e, 1)

            query_out(0, 0, 0)
            soft_exp(0, 0, 2, P)
            with act.Fori(0, PH - 1) as i:
                for half in range(2):
                    n0 = B_LATE + half
                    act.wait_ge(mm_done, n0 - 1 + i * 2)
                    hi(n0, i, 2)
                query_out(1, i, 2)
                soft_exp(1, i, 2, P)
            act.wait_ge(rep_mm, 1)
            for j in range(4):
                a.activation(xs_rep[:, j * 512:(j + 1) * 512], bank[4 + j][:], ACT.Copy).then_inc(rep_ready, 1)
            soft_exp(PH, 0, 1, PH * TS)
            W = 2 * TOPK
            act.wait_ge(w_ready, ONE + 1)
            a.activation(w_all[:], w_all[:], ACT.Gelu).then_inc(gelu_done, 1)
            act.wait_ge(dve_used, N_DVE)
            a.activation(w_s[:], dots_s[:], ACT.Gelu).then_inc(gelu_done, 1)

            def y_norm(t):
                q, nth = P if t < 2 else TS, ORDER.index(t)
                act.wait_ge(y_sum, 4 * nth + 4)
                if nth:
                    act.wait_ge(y_ss, nth)
                a.activation(y_sq[0:q, :], y_tok[0:q, t, :], ACT.Square,
                             accum_out=ssq[0:q, t:t + 1]).then_inc(y_ss, 1)
                act.wait_ge(y_mean, nth + 1)
                a.activation(root[0:q, t:t + 1], mean_sq[0:q, t:t + 1], ACT.Sqrt).then_inc(y_root, 1)

            act.wait_ge(w_ready, ONE + 3)
            per = N_PE * TOPK // RING
            for t in range(2):
                with act.Fori(0, PH) as i:
                    for s in range(TOPK):
                        if s % RING in DVE_SLOTS:
                            continue
                        nth = s // RING * N_PE + PE_SLOTS.index(s % RING)
                        n = t * (PE_TILE + PH) + nth
                        act.wait_ge(pe_used, i * per + n + N_PE - 3)
                        a.activation(diag[nth % 4][:], ident[:], ACT.Copy,
                                     scale=w_all[:, bass.ds(i * W + t * TOPK + s, 1)]).then_inc(diag_ready, 1)
                if t == 0:
                    for s in range(PH):
                        act.wait_ge(pe_used, PE_TILE + s + N_PE - 3)
                        a.activation(diag_s[s % 4][:], gather8[:], ACT.Copy, scale=w_s[:, s:s + 1]).then_inc(diag_ready, 1)
                    y_norm(0)
                    y_norm(2)
            y_norm(1)
            act.wait_ge(u_out, ONE + 32 * H)
            act.wait_ge(S_out, ONE + 16 * H)

        @block.vector
        def _(dve):
            v = nc.vector
            count = [0]

            def lo(n0, i=0, L=0):
                s = raw_slot(n0)[0]
                dve.wait_ge(hi_done, n0 + 1 + i * L)
                v.tensor_tensor(w_lo[n0 % 2][:], raw[s][:], w_hi[n0 % 2][:].bitcast(F32),
                                ALU.subtract).then_inc(lo_done, 1)

            def norm():
                dve.wait_ge(ss_done, 3)
                v.tensor_scalar(mean_sq[:], ssq[:], 1.0 / D, EPS, ALU.mult, ALU.add).then_inc(ms_done, 1)
                dve.wait_ge(rt_done, 1)
                v.reciprocal(rstd[:], root[:]).then_inc(rs_done, 1)
                dve.wait_ge(rs_done, 1)
                for t in range(3):
                    q = P if t < 2 else TS
                    v.tensor_scalar(x_tok[0:q, t, :], x_tok[0:q, t, :], rstd[0:q, t:t + 1], None,
                                    ALU.mult).then_inc(xn_done, 1)

            def act_parts(p, gcol):
                for k in range(KT):
                    dve.wait_ge(ah_done, (2 * p) * KT + k + 1)
                    v.scalar_tensor_tensor(out=act_lo[:, k, :], in0=bank[2 + k % 6][:, 0:T],
                                           scalar=pcol[:, gcol + k:gcol + k + 1],
                                           in1=act_hi[:, k, :].bitcast(F32),
                                           op0=ALU.mult, op1=ALU.subtract).then_inc(al_done, 1)

            v.memset(ssq[:], 1.0).then_inc(chain, 1)
            for s in range(2):
                v.memset(u_pad[s][:], 0.0).then_inc(chain, 1)
            v.memset(gss[:], 1.0).then_inc(chain, 1)
            N0 = 4
            norm()
            lo(0)
            act_parts(0, 80)
            lo(1)
            lo(2)
            for m in range(H * KD):
                dve.wait_ge(la_mm, m + 1)
                v.tensor_scalar(la[:, m, :], bank[2 + m % 6][:, 0:T],
                                pcol[:, 80 + 2 * KT + m:81 + 2 * KT + m], None, ALU.add).then_inc(la_ev, 1)

            for b in range(3):
                lo(B_Q + b + 2)
            dve.wait_ge(la_step, 3)
            v.scalar_tensor_tensor(out=la[:], in0=la[:], scalar=0.0, in1=la_tmp[:], op0=ALU.min,
                                   op1=ALU.subtract).then_inc(la_step, 1)
            dve.wait_ge(la_step, 4)
            v.memset(attn[:], 1.0).then_inc(chain, 1)
            dve.wait_ge(chain, N0 + 1)
            for m in range(H * KD):
                if m == H * KD // 2:
                    lo(B_Q + 5)
                for c in range(2):
                    run = la[:, m, c * P:(c + 1) * P]
                    v.tensor_tensor_scan(run, attn[:], run, 0.0, ALU.mult, ALU.add).then_inc(chain, 1)
            dve.wait_ge(chain, N0 + 1 + 2 * H * KD)
            mid = la[:, :, P // 2 - 1:P // 2 + P:P]
            last = la[:, :, P - 1:2 * P:P]
            v.tensor_scalar(cols[:, :, 0:2], mid, -1.0 / TAU, None, ALU.mult)
            v.tensor_scalar(cols[:, :, 2:4], mid, 1.0 / TAU, None, ALU.mult)
            v.tensor_scalar(cols[:, :, 4:6], last, 1.0 / TAU, None, ALU.mult).then_inc(la_step, 1)
            dve.wait_ge(la_step, 5)
            dve.sem_inc(la_ready, 1)

            with dve.Fori(0, 3) as i:
                for b in range(4):
                    lo(B_Q + 4 + b + 2, i, 4)

            def v_copy(n0, i, L):
                dve.wait_ge(v_tr, n0 - B_V + 1 + i * L)
                col = bass.ds((n0 - B_V) * P + i * (L * P), P) if L else slice((n0 - B_V) * P, (n0 - B_V + 1) * P)
                src = bank[MISC + n0 % 2]
                v.tensor_copy(v_tok[:, 0:2, col], src[:, 0:2 * P].rearrange("p (t c) -> p t c", t=2))
                v.tensor_copy(v_tok[0:TS, 2, col], src[0:TS, 2 * P:3 * P]).then_inc(post_done, 1)

            with dve.Fori(0, 4) as i:
                for b in range(4):
                    lo(B_V + b + 2, i, 4)
                    v_copy(B_V + b, i, 4)

            def head_step(i, b, link):
                n0 = B_SIX + b
                cg, t, half = b // 12, (b // 2) % 6, b % 2
                q = cg * 2 + half
                lo(n0 + 2, i, 24)
                if b == 2:
                    dve.wait_ge(staged, i * 8 + 7)
                dve.wait_ge(acc_read, ONE + n0 + 1 + i * 24)
                dve.wait_ge(post_done, ONE + posts(n0 - 1) + i * POSTS)
                up = u_pad[half]
                if t == 0:
                    v.tensor_tensor(tR[half][:], tR[half][:], tA[half][:], ALU.mult).then_inc(post_done, 1)
                elif t == 1:
                    v.scalar_tensor_tensor(out=gate[:, q, :], in0=gate[:, q, :], scalar=pcol_h[:, q:q + 1],
                                           in1=tR[half][:], op0=ALU.mult, op1=ALU.mult).then_inc(post_done, 1)
                elif t == 4:
                    wcol = lambda j: pcol_h[:, 4 + 4 * j + q:5 + 4 * j + q]
                    bcol = pcol_h[:, 16 + q:17 + q]
                    z, zs = tA[half], tA[half][:, TP:T]
                    link(v.tensor_tensor(up[:, 2:2 + T], tR[half][:], tA[half][:], ALU.mult))
                    dve.sem_inc(u_ready, 1)
                    link(v.tensor_scalar(z[:], up[:, 2:2 + T], wcol(2), bcol, ALU.mult, ALU.add))
                    for j in (1, 0):
                        v.scalar_tensor_tensor(out=z[:, 0:TP], in0=up[:, j:j + TP], scalar=wcol(j),
                                               in1=z[:, 0:TP], op0=ALU.mult, op1=ALU.add)
                        link(v.scalar_tensor_tensor(out=zs, in0=convT_h[:, q, j:2 * TS:2], scalar=wcol(j),
                                                    in1=zs, op0=ALU.mult, op1=ALU.add))
                    v.tensor_tensor(yb[:, q, :], yb[:, q, :], z[:], ALU.mult).then_inc(post_done, 1)
                elif t == 5:
                    v.tensor_tensor(yb[:, q, :], yb[:, q, :], tR[half][:], ALU.mult).then_inc(post_done, 1)

                for c in (0, 1):
                    if b == 8 * c + 2:
                        dve.wait_ge(exps, (i * 2 + c + 1) * (3 * KD + 1))
                        dve.wait_ge(attn_mm, ONE + i * 2 + c)
                        span = slice(c * P, (c + 1) * P)
                        for out, src, sc in ((dq, q_h, DK ** -0.5), (dk, k_h, 1.0), (dq0, q_h, DK ** -0.5),
                                             (dk1, k_h, 1.0)):
                            ins = v.scalar_tensor_tensor(out=out[:], in0=src[:, :, span], scalar=sc, in1=out[:],
                                                         op0=ALU.mult, op1=ALU.mult)
                        ins.then_inc(decayed, 1)
                    if b == 8 * c + 4:
                        dve.wait_ge(k_read, ONE + i * 2 + c + 1)
                        v.tensor_tensor(attn[:], bank[MISC][:, 0:P], causal[:], ALU.mult).then_inc(attn_ready, 1)
                    if b == 8 * c + 6:
                        dve.wait_ge(o_mm, ONE + i * 2 + c + 1)
                        if c == 0:
                            dve.wait_ge(S_out, ONE + i * 16)
                            for k in range(KD):
                                ins = v.tensor_copy(S[:, k, :], bank[KV0 + k][:])
                        else:
                            for k in range(KD):
                                ins = v.scalar_tensor_tensor(out=S[:, k, :], in0=S[:, k, :],
                                                             scalar=cols_h[:, k, 6 + c:7 + c],
                                                             in1=bank[KV0 + k][:], op0=ALU.mult, op1=ALU.add)
                        ins.then_inc(S_ready, 1)
                for c, at in ((0, 6), (1, 14), (2, 20)):
                    if b == at:
                        q_ = P if c < 2 else TS
                        dve.wait_ge(o_sum, i * 3 + c + 1)
                        dve.wait_ge(o_ready, ONE + i * 3 + c)
                        v.tensor_scalar(gss[0:q_, 3:4], gss[0:q_, c:c + 1], 1.0 / DV, EPS, ALU.mult,
                                        ALU.add).then_inc(o_mean, 1)
                    if b == at + 1:
                        q_ = P if c < 2 else TS
                        dve.wait_ge(o_root, i * 3 + c + 1)
                        v.reciprocal(gss[0:q_, 4:5], gss[0:q_, 3:4]).then_inc(o_rstd, 1)
                if b == 2:
                    dve.wait_ge(os_mm, ONE + i * (KD * TS))
                    for k in range(KD):
                        ins = v.scalar_tensor_tensor(
                            out=q_sel[:, k, :, :], in0=q_h[:, k, TP:T].unsqueeze(2).broadcast_to([P, TS, TS]),
                            scalar=DK ** -0.5, in1=eye8[:], op0=ALU.mult, op1=ALU.mult)
                    ins.then_inc(q_sel_ready, 1)
                M = KD * TS
                m = b - 3
                if 0 <= m < M:
                    dve.wait_ge(kv_ready, ONE + i * M + m + 1)
                    dve.wait_ge(s_in[m % 4], i * 64 + 16 * (m // 4) + 16)
                    v.scalar_tensor_tensor(out=s_ring[m % 4][:], in0=s_ring[m % 4][:],
                                           scalar=decS_h[:, m % KD, m // KD:m // KD + 1], in1=kv_at(m)[:],
                                           op0=ALU.mult, op1=ALU.add).then_inc(s_new, 1)

            with dve.Fori(0, H) as i:
                links = [0]
                base = N0 + 1 + 2 * H * KD

                def link(ins):
                    links[0] += 1
                    ins.then_inc(chain, 1)
                    dve.wait_ge(chain, i * N_LINKS + base + links[0])

                for b in range(SIX_PER_HEAD):
                    head_step(i, b, link)
                dve.wait_ge(oT_ready, ONE + i * 3 + 3)
                dve.wait_ge(post_done, ONE + posts(B_SIX + 23) + i * POSTS)
                link(v.tensor_tensor(gate[:], gate[:], oT[:], ALU.mult))
                for half in (0, 1):
                    v.tensor_tensor(mT[:, bass.ds(i * 2 + half * (KT // 2), 2), :], yb[:, 2 * half:2 * half + 2, :],
                                    gate[:, 2 * half:2 * half + 2, :], ALU.add).then_inc(m_ready, 1)
                assert links[0] == N_LINKS, links[0]
                dve.wait_ge(os_mm, ONE + i * (KD * TS) + KD * TS)
                dve.wait_ge(m_ready, i * 2 + 2)
                dve.sem_inc(head_done, 1)

            for k in range(0, KT, 2):
                dve.wait_ge(ah_done, KT + k + 2)
                v.tensor_tensor(act_lo[:, k:k + 2, :], mT[:, m_at(k):m_at(k) + 2, :],
                                act_hi[:, k:k + 2, :].bitcast(F32), ALU.subtract).then_inc(al_done, 2)

            def x_add(n0, i, L):
                if n0 == B_OUT:
                    dve.wait_ge(x2_in, 32)
                dve.wait_ge(v_tr, KT + n0 - B_OUT + 1 + i * L)
                col = bass.ds((n0 - B_OUT) * P + i * (L * P), P)
                src = bank[MISC + n0 % 2]
                v.tensor_tensor(x2_tok[:, 0:2, col], src[:, 0:2 * P].rearrange("p (t c) -> p t c", t=2),
                                x2_tok[:, 0:2, col], ALU.add)
                v.tensor_tensor(x2_tok[0:TS, 2, col], src[0:TS, 2 * P:3 * P], x2_tok[0:TS, 2, col],
                                ALU.add).then_inc(post_done, 1)

            with dve.Fori(0, 4) as i:
                for b in range(4):
                    lo(B_OUT + b + 2, i, 4)
                    x_add(B_OUT + b, i, 4)
            def inverse_roots(nth, cols_):
                dve.wait_ge(ss_done, (4, 6)[nth])
                v.tensor_scalar(mean_sq[:, cols_], ssq[:, cols_], 1.0 / D, EPS, ALU.mult, ALU.add).then_inc(ms_done, 1)
                dve.wait_ge(rt_done, 2 + nth)
                v.reciprocal(rstd[:, cols_], root[:, cols_]).then_inc(rs_done, 1)
                dve.wait_ge(rs_done, 2 + nth)

            dve.wait_ge(S_out, ONE + 16 * H)
            dve.wait_ge(u_out, ONE + 32 * H)
            dve.sem_inc(cleared, 1)
            inverse_roots(0, slice(2, 3))
            v.tensor_scalar(xn_tok[0:TS, 2, :], x2_tok[0:TS, 2, :], rstd[0:TS, 2:3], None, ALU.mult).then_inc(xn_done, 1)
            act_parts(1, 80 + KT)
            inverse_roots(1, slice(0, 2))
            dve.wait_ge(row_in, 16)
            dve.wait_ge(tr_done, 2 * KT)
            v.tensor_tensor(xn_tok[0:TS, 2, :], xn_tok[0:TS, 2, :], g_row[0:TS, :], ALU.mult).then_inc(h2_ready, 1)

            base = N0 + 1 + 2 * H * KD + H * N_LINKS
            N_TOP = 20

            def scores(n0, i, L):
                dve.wait_ge(v_tr, 2 * KT + n0 - B_QRY + 1 + i * L)
                for t in range(2):
                    ins = v.tensor_scalar(sc[:, (n0 - B_QRY) % 2, t, :], bank[MISC + n0 % 2][:, t * P:(t + 1) * P],
                                          rstd[:, t:t + 1], None, ALU.mult)
                ins.then_inc(post_done, 1)

            def retrieval(h0, i, tiles, rows):
                steps = [0]
                r = slice(0, rows)
                ts = slice(0, tiles)

                def link(ins):
                    steps[0] += 1
                    ins.then_inc(chain, 1)
                    dve.wait_ge(chain, i * N_TOP + base + h0 * N_TOP + steps[0])
                    dve.sem_inc(granted, 1)

                def top16(work):
                    for turn in range(2):
                        eight = slice(8 * turn, 8 * turn + 8)
                        for src, vals, at in work:
                            ins = v.max(vals[:, eight], src)
                        link(ins)
                        for src, vals, at in work:
                            ins = v.max_index(at[:, eight], vals[:, eight], src)
                        link(ins)
                        if turn == 0:
                            for src, vals, at in work:
                                ins = v.match_replace(src, vals[:, eight], src, NEG_BIG)
                            link(ins)

                def best_keys():
                    top16([(sc[r, s, t, :], val[r, s, t, :], key_u[r, s, t, :])
                           for s in range(2) for t in range(tiles)])

                def best_pairs():
                    for t in range(tiles):
                        ins = v.tensor_tensor(cand[r, t, :].rearrange("p (a b) -> p a b", a=TOPK),
                                              val[r, 0, t, :].unsqueeze(2).broadcast_to([rows, TOPK, TOPK]),
                                              val[r, 1, t, :].unsqueeze(1).broadcast_to([rows, TOPK, TOPK]), ALU.add)
                    link(ins)
                    top16([(cand[r, t, :], best[r, t, :], pos[r, t, :]) for t in range(tiles)])
                    link(v.tensor_tensor(soft[r, ts], best[r, ts],
                                         best[r, ts, 0:1].broadcast_to([rows, tiles, TOPK]), ALU.subtract))
                    dve.sem_inc(soft_in, 1)

                def experts():
                    shape = [rows, tiles, TOPK, TOPK]
                    for s in range(2):
                        v.tensor_copy(key_f[r, s, ts], key_u[r, s, ts])
                    v.tensor_scalar(pos_u[r, 0, ts], pos[r, ts], 4, None, ALU.logical_shift_right)
                    link(v.tensor_scalar(pos_u[r, 1, ts], pos[r, ts], 15, None, ALU.bitwise_and))
                    for s in range(2):
                        ins = v.tensor_copy(pos_f[r, s, ts], pos_u[r, s, ts])
                    link(ins)
                    for s in range(2):
                        ins = v.tensor_tensor(hot[s][r, ts], pos_f[r, s, ts].unsqueeze(3).broadcast_to(shape),
                                              iota16[r].unsqueeze(1).unsqueeze(1).broadcast_to(shape), ALU.is_equal)
                    link(ins)
                    for s in range(2):
                        ins = v.tensor_tensor(hot[s][r, ts], hot[s][r, ts],
                                              key_f[r, s, ts].unsqueeze(2).broadcast_to(shape), ALU.mult)
                    link(ins)
                    for s in range(2):
                        ins = v.tensor_reduce(key_sel[r, s, ts], hot[s][r, ts], AX_X, ALU.add)
                    link(ins)
                    dve.wait_ge(soft_e, i + h0 + 1)
                    v.scalar_tensor_tensor(out=picks[r, 0, ts], in0=key_sel[r, 0, ts], scalar=float(NKEY),
                                           in1=key_sel[r, 1, ts], op0=ALU.mult, op1=ALU.add)
                    link(v.tensor_reduce(soft_s[r, ts], soft[r, ts], AX_X, ALU.add))
                    link(v.reciprocal(soft_r[r, ts], soft_s[r, ts]))
                    link(v.tensor_tensor(picks[r, 1, ts], soft[r, ts],
                                         soft_r[r, ts].unsqueeze(2).broadcast_to([rows, tiles, TOPK]), ALU.mult))
                    assert steps[0] == N_TOP, steps[0]

                return best_keys, best_pairs, experts

            W = 2 * TOPK

            def keep_picks(h0, i):
                to = bass.ds(h0 * W + i * W, W)
                v.tensor_copy(idx_all[:, to], picks[:, 0].rearrange("p t k -> p (t k)"))
                v.tensor_copy(g_all[:, to], picks[:, 1].rearrange("p t k -> p (t k)")).then_inc(retrieved, 1)
                dve.wait_ge(retrieved, i + h0 + 1)
                dve.sem_inc(granted, 1)

            def query_ready(h0, i):
                dve.wait_ge(post_done, ONE + posts(B_QRY + 2 * h0 + 1) + i * 2)
                dve.sem_inc(granted, 1)

            def dot(s, i):
                k = s % RING
                dve.wait_ge(ring_in[k], i * (16 * W // RING) + 16 * (s // RING + 1))
                v.tensor_tensor_reduce(ring[k][:], ring[k][:], xn_tok[:, s // TOPK, :], 1.0, 0.0, ALU.mult,
                                       ALU.add, dots[:, s:s + 1]).then_inc(u_used, 1)

            def keep_dots(i):
                dve.wait_ge(u_used, i * W + W + RING)
                v.tensor_copy(w_all[:, bass.ds(i * W, W)], dots[:]).then_inc(h2_ready, 1)
                dve.wait_ge(h2_ready, i + 4)
                dve.sem_inc(granted, 1)

            for half in range(2):
                scores(B_QRY + half, 0, 0)
            query_ready(0, 0)
            for piece in retrieval(0, 0, 2, P):
                piece()
            keep_picks(0, 0)
            dve.sem_inc(u_used, RING)
            for t in (0, 1):
                v.scalar_tensor_tensor(out=xn_tok[:, t, :], in0=x2_tok[:, t, :], scalar=rstd[:, t:t + 1],
                                       in1=g_row[:], op0=ALU.mult, op1=ALU.mult).then_inc(h2_ready, 1)
            dve.wait_ge(h2_ready, 3)
            with dve.Fori(0, PH - 1) as i:
                keys_, pairs_, experts_ = retrieval(1, i, 2, P)
                for s in range(W):
                    if s in (2, 6):
                        lo(B_LATE + (s == 6), i, 2)
                    if s in (10, 12):
                        scores(B_LATE + (s == 12), i, 2)
                    if s == 13:
                        query_ready(1, i)
                        keys_()
                    if s == 17:
                        pairs_()
                    if s == 21:
                        experts_()
                        keep_picks(1, i)
                    dot(s, i)
                keep_dots(i)
            R = PH * TS
            keys_, pairs_, experts_ = retrieval(PH, 0, 1, R)
            for s in range(W):
                if s == 4:
                    dve.wait_ge(s_scores, 1)
                    v.tensor_copy(sc[0:R, :, 0, :], bank[4][0:R, 0:2 * P].rearrange("p (s c) -> p s c", s=2)).then_inc(chain, 1)
                    n_chain = base + PH * N_TOP + 1
                    dve.wait_ge(chain, n_chain)
                    base += 1
                    keys_()
                if s == 8:
                    pairs_()
                if s == 12:
                    experts_()
                    for m in range(2):
                        ins = v.tensor_tensor(wide[0:R, m], picks[0:R, m, 0, :].unsqueeze(1).broadcast_to([R, PH, TOPK]),
                                              same_h[0:R, :].unsqueeze(2).broadcast_to([R, PH, TOPK]), ALU.mult)
                    ins.then_inc(wide_ready, 1)
                if s == 16:
                    dve.wait_ge(spread_mm, 1)
                    for m in range(2):
                        ins = v.tensor_tensor(own[:, m], bank[5][:, m * P:(m + 1) * P].rearrange("p (h k) -> p h k", h=PH),
                                              own16[:].unsqueeze(1).broadcast_to([P, PH, TOPK]), ALU.mult)
                    ins.then_inc(chain, 1)
                    dve.wait_ge(chain, base + (PH + 1) * N_TOP + 1)
                    v.tensor_reduce(own_s[:], own[:], AX_X, ALU.add).then_inc(chain, 1)
                    dve.wait_ge(chain, base + (PH + 1) * N_TOP + 2)
                    v.tensor_copy(idx_s[:], own_s[:, 0])
                    v.tensor_copy(g_s[:], own_s[:, 1]).then_inc(retrieved, 1)
                dot(s, PH - 1)
            keep_dots(PH - 1)
            dve.sem_inc(w_ready, 1)
            dve.wait_ge(rep_ready, 4)
            for s in range(PH):
                dve.wait_ge(ring_in[s], 16 * (PH * W // RING + 1))
                v.tensor_tensor_reduce(ring[s][:], ring[s][:], xs_rep[:], 1.0, 0.0, ALU.mult, ALU.add,
                                       dots_s[:, s:s + 1]).then_inc(dve_used if s in DVE_SLOTS else pe_used, 1)
            v.memset(zeros[:], 0.0).then_inc(cleared, 1)
            dve.wait_ge(gelu_done, ONE + 1)
            v.tensor_tensor(w_all[:], w_all[:], g_all[:], ALU.mult).then_inc(w_ready, 1)
            dve.wait_ge(gelu_done, ONE + 2)
            v.tensor_tensor(w_s[:], w_s[:], g_s[:], ALU.mult).then_inc(w_ready, 1)
            dve.wait_ge(w_ready, ONE + 3)
            dve.wait_ge(x2_back, 32)

            def y_out_tile(t):
                q, nth = P if t < 2 else TS, ORDER.index(t)
                dve.wait_ge(sum_ready, nth + 1)
                for j in range(4):
                    part = y_tok[0:q, t, j * 512:(j + 1) * 512]
                    v.tensor_tensor(part, bank[sum_bank(t) + j][0:q, :], part, ALU.add).then_inc(y_sum, 1)
                dve.wait_ge(y_ss, nth + 1)
                v.tensor_scalar(mean_sq[0:q, t:t + 1], ssq[0:q, t:t + 1], 1.0 / D, EPS, ALU.mult,
                                ALU.add).then_inc(y_mean, 1)
                dve.wait_ge(y_root, nth + 1)
                v.reciprocal(rstd[0:q, t:t + 1], root[0:q, t:t + 1]).then_inc(y_rstd, 1)
                dve.wait_ge(y_rstd, nth + 1)
                v.scalar_tensor_tensor(out=y_tok[0:q, t, :], in0=y_tok[0:q, t, :], scalar=rstd[0:q, t:t + 1],
                                       in1=g_row[0:q, :], op0=ALU.mult, op1=ALU.mult).then_inc(y_ready, 1)

            n_u = 2 * PH * TOPK // RING + 1
            per = N_DVE * TOPK // RING
            dve.wait_ge(row_in, 32)
            for t in range(2):
                with dve.Fori(0, PH) as i:
                    for s in range(TOPK):
                        k = s % RING
                        if k not in DVE_SLOTS:
                            continue
                        nth = s // RING * N_DVE + DVE_SLOTS.index(k)
                        dve.wait_ge(ring_in[k], i * (16 * TOPK // RING)
                                    + 16 * (n_u + v_fills(t, k) + s // RING + 1))
                        dve.wait_ge(dve_used, i * per + t * PH * per + nth + N_DVE)
                        v.scalar_tensor_tensor(out=y_tok[:, t, :], in0=ring[k][:],
                                               scalar=w_all[:, bass.ds(i * W + t * TOPK + s, 1)],
                                               in1=y_tok[:, t, :], op0=ALU.mult, op1=ALU.add).then_inc(dve_used, 1)
                dve.wait_ge(dve_used, (t + 1) * PH * per + N_DVE)
                y_out_tile(t)
                if t == 0:
                    y_out_tile(2)

        @block.tensor
        def _(pe):
            mm = nc.tensor.matmul
            tr = nc.tensor.transpose

            def turn(p, src):
                for k in range(KT):
                    if k >= 6:
                        pe.wait_ge(al_done, 2 * p * KT + k - 5)
                    b = bank[2 + k % 6]
                    for t in range(3):
                        q = P if t < 2 else TS
                        if k == 0 and t in (0, 2):
                            if p == 0 or t == 2:
                                pe.wait_ge(xn_done, 3 + p)
                            else:
                                pe.wait_ge(post_done, ONE + posts(B_QRY - 1))
                        ins = tr(b[:, t * P:t * P + q], src[t][0:q, t, k * P:(k + 1) * P], ident[0:q, 0:q])
                    ins.then_inc(tr_done, 1)

            def project(n0, i=0, L=0, parts_from=None):
                pe.wait_ge(lo_done, n0 + 1 + i * L)
                if n0:
                    pe.wait_ge(acc_read, ONE + n0 - 1 + i * L)
                out = bank[ACC + n0 % 2][:, 0:T]
                for k in range(KT):
                    hi_, lo_ = w_hi[n0 % 2][:, k, :], w_lo[n0 % 2][:, k, :]
                    if parts_from is not None and k % 2 == 0:
                        pe.wait_ge(al_done, parts_from + k + 2)
                    mm(out, hi_, act_hi[:, k, :], start=(k == 0), stop=False)
                    mm(out, hi_, act_lo[:, k, :], start=False, stop=False)
                    ins = mm(out, lo_, act_hi[:, k, :], start=False, stop=(k == KT - 1))
                ins.then_inc(mm_done, 1)

            def to_tokens(n0, i=0, L=0):
                pe.wait_ge(acc_read, ONE + n0 + 1 + i * L)
                pe.wait_ge(post_done, ONE + posts(n0 - 2) + i * L)
                b = bank[MISC + n0 % 2]
                st = stage[n0 % 2]
                for t in range(2):
                    tr(b[:, t * P:(t + 1) * P], st[:, t * P:(t + 1) * P], ident[:])
                mm(b[0:TS, 2 * P:3 * P], st[:, TP:T], ident[:], start=True, stop=True).then_inc(v_tr, 1)

            pe.wait_ge(consts, N_CONSTS)
            pe.wait_ge(par_in, 16 * N_PAR)
            tr(bank[2][:, 0:120], prow[0:120, :], ident[0:120, 0:120]).then_inc(par_T, 1)
            pe.wait_ge(keys_in, 16)
            for s in range(2):
                ins = tr(bank[3][:, s * P:(s + 1) * P], krow[:, s, :], ident[:])
            ins.then_inc(par_T, 1)
            pe.wait_ge(conv_in, 16)
            R = 2 * TS
            for k in range(KT):
                ins = tr(bank[4][:, k * R:(k + 1) * R], crow[0:R, k * P:(k + 1) * P], ident[0:R, 0:R])
            ins.then_inc(par_T, 1)
            pe.wait_ge(par_ready, 3)
            turn(0, [x_tok] * 3)
            project(0, parts_from=0)
            project(B_Q)
            pe.wait_ge(wau_in, 16)
            pe.wait_ge(acc_read, ONE + 1)
            for m in range(H * KD):
                if m >= 6:
                    pe.wait_ge(la_ev, m - 5)
                mm(bank[2 + m % 6][:, 0:T], wau[0:RANK, m * P:(m + 1) * P], alr[0:RANK, :],
                   start=True, stop=True).then_inc(la_mm, 1)
            for b in range(1, 4):
                project(B_Q + b)
            with pe.Fori(0, 3) as i:
                for b in range(4):
                    project(B_Q + 4 + b, i, 4)
            pe.wait_ge(la_ev, H * KD)
            project(B_V)
            with pe.Fori(0, 3) as i:
                for b in range(4):
                    project(B_V + b + 1, i, 4)
                    to_tokens(B_V + b, i, 4)
            for b in range(KT - 4, KT):
                if b + 1 < KT:
                    project(B_V + b + 1)
                to_tokens(B_V + b)

            def head_step(i, b):
                M = KD * TS
                project(B_SIX + b, i, 24)
                for c in (0, 1):
                    if b == 8 * c + 3:
                        pe.wait_ge(decayed, ONE + i * 2 + c + 1)
                        pe.wait_ge(attn_ready, ONE + i * 2 + c)
                        pe.wait_ge(k_read, ONE + i * 2 + c)
                        for k in range(KD):
                            mm(bank[MISC][:, 0:P], dk[:, k, :], dq[:, k, :], start=(k == 0), stop=(k == KD - 1))
                        for k in range(KD):
                            ins = tr(bank[MISC][:, (1 + k) * P:(2 + k) * P], dk1[:, k, :], ident[:])
                        ins.then_inc(attn_mm, 1)
                    if b == 8 * c + 5:
                        pe.wait_ge(attn_ready, ONE + i * 2 + c + 1)
                        pe.wait_ge(k_read, ONE + i * 2 + c + 1)
                        pe.wait_ge(o_ready, ONE + i * 3 + c)
                        if c == 0:
                            pe.wait_ge(staged, i * 8 + 8)
                        else:
                            pe.wait_ge(S_ready, i * 2 + 1)
                        pe.wait_ge(oT_ready, ONE + i * 3 + c)
                        pe.wait_ge(u_read, ONE + i * 4 + 2 * c)
                        mm(bank[OB][:], attn[:], v_h[:, c, :], start=True, stop=(c == 0))
                        if c:
                            for k in range(KD):
                                mm(bank[OB][:], dq0[:, k, :], S[:, k, :], start=False, stop=(k == KD - 1))
                        for k in range(KD):
                            ins = mm(bank[KV0 + k][:], k_tok[:, k, :], v_h[:, c, :], start=True, stop=True)
                        ins.then_inc(o_mm, 1)
                for c, at in ((0, 9), (1, 17), (2, 23)):
                    if b == at:
                        pe.wait_ge(o_ready, ONE + i * 3 + c + 1)
                        if c < 2:
                            pe.wait_ge(S_ready, i * 2 + c + 1)
                        pe.wait_ge(oT_ready, ONE + i * 3 + c)
                        q, src = P if c < 2 else TS, o_sb
                        pe.sem_inc(granted, 1)
                        for d in range(HV):
                            ins = tr(bank[KV1 if c < 2 else OB][:, d * q:(d + 1) * q], src[0:q, d * P:(d + 1) * P], ident[0:q, 0:q])
                        ins.then_inc(o_tr, 1)
                m = b - 4
                if 0 <= m < M:
                    if m == 0:
                        pe.wait_ge(q_sel_ready, i + 1)
                        pe.wait_ge(o_ready, ONE + i * 3)
                    pe.wait_ge(s_new, ONE + i * M + m + 1)
                    mm(bank[OS][0:TS, :], q_sel[:, m % KD, m // KD, :], s_ring[m % 4][:], start=(m == 0),
                       stop=(m == M - 1)).then_inc(os_mm, 1)
                if (b // 2) % 6 == 5:
                    q = (b // 12) * 2 + b % 2
                    pe.wait_ge(u_ready, i * 4 + q + 1)
                    pe.wait_ge(u_read, ONE + i * 4 + q)
                    pe.wait_ge(oT_ready, ONE + i * 3 + (1 if q < 2 else 2))
                    mm(bank[KV1][0:2 + TS, 0:P], u_pad[b % 2][:, TP:2 + T], ident[:],
                       start=True, stop=True).then_inc(u_tr, 1)

            with pe.Fori(0, H) as i:
                for b in range(SIX_PER_HEAD):
                    head_step(i, b)
            project(B_OUT, parts_from=KT)
            with pe.Fori(0, 3) as i:
                for b in range(4):
                    project(B_OUT + b + 1, i, 4)
                    to_tokens(B_OUT + b, i, 4)
            for b in range(KT - 4, KT):
                if b + 1 < KT:
                    project(B_OUT + b + 1)
                to_tokens(B_OUT + b)
            turn(1, [x2_tok, x2_tok, xn_tok])

            def scores(n0, i=0, L=0):
                pe.wait_ge(acc_read, ONE + n0 + 1 + i * L)
                pe.wait_ge(post_done, ONE + posts(n0 - 2) + i * L)
                b, st, s = bank[MISC + n0 % 2], stage[n0 % 2], (n0 - B_QRY) % 2
                for t in range(2):
                    ins = mm(b[:, t * P:(t + 1) * P], st[:, t * P:(t + 1) * P], keysT[:, s, :], start=True, stop=True)
                ins.then_inc(v_tr, 1)

            for half in range(2):
                project(B_QRY + half, parts_from=None if half else 2 * KT)
            for half in range(2):
                scores(B_QRY + half)
            pe.wait_ge(h2_ready, 1)
            pe.wait_ge(consts, N_CONSTS + N_LATE_CONSTS)
            for j in range(4):
                ins = mm(bank[4 + j][:], spread[0:TS, :], xn_tok[0:TS, 2, j * 512:(j + 1) * 512], start=True, stop=True)
            ins.then_inc(rep_mm, 1)
            with pe.Fori(0, PH - 1) as i:
                for half in range(2):
                    project(B_LATE + half, i, 2)
                for half in range(2):
                    scores(B_LATE + half, i, 2)
            R = PH * TS
            pe.wait_ge(q_s_ready, 2 * PH)
            pe.wait_ge(rep_ready, 4)
            for s in range(2):
                ins = mm(bank[4][0:R, s * P:(s + 1) * P], q_s[:, s].rearrange("p h j -> p (h j)"), keysT[:, s, :],
                         start=True, stop=True)
            ins.then_inc(s_scores, 1)
            pe.wait_ge(wide_ready, 1)
            for m in range(2):
                ins = mm(bank[5][:, m * P:(m + 1) * P], same_j[0:R, :], wide[0:R, m].rearrange("p h k -> p (h k)"),
                         start=True, stop=True)
            ins.then_inc(spread_mm, 1)

            def open_sums(t, q):
                for j in range(4):
                    mm(bank[sum_bank(t) + j][0:q, :], zeros[:, 0:q], zeros[:], start=True, stop=False)

            def close_sums(t, q):
                for j in range(4):
                    ins = mm(bank[sum_bank(t) + j][0:q, :], zeros[:, 0:q], zeros[:], start=False, stop=True)
                ins.then_inc(sum_ready, 1)

            pe.wait_ge(cleared, 2)
            n_u = 2 * PH * TOPK // RING + 1
            per = N_PE * TOPK // RING
            for t in range(2):
                if t:
                    pe.wait_ge(y_sum, 4)
                open_sums(t, P)
                with pe.Fori(0, PH) as i:
                    for s in range(TOPK):
                        k = s % RING
                        if k in DVE_SLOTS:
                            continue
                        nth = s // RING * N_PE + PE_SLOTS.index(k)
                        pe.wait_ge(diag_ready, ONE + i * per + t * (PE_TILE + PH) + nth + 1)
                        pe.wait_ge(ring_in[k], i * (16 * TOPK // RING)
                                   + 16 * (n_u + v_fills(t, k) + s // RING + 1))
                        for j in range(4):
                            ins = mm(bank[sum_bank(t) + j][:], diag[nth % 4][:], ring[k][:, j * 512:(j + 1) * 512],
                                     start=False, stop=False, skip_group_check=True)
                        ins.then_inc(pe_used, 1)
                close_sums(t, P)
                if t == 0:
                    open_sums(2, TS)
                    for s in range(PH):
                        k = sample_slot[s]
                        pe.wait_ge(diag_ready, ONE + PE_TILE + s + 1)
                        pe.wait_ge(ring_in[k], 16 * (n_u + TURNS + sample_slot[:s + 1].count(k)))
                        for j in range(4):
                            ins = mm(bank[sum_bank(2) + j][0:TS, :], diag_s[s % 4][:], ring[k][:, j * 512:(j + 1) * 512],
                                     start=False, stop=False, skip_group_check=True)
                        ins.then_inc(pe_used, 1)
                    close_sums(2, TS)


_INS = ["x_prompt", "x_sample", "state_gla", "state_conv", "norm1_g", "w_in", "w_alpha_up", "b_alpha",
        "gla_norm_g", "conv_w", "conv_b", "w_out", "norm2_g", "w_query", "sub_keys", "expert_u", "expert_v",
        "norm_f_g"]


def kernel(**inputs):
    import numpy as np
    import concourse.bacc as bacc
    from concourse.bass_utils import run_bass_kernel_spmd

    nc = bacc.Bacc("TRN2", target_bir_lowering=False, num_devices=1)
    arrays, args = {}, []
    for name in _INS:
        x = np.ascontiguousarray(inputs[name])
        arrays[f"in_{name}"] = x
        args.append(nc.dram_tensor(f"in_{name}", x.shape, mybir.dt.from_np(x.dtype), kind="ExternalInput").ap())
    xp, xs, sg, sc = (inputs[n].shape for n in _INS[:4])
    outs = [xp, xs, (sg[0], xp[0], *sg[2:]), (sc[0], xp[0], *sc[2:]), sg, sc]
    for n, shape in enumerate(outs):
        args.append(nc.dram_tensor(f"out_{n}", tuple(shape), F32, kind="ExternalOutput").ap())
    hybrid_step(nc, *args)
    r = run_bass_kernel_spmd(nc, [arrays], core_ids=[0])
    return tuple(r.results[0][f"out_{n}"] for n in range(len(outs)))
```
